# Optimizing a Trainium2 kernel written in Bass

```python
import jax
import jax.numpy as jnp
from jax import lax
import numpy as np

D_MODEL = 1024
BATCH = 1
SEQ = 512
DEPTH = 2

PLE_DIM = 256
HEAD_DIM = 64
CHUNK = 128
A_HEADS = 4
A_WIDTH = A_HEADS * HEAD_DIM
B_HEADS = 6
B_WIDTH = B_HEADS * HEAD_DIM
RET_THETA = 10000.0
C_HEADS = 6
C_KV_HEADS = 2
C_GROUP = C_HEADS // C_KV_HEADS
C_WIDTH = C_HEADS * HEAD_DIM
C_KV_WIDTH = C_KV_HEADS * HEAD_DIM
WINDOW = 128
ROPE_THETA = 500000.0
ROPE_DIM = HEAD_DIM // 4
MIX_WIDTH = A_WIDTH + B_WIDTH + C_WIDTH
IN_SIZES = (A_WIDTH, A_WIDTH, B_WIDTH, B_WIDTH, B_WIDTH, B_WIDTH, C_WIDTH, C_KV_WIDTH, C_KV_WIDTH)
IN_WIDTH = 2 * A_WIDTH + 4 * B_WIDTH + C_WIDTH + 2 * C_KV_WIDTH
D_FF = ((8 * D_MODEL + 3 * 256 - 1) // (3 * 256)) * 256
EPS = 1e-6
NEG_INF = -1e30

kernel_name = 'hymba_style_gmlp_retention_swa_hybrid'

def rms_norm(x, w):
    xf = x.astype(jnp.float32)
    y = xf * lax.rsqrt(jnp.mean(xf * xf, axis=-1, keepdims=True) + EPS)
    return (y * w.astype(jnp.float32)).astype(x.dtype)

def head_norm(x):
    xf = x.astype(jnp.float32)
    mu = jnp.mean(xf, axis=-1, keepdims=True)
    var = jnp.mean(jnp.square(xf - mu), axis=-1, keepdims=True)
    return (xf - mu) * lax.rsqrt(var + EPS)

def rope(x, rot_dim, theta):
    s = x.shape[1]
    half = rot_dim // 2
    inv = 1.0 / (theta ** (jnp.arange(half, dtype=jnp.float32) / half))
    ang = jnp.arange(s, dtype=jnp.float32)[:, None] * inv[None, :]
    cos = jnp.cos(ang)[None, :, None, :]
    sin = jnp.sin(ang)[None, :, None, :]
    xr = x[..., :rot_dim].astype(jnp.float32)
    x1, x2 = xr[..., :half], xr[..., half:]
    rot = jnp.concatenate([x1 * cos - x2 * sin, x2 * cos + x1 * sin], axis=-1).astype(x.dtype)
    return jnp.concatenate([rot, x[..., rot_dim:]], axis=-1)

def split_cols(t, sizes):
    out, start = [], 0
    for s in sizes:
        out.append(t[..., start:start + s])
        start += s
    return out

def gmlp_mixer(u, v, ln_w, ln_b, w_s, b_s):
    b, s, _ = u.shape
    nc = s // CHUNK
    u = jax.nn.gelu(u)
    v = jax.nn.gelu(v)
    vn = head_norm(v.reshape(b, s, A_HEADS, HEAD_DIM)).reshape(b, s, A_WIDTH)
    vn = (vn * ln_w.astype(jnp.float32) + ln_b.astype(jnp.float32)).astype(v.dtype)
    vc = vn.reshape(b, nc, CHUNK, A_HEADS, HEAD_DIM)
    causal = jnp.tril(jnp.ones((CHUNK, CHUNK), dtype=bool))
    ws = jnp.where(causal[None], w_s, 0.0)
    mixed = jnp.einsum('hts,bcshd->bcthd', ws, vc) + b_s.T[None, None, :, :, None]
    return u * mixed.reshape(b, s, A_WIDTH)

def retention_mixer(q, k, v, g, gn_w):
    b, s, _ = q.shape
    nc = s // CHUNK
    f32 = jnp.float32
    q = rope(q.reshape(b, s, B_HEADS, HEAD_DIM), HEAD_DIM, RET_THETA).astype(f32)
    k = rope(k.reshape(b, s, B_HEADS, HEAD_DIM), HEAD_DIM, RET_THETA).astype(f32) * (HEAD_DIM ** -0.5)
    v = v.reshape(b, s, B_HEADS, HEAD_DIM).astype(f32)
    gamma = 1.0 - 2.0 ** (-5.0 - jnp.arange(B_HEADS, dtype=f32))
    log_g = jnp.log(gamma)
    idx = jnp.arange(CHUNK, dtype=f32)
    diff = idx[:, None] - idx[None, :]
    d_intra = jnp.where(diff[None] >= 0,
                        jnp.exp(jnp.maximum(diff, 0.0)[None] * log_g[:, None, None]), 0.0)
    d_to_end = jnp.exp((CHUNK - 1 - idx)[:, None] * log_g[None, :])
    d_from_start = jnp.exp((idx + 1.0)[:, None] * log_g[None, :])
    d_chunk = jnp.exp(CHUNK * log_g)
    qc = q.reshape(b, nc, CHUNK, B_HEADS, HEAD_DIM)
    kc = k.reshape(b, nc, CHUNK, B_HEADS, HEAD_DIM)
    vc = v.reshape(b, nc, CHUNK, B_HEADS, HEAD_DIM)
    sc = jnp.einsum('bcthd,bcshd->bchts', qc, kc) * d_intra[None, None]
    o_intra = jnp.einsum('bchts,bcshe->bcthe', sc, vc)
    kv = jnp.einsum('bcshd,sh,bcshe->bchde', kc, d_to_end, vc)

    def step(state, kv_c):
        return state * d_chunk[None, :, None, None] + kv_c, state

    init = jnp.zeros((b, B_HEADS, HEAD_DIM, HEAD_DIM), f32)
    _, prev = lax.scan(step, init, jnp.moveaxis(kv, 1, 0))
    prev = jnp.moveaxis(prev, 0, 1)
    o_cross = jnp.einsum('bcthd,bchde->bcthe', qc, prev) * d_from_start[None, None, :, :, None]
    o = (o_intra + o_cross).reshape(b, s, B_HEADS, HEAD_DIM)
    o = head_norm(o).reshape(b, s, B_WIDTH) * gn_w.astype(f32)
    return (jax.nn.silu(g.astype(f32)) * o).astype(g.dtype)

def swa_sink_mixer(q, k, v, sinks):
    b, s, _ = q.shape
    nc = s // CHUNK
    q = rope(q.reshape(b, s, C_HEADS, HEAD_DIM), ROPE_DIM, ROPE_THETA)
    k = rope(k.reshape(b, s, C_KV_HEADS, HEAD_DIM), ROPE_DIM, ROPE_THETA)
    v = v.reshape(b, s, C_KV_HEADS, HEAD_DIM)
    qb = q.reshape(b, nc, CHUNK, C_KV_HEADS, C_GROUP, HEAD_DIM)

    def banded(t):
        tb = t.reshape(b, nc, CHUNK, C_KV_HEADS, HEAD_DIM)
        prev = jnp.pad(tb[:, :-1], ((0, 0), (1, 0), (0, 0), (0, 0), (0, 0)))
        return jnp.concatenate([prev, tb], axis=2)

    kb, vb = banded(k), banded(v)
    sc = jnp.einsum('bcqhgd,bckhd->bchgqk', qb, kb).astype(jnp.float32) * (HEAD_DIM ** -0.5)
    qpos = jnp.arange(CHUNK)[:, None] + CHUNK
    kpos = jnp.arange(2 * CHUNK)[None, :]
    rel = qpos - kpos
    in_window = (rel >= 0) & (rel < WINDOW)
    first_pad = (jnp.arange(nc)[:, None, None] == 0) & (kpos < CHUNK)[None]
    mask = in_window[None] & ~first_pad
    sc = jnp.where(mask[None, :, None, None], sc, NEG_INF)
    sink = jnp.broadcast_to(sinks.astype(jnp.float32).reshape(1, 1, C_KV_HEADS, C_GROUP, 1, 1),
                            sc.shape[:-1] + (1,))
    probs = jax.nn.softmax(jnp.concatenate([sc, sink], axis=-1), axis=-1)[..., :-1]
    o = jnp.einsum('bchgqk,bckhd->bcqhgd', probs.astype(vb.dtype), vb)
    return o.reshape(b, s, C_WIDTH)

def setup_inputs(seed: int = 0) -> dict:
    key = jax.random.key(seed)
    ks = jax.random.split(key, 19)
    f32 = jnp.float32

    def nrm(k, shape, scale):
        return jax.random.normal(k, shape, f32) * scale

    def gain(k, shape):
        return 1.0 + 0.1 * jax.random.normal(k, shape, f32)

    return {
        'x': nrm(ks[0], (BATCH, SEQ, D_MODEL), 1.0),
        'p': nrm(ks[1], (DEPTH, BATCH, SEQ, PLE_DIM), 1.0),
        'norm_mix_pre': gain(ks[2], (DEPTH, D_MODEL)),
        'w_in': nrm(ks[3], (DEPTH, D_MODEL, IN_WIDTH), D_MODEL ** -0.5),
        'gmlp_ln_w': gain(ks[4], (DEPTH, A_WIDTH)),
        'gmlp_ln_b': nrm(ks[5], (DEPTH, A_WIDTH), 0.02),
        'gmlp_ws': nrm(ks[6], (DEPTH, A_HEADS, CHUNK, CHUNK), CHUNK ** -0.5),
        'gmlp_bs': 1.0 + nrm(ks[7], (DEPTH, A_HEADS, CHUNK), 0.1),
        'ret_gn_w': gain(ks[8], (DEPTH, B_WIDTH)),
        'attn_sinks': nrm(ks[9], (DEPTH, C_HEADS), 0.5),
        'w_out': nrm(ks[10], (DEPTH, MIX_WIDTH, D_MODEL), MIX_WIDTH ** -0.5),
        'norm_mix_post': gain(ks[11], (DEPTH, D_MODEL)),
        'norm_ffn_pre': gain(ks[12], (DEPTH, D_MODEL)),
        'w_ffn_in': nrm(ks[13], (DEPTH, D_MODEL, 2 * D_FF), D_MODEL ** -0.5),
        'w_ffn_out': nrm(ks[14], (DEPTH, D_FF, D_MODEL), D_FF ** -0.5),
        'norm_ffn_post': gain(ks[15], (DEPTH, D_MODEL)),
        'w_ple_gate': nrm(ks[16], (DEPTH, D_MODEL, D_MODEL), D_MODEL ** -0.5),
        'w_ple_proj': nrm(ks[17], (DEPTH, PLE_DIM, D_MODEL), PLE_DIM ** -0.5),
        'ple_norm': gain(ks[18], (DEPTH, D_MODEL)),
    }

def reference(x, p, norm_mix_pre, w_in, gmlp_ln_w, gmlp_ln_b, gmlp_ws, gmlp_bs, ret_gn_w,
              attn_sinks, w_out, norm_mix_post, norm_ffn_pre, w_ffn_in, w_ffn_out,
              norm_ffn_post, w_ple_gate, w_ple_proj, ple_norm):
    for i in range(DEPTH):
        h = rms_norm(x, norm_mix_pre[i])
        proj = h @ w_in[i]
        a_u, a_v, b_q, b_k, b_v, b_g, c_q, c_k, c_v = split_cols(proj, IN_SIZES)
        y_a = gmlp_mixer(a_u, a_v, gmlp_ln_w[i], gmlp_ln_b[i], gmlp_ws[i], gmlp_bs[i])
        y_b = retention_mixer(b_q, b_k, b_v, b_g, ret_gn_w[i])
        y_c = swa_sink_mixer(c_q, c_k, c_v, attn_sinks[i])
        mix = jnp.concatenate([y_a, y_b, y_c], axis=-1) @ w_out[i]
        x = x + rms_norm(mix, norm_mix_post[i])
        h = rms_norm(x, norm_ffn_pre[i])
        gate, up = split_cols(h @ w_ffn_in[i], (D_FF, D_FF))
        f = (jax.nn.silu(gate) * up) @ w_ffn_out[i]
        x = x + rms_norm(f, norm_ffn_post[i])
        ple = rms_norm(p[i] @ w_ple_proj[i], ple_norm[i])
        x = x + jax.nn.sigmoid(x @ w_ple_gate[i]) * ple
    return x


_drawn_inputs = setup_inputs


def setup_inputs(seed=0):
    import zlib

    import numpy as np

    out = dict(_drawn_inputs(seed))
    spreads = {}
    factors = {'gmlp_ln_b': 6.022, 'attn_sinks': 3.251}
    for name, (base, spread) in spreads.items():
        noise = np.random.default_rng([zlib.crc32(name.encode()), seed]).standard_normal(out[name].shape)
        drawn = base * np.exp(spread * noise) if base else spread * noise
        out[name] = jnp.asarray(drawn.astype(out[name].dtype))
    for name, factor in factors.items():
        out[name] = (out[name] * factor).astype(out[name].dtype)
    return out
```

```python
import numpy as np

import concourse.bass as bass
from concourse import mybir

F32 = mybir.dt.float32
F32R = mybir.dt.float32r
BF16 = mybir.dt.bfloat16
I32 = mybir.dt.int32
ALU = mybir.AluOpType
ACT = mybir.ActivationFunctionType
AX = mybir.AxisListType

P = 128
D = 1024
S = 512
TILES = S // P
KD = D // P
HD = 64
A_HEADS = 4
B_HEADS = 6
C_HEADS = 6
BW = B_HEADS * HD
AW = A_HEADS * HD
FF = 2816
FCH = FF // P
PLE = 256
EPS = 1e-6
NEG = -1e30
SLOTS = 3
RAWS = 3
PIECE = 1024

GROUPS = {
    "cqk": (2 * AW + 4 * BW, 512),
    "cv": (2 * AW + 4 * BW + 512, 128),
    "bk": (2 * AW + BW, BW),
    "bq": (2 * AW, BW),
    "bv": (2 * AW + 2 * BW, BW),
    "bg": (2 * AW + 3 * BW, BW),
    "a": (0, 2 * AW),
}
GNAMES = list(GROUPS)


def plan_strips():
    strips = []
    for g, (_, width) in GROUPS.items():
        n = 1 if width == 128 else 2
        strips += [("in", g, i) for i in range(n)]
    strips += [("out", None, i) for i in (3, 2, 1, 0)]
    strips += [("ffn", None, j) for j in range(FCH)]
    strips += [("fo", None, i) for i in range(FCH // 2)]
    strips += [("ple", None, 0)]
    strips += [("gate", None, i) for i in range(4)]
    return strips


STRIPS = plan_strips()
NS = len(STRIPS)
SIDX = {s: i for i, s in enumerate(STRIPS)}


def plan_schedule():
    ev = []
    done = set()

    def mm(strip, m):
        ev.append(("mm", strip, m))

    def close(strip):
        ev.append(("conv", SIDX[strip] + SLOTS))
        done.add(strip)

    at = {}

    def put(u, *e):
        at.setdefault(u, []).append(e)

    for c in range(TILES):
        put(5 + c, "swa_T", c)
        put(12 + 7 * c, "swa_cur", c)
        put(13 + 7 * c, "swa_prev", c)
        put(17 + 7 * c, "swa_PT", c)
        put(18 + 7 * c, "swa_o", c)
        put(19 + 7 * c if c < 3 else 40, "swa_yT", c)
        u = 36 + 4 * c
        put(u, "ret_T", c)
        put(u + 1, "ret_sc", c)
        put(u + 2, "ret_o", c)
        put(u + 4, "ret_norm", c)
        put(u + 5, "ret_yT", c)
    ins = [s for s in STRIPS if s[0] == "in"]
    ev += [("T", "mix", 0), ("T", "mix", 1)]
    for m in (0, 1):
        mm(ins[0], m)
    ev.append(("T", "mix", 2))
    mm(ins[0], 2)
    ev.append(("T", "mix", 3))
    mm(ins[0], 3)
    close(ins[0])
    u = 4
    for s in ins[1:]:
        for m in range(TILES):
            mm(s, m)
            for e in at.pop(u, ()):
                ev.append(e)
            u += 1
        close(s)
    rest = [e for k in sorted(at) for e in at[k]]
    o = [s for s in STRIPS if s[0] == "out"]
    fill = [(s, m) for s in o[:2] for m in (0, 1, 2)]
    for i, (s, m) in enumerate(fill):
        mm(s, m)
        if i == 1:
            ev += rest
        if i == 2:
            ev.append(("gmlp_mix",))
        if i == 4:
            ev.append(("gmlp_yT",))
    mm(o[0], 3)
    close(o[0])
    mm(o[1], 3)
    close(o[1])

    def tail(pair, stage, pre):
        for m in range(TILES):
            mm(pair[0], m)
            mm(pair[1], m)
            if m == TILES - 1:
                close(pair[0])
                close(pair[1])
            if m >= 2:
                ev.append(("T", pre, m - 2))
            ev.append(("post", stage, m))
            if pre == "ffn":
                ev.append(("pre", pre, m))

    tail(o[2:], "mix", "ffn")
    f = [s for s in STRIPS if s[0] == "ffn"]
    mm(f[0], 0), mm(f[0], 1), mm(f[1], 0), mm(f[1], 1)
    ev.append(("T", "ffn", 2))
    mm(f[0], 2), mm(f[1], 2)
    mm(f[2], 0), mm(f[2], 1)
    ev.append(("T", "ffn", 3))
    mm(f[2], 2)
    for j in range(3):
        mm(f[j], 3)
        close(f[j])
        ev.append(("mid", j))
    for j in range(3, FCH):
        mm(f[j], None)
        close(f[j])
        ev.append(("mid", j))
    fo = [s for s in STRIPS if s[0] == "fo"]
    for s in fo[:-2]:
        for m in (2, 3, 0, 1):
            mm(s, m)
        close(s)
    tail(fo[-2:], "ffn", "gate")
    ple = SIDX_PLE = ("ple", None, 0)
    g = [s for s in STRIPS if s[0] == "gate"]
    mm(ple, 0), ev.append(("post", "ple", 0))
    mm(ple, 1), ev.append(("post", "ple", 1))
    ev.append(("T", "gate", 2))
    ev.append(("T", "gate", 3))
    mm(ple, 2), ev.append(("post", "ple", 2))
    mm(ple, 3)
    close(ple)
    ev.append(("post", "ple", 3))
    for s in g[:2]:
        for m in range(TILES):
            mm(s, m)
        close(s)
    for m in range(TILES):
        mm(g[2], m)
        mm(g[3], m)
        if m == TILES - 1:
            close(g[2])
            close(g[3])
        ev.append(("gated", m))
        ev.append(("pre", "mix", m))
    return ev


SCHEDULE = plan_schedule()
BLOCKS = [e[1:] for e in SCHEDULE if e[0] == "mm"]
NB = len(BLOCKS)
BIDX = {b: i for i, b in enumerate(BLOCKS)}
STRIP_LAST = {s: max(i for i, b in enumerate(BLOCKS) if b[0] == s) for s in STRIPS}
ACT_EVAC = ["cqk", "cv", "bv", "bg", "a"]
DVE_EVAC = ["bk", "bq"]
POSTS = ["mix", "ffn", "ple"]
TSTAGES = ["mix", "ffn", "gate"]


def small_tables():
    f = np.float32
    pos = np.arange(S, dtype=f)

    def angles(half, theta):
        inv = (1.0 / (f(theta) ** (np.arange(half, dtype=f) / f(half)))).astype(f)
        a = (pos[:, None] * inv[None, :]).astype(f).reshape(TILES, P, half).transpose(1, 0, 2)
        return np.cos(a).astype(f).reshape(P, -1), np.sin(a).astype(f).reshape(P, -1)

    rc, rs = angles(HD // 2, 10000.0)
    sc, ss = angles(HD // 8, 500000.0)
    i = np.arange(P)
    lower_t = (i[:, None] <= i[None, :]).astype(f)
    upper_t = (i[:, None] > i[None, :]).astype(f)
    later = (i[None, :] > i[:, None]).astype(np.int32)
    g = np.log(1.0 - 2.0 ** (-5.0 - np.arange(B_HEADS, dtype=np.float64)))
    qs = np.exp((i[:, None] + 1.0) * g[None, :])
    ks = np.exp(-(i[:, None] + 1.0) * g[None, :]) * HD ** -0.5
    gc = np.exp(P * g)
    gcol = np.stack([np.where(i < HD, gc[2 * j], gc[2 * j + 1]) for j in range(3)], 1)
    table = np.concatenate([np.eye(P), rc, rs, sc, ss, lower_t, upper_t, qs, ks, gcol], 1)
    return np.ascontiguousarray(table.astype(f)), later


TABLE_COLS = {}
_at = 0
for _n, _w in (("ident", P), ("rcos", 128), ("rsin", 128), ("scos", 32), ("ssin", 32), ("lowT", P),
               ("upT", P), ("qs", 6), ("ks", 6), ("gcol", 3)):
    TABLE_COLS[_n] = (_at, _at + _w)
    _at += _w
TABLE_W = _at


def build_trunk(nc, depth, x_in, p_t, pre_mix, w_in, ln_w, ln_b, ws_t, bs_t, gn_w, sinks, w_out,
                post_mix, pre_ffn, w_ffn_in, w_ffn_out, post_ffn, w_gate, w_ple, ple_norm,
                table, later, out):
    KB = 1024
    BASE = (nc.sbuf_base + 31) // 32 * 32

    def place(name, shape, dt, kb):
        return nc.alloc_sbuf_tensor_at(name, shape, dt, offset=BASE + int(kb * KB))

    x = place("x", [P, TILES, D], F32, 0)
    h_hi = place("h_hi", [P, KD, S], F32R, 16)
    h_lo = place("h_lo", [P, KD, S], F32R, 32)
    mid_hi = place("mid_hi", [P, FCH, S], F32R, 48)
    mid_lo = place("mid_lo", [P, FCH, S], F32R, 92)
    raw = [place(f"raw{i}", [P, PIECE], F32, 136 + 4 * i) for i in range(RAWS)]
    w_hi = [place(f"w_hi{i}", [P, 2 * PIECE], F32R, 148 + 8 * i) for i in range(SLOTS)]
    w_lo = [place(f"w_lo{i}", [P, 2 * PIECE], F32R, 172 + 8 * i) for i in range(SLOTS)]
    post_w = place("post_w", [P, D], F32, 196)
    tab = place("tab", [P, TABLE_W], F32, 200)
    later_m = place("later_m", [P, P], I32, 203)
    tiny = place("tiny", [P, 192], F32, 203.5)
    gnw = place("gnw", [P, BW], F32, 204.25)
    lnw = place("lnw", [P, AW], F32, 205.75)
    lnb = place("lnb", [P, AW], F32, 206.75)
    silu_g = place("silu_g", [P, S], F32, 205.75)
    y_hi = place("y_hi", [P, KD, S], F32R, 48)
    y_lo = place("y_lo", [P, KD, S], F32R, 64)
    bg = place("bg", [P, TILES, BW], F32, 80)
    bv = place("bv", [P, TILES, BW], F32, 86)
    bk = place("bk", [P, TILES, BW], F32, 92)
    bq = place("bq", [P, TILES, BW], F32, 98)
    kqT = place("kqT", [P, 2, 3, P], F32, 104)
    scm = place("scm", [P, 2, 3, P], F32, 107)
    prob = place("prob", [P, C_HEADS, P], F32, 110)
    ptl = place("ptl", [P, C_HEADS, P], F32, 113)
    ptu = place("ptu", [P, C_HEADS, P], F32, 116)
    cqk = [place(f"cqk{i}", [P, 512], F32, 113 + 2 * i) for i in range(2)]
    swa_y = place("swa_y", [P, C_HEADS, HD], F32, 110)
    rope_x = place("rope_x", [P, BW], F32, 119)
    rope_a = place("rope_a", [P, BW], F32, 120.5)
    rope_b = place("rope_b", [P, BW], F32, 122)
    ret_oc = place("ret_oc", [P, BW], F32, 119)
    ret_sq = place("ret_sq", [P, BW], F32, 120.5)
    ret_y = place("ret_y", [P, BW], F32, 122)
    cT = place("cT", [P, 4, S], F32, 123.5)
    uv = place("uv", [P, TILES, 2 * AW], F32, 123.5)
    cv = place("cv", [P, TILES, P], F32, 131.5)
    wsT = place("wsT", [P, A_HEADS, P], F32, 133.5)
    vn = place("vn", [P, TILES, AW], F32, 110)
    vc = place("vc", [P, AW], F32, 114)
    vsq = place("vsq", [P, AW], F32, 115)
    state = place("state", [P, 3, P], F32, 196)
    upd = place("upd", [P, D], F32, 92)
    xn = [place(f"xn{i}", [P, D], F32, 96 + 4 * i) for i in range(2)]
    junk = place("junk", [P, D], BF16, 104)
    hT = [place(f"hT{i}", [P, 4, P], F32, 106 + 2 * i) for i in range(2)]
    ple_n = place("ple_n", [P, TILES, D], F32, 48)
    ple_w = place("ple_w", [P, D], F32, 64)
    p_raw = place("p_raw", [P, 2, S], F32, 68)
    p_hi = place("p_hi", [P, 2, S], F32R, 72)
    p_lo = place("p_lo", [P, 2, S], F32R, 76)
    sig = place("sig", [P, D], F32, 80)

    def T_(name):
        a, b = TABLE_COLS[name]
        return tab[:, a:b]

    tiny_at = [0]

    def small(n):
        a = tiny_at[0]
        tiny_at[0] += n
        return tiny[:, a:a + n]

    prew = small(2 * depth * KD).rearrange("p (s l k) -> p s l k", s=2, l=depth)
    bs = small(A_HEADS)
    snk = small(C_HEADS)
    ss_post = [small(2) for _ in range(2)]
    r_post = [small(1) for _ in range(2)]
    ss_pre = [small(1) for _ in range(2)]
    t_pre = small(1)
    t_post = small(1)
    r_pre = [small(1) for _ in range(2)]
    half_neg = small(6)
    neg_big = small(1)
    mx = small(6)
    negm = small(6)
    lsum = small(6)
    esink = small(6)
    rl = small(6)
    dsink = small(6)
    rmu = small(6)
    rvar = small(6)
    rr = small(6)
    rvt = small(6)
    gmu = small(4)
    gvar = small(4)
    gvt = small(4)
    gr = small(4)

    banks = [nc.alloc_psum_tensor(f"bank{i}", [P, 512], F32) for i in range(8)]

    sems = {}

    def sem(name):
        sems[name] = nc.alloc_semaphore(name)
        return sems[name]

    x_loaded = [sem(f"x_loaded{m}") for m in range(TILES)]
    raw_loaded = [sem(f"raw_loaded{i}") for i in range(RAWS)]
    consts_loaded = sem("consts_loaded")
    params_loaded = sem("params_loaded")
    ws_loaded = sem("ws_loaded")
    post_w_loaded = sem("post_w_loaded")
    ple_w_loaded = sem("ple_w_loaded")
    p_loaded = sem("p_loaded")
    stored = sem("stored")
    hi_ready = sem("hi_ready")
    lo_ready = sem("lo_ready")
    mm_done = sem("mm_done")
    x_T = sem("x_T")
    hT_ready = sem("hT_ready")
    h_hi_ready = sem("h_hi_ready")
    h_lo_ready = sem("h_lo_ready")
    post_sq = sem("post_sq")
    post_r = sem("post_r")
    x_new = sem("x_new")
    ple_ready = sem("ple_ready")
    pre_sq = sem("pre_sq")
    pre_r = sem("pre_r")
    xn_ready = sem("xn_ready")
    evac_act = sem("evac_act")
    evac_dve = sem("evac_dve")
    cqk_roped = sem("cqk_roped")
    b_roped = sem("b_roped")
    gs_ready = sem("gs_ready")
    swa_T = sem("swa_T")
    swa_cT = sem("swa_cT")
    swa_cur = sem("swa_cur")
    swa_S = sem("swa_S")
    swa_prev = sem("swa_prev")
    swa_m = sem("swa_m")
    swa_exp = sem("swa_exp")
    swa_PT = sem("swa_PT")
    swa_PTm = sem("swa_PTm")
    swa_o = sem("swa_o")
    swa_yr = sem("swa_yr")
    ret_T = sem("ret_T")
    ret_kqT = sem("ret_kqT")
    ret_sc = sem("ret_sc")
    ret_scm = sem("ret_scm")
    ret_o = sem("ret_o")
    ret_kv = sem("ret_kv")
    ret_state = sem("ret_state")
    ret_oread = sem("ret_oread")
    ret_v = sem("ret_v")
    ret_r = sem("ret_r")
    ret_yr = sem("ret_yr")
    y_T = sem("y_T")
    y_hi_ready = sem("y_hi_ready")
    y_lo_ready = sem("y_lo_ready")
    ws_ready = sem("ws_ready")
    gm_v = sem("gm_v")
    gm_r = sem("gm_r")
    gm_vn = sem("gm_vn")
    gm_mix = sem("gm_mix")
    gm_ya = sem("gm_ya")
    silu_ready = sem("silu_ready")
    prod_ready = sem("prod_ready")
    mid_hi_ready = sem("mid_hi_ready")
    mid_lo_ready = sem("mid_lo_ready")
    p_hi_ready = sem("p_hi_ready")
    p_lo_ready = sem("p_lo_ready")
    sig_ready = sem("sig_ready")
    pool_step = sem("pool_step")
    pool_init = sem("pool_init")
    dve_step = sem("dve_step")

    order_yT = [e for e in SCHEDULE if e[0] in ("swa_yT", "ret_yT", "gmlp_yT")]
    NY = len(order_yT) + 1

    def y_count(layer, e):
        i = order_yT.index(e)
        return layer * NY + i + 1 + sum(f[0] == "gmlp_yT" for f in order_yT[:i + 1])

    order_T = [e for e in SCHEDULE if e[0] == "T"]
    NT = 2 * len(order_T)

    def t_count(layer, stage, m, half=1):
        return layer * NT + 2 * order_T.index(("T", stage, m)) + half + 1

    order_hT = [e for e in order_T if e[1] != "gate"]
    NHT = 2 * len(order_hT)

    def hT_count(layer, stage, m, half):
        return layer * NHT + 2 * order_hT.index(("T", stage, m)) + half + 1

    order_post = [e for e in SCHEDULE if e[0] == "post"]

    def post_count(layer, stage, m):
        return layer * len(order_post) + order_post.index(("post", stage, m)) + 1

    def post_used(n):
        layer, i = divmod(n - 1, len(order_post))
        _, stage, m = order_post[i]
        if stage == "ple":
            return ple_ready, layer * TILES + m + 1
        return x_new, x_count(layer, stage, m)

    def x_count(layer, stage, m):
        return layer * 3 * TILES + TSTAGES.index(stage) * TILES + m + 1

    def pre_count(layer, stage, m):
        return layer * 2 * TILES + (TILES if stage == "ffn" else 0) + m + 1

    def mm_count(layer, strip, m):
        return layer * NB + BIDX[(strip, m)] + 1

    def used_count(g):
        return (g // NS) * NB + STRIP_LAST[STRIPS[g % NS]] + 1

    def group_final(gname):
        n = 1 if GROUPS[gname][1] == 128 else 2
        return ("in", gname, n - 1)

    def evac(layer, gname, m):
        if gname in ACT_EVAC:
            return evac_act, layer * 4 * len(ACT_EVAC) + 4 * ACT_EVAC.index(gname) + m + 1
        return evac_dve, layer * 4 * len(DVE_EVAC) + 4 * DVE_EVAC.index(gname) + m + 1

    def pieces(g):
        layer, (kind, name, i) = g // NS, STRIPS[g % NS]

        def view(w, k0, kn, c0, cn):
            return w[layer, k0 * P:(k0 + kn) * P, c0:c0 + cn].rearrange("(k p) c -> p k c", p=P)

        if kind == "in":
            c0, width = GROUPS[name]
            kn = KD // (1 if width == 128 else 2)
            return [view(w_in, i * kn + j * kn // 2, kn // 2, c0, width) for j in range(2)]
        if kind == "ffn":
            return [view(w_ffn_in, 0, KD, j * FF + i * P, P) for j in range(2)]
        w = {"out": w_out, "fo": w_ffn_out, "gate": w_gate, "ple": w_ple}[kind]
        return [view(w, 2 * i + j, 1, 0, D) for j in range(2)]

    def piece_size(g):
        kind, name, _ = STRIPS[g % NS]
        return GROUPS[name][1] * (4 if GROUPS[name][1] == 128 else 2) if kind == "in" else PIECE

    def bc_row(ap_row, n):
        return ap_row.partition_broadcast(P) if n is None else ap_row.partition_broadcast(n)

    with nc.Block() as block:

        @block.sync
        def _(sp):
            for m in range(TILES):
                if m == 1:
                    sp.dma_start(tab[:], table).then_inc(consts_loaded, 16)
                    sp.dma_start(later_m[:], later).then_inc(consts_loaded, 16)
                    sp.dma_start(prew[:, 0], pre_mix).then_inc(consts_loaded, 16)
                    sp.dma_start(prew[:, 1], pre_ffn).then_inc(consts_loaded, 16)
                sp.dma_start(x[:, m, :], x_in[m * P:(m + 1) * P, :]).then_inc(x_loaded[m], 16)
            for g in range(depth * NS):
                layer, s = divmod(g, NS)
                if s == 3:
                    if layer:
                        sp.wait_ge(mm_done, used_count((layer - 1) * NS + SIDX[("gate", None, 0)]))
                        sp.wait_ge(x_new, x_count(layer - 1, "ffn", 3))
                    sp.dma_start(wsT[:], ws_t[layer]).then_inc(ws_loaded, 16)
                    sp.dma_start(bs, bs_t[layer]).then_inc(params_loaded, 16)
                    sp.dma_start(snk, sinks[layer:layer + 1, :].partition_broadcast(P)).then_inc(params_loaded, 16)
                    sp.dma_start(gnw[:], gn_w[layer:layer + 1, :].partition_broadcast(P)).then_inc(params_loaded, 16)
                    sp.dma_start(lnw[:], ln_w[layer:layer + 1, :].partition_broadcast(P)).then_inc(params_loaded, 16)
                    sp.dma_start(lnb[:], ln_b[layer:layer + 1, :].partition_broadcast(P)).then_inc(params_loaded, 16)
                if s == SIDX[("ffn", None, 0)]:
                    sp.wait_ge(ret_o, (layer + 1) * TILES)
                    sp.dma_start(post_w[:], post_mix[layer:layer + 1, :].partition_broadcast(P)).then_inc(post_w_loaded, 16)
                if s == SIDX[("ffn", None, 6)]:
                    sp.wait_ge(x_new, x_count(layer, "mix", 3))
                    sp.dma_start(post_w[:], post_ffn[layer:layer + 1, :].partition_broadcast(P)).then_inc(post_w_loaded, 16)
                if s == SIDX[("ple", None, 0)]:
                    sp.wait_ge(mm_done, used_count(layer * NS + SIDX[("fo", None, 5)]))
                    sp.dma_start(ple_w[:], ple_norm[layer:layer + 1, :].partition_broadcast(P)).then_inc(ple_w_loaded, 16)
                    sp.dma_start(p_raw[:], p_t[layer].rearrange("(k p) t -> p k t", p=P)).then_inc(p_loaded, 16)
                n = piece_size(g)
                for j, view in enumerate(pieces(g)):
                    q = 2 * g + j
                    if q >= RAWS:
                        sp.wait_ge(lo_ready, q - RAWS + 1)
                    dst = raw[q % RAWS][:, 0:n].rearrange("p (k c) -> p k c", k=view.shape[1])
                    sp.dma_start(dst, view).then_inc(raw_loaded[q % RAWS], 16)
            for m in range(TILES):
                sp.wait_ge(x_new, x_count(depth - 1, "gate", m))
                sp.dma_start(out[m * P:(m + 1) * P, :], x[:, m, :]).then_inc(stored, 16)
            sp.wait_ge(stored, 16 * TILES)

        @block.tensor
        def _(pe):
            def mm3(out_ap, a_hi, a_lo, b_hi, b_lo, start, stop):
                pe.matmul(out_ap, a_hi, b_hi, start=start, stop=False, skip_group_check=True)
                pe.matmul(out_ap, a_hi, b_lo, start=False, stop=False, skip_group_check=True)
                return pe.matmul(out_ap, a_lo, b_hi, start=False, stop=stop, skip_group_check=True)

            def ts(m):
                return slice(m * P, (m + 1) * P)

            def mm_in(layer, g, strip, m):
                _, name, i = strip
                width = GROUPS[name][1]
                n = 1 if width == 128 else 2
                kn = KD // n
                if i == 0:
                    gi = GNAMES.index(name)
                    if gi:
                        pe.wait_ge(*evac(layer, GNAMES[gi - 1], m))
                    else:
                        pe.wait_ge(h_lo_ready, t_count(layer, "mix", m))
                hi = w_hi[g % SLOTS][:, 0:kn * width].rearrange("p (k c) -> p k c", k=kn)
                lo = w_lo[g % SLOTS][:, 0:kn * width].rearrange("p (k c) -> p k c", k=kn)
                for k in range(kn):
                    kk = i * kn + k
                    last = mm3(banks[m][:, 0:width], h_hi[:, kk, ts(m)], h_lo[:, kk, ts(m)],
                               hi[:, k, :], lo[:, k, :], kk == 0, kk == KD - 1)
                return last

            def mm_rows(a_hi, a_lo, k0, g, m, first, final):
                for k in range(2):
                    for half in range(2):
                        c = slice(k * D + half * 512, k * D + half * 512 + 512)
                        last = mm3(banks[2 * m + half][:, :], a_hi[:, k0 + k, ts(m)], a_lo[:, k0 + k, ts(m)],
                                   w_hi[g % SLOTS][:, c], w_lo[g % SLOTS][:, c],
                                   first and k == 0, final and k == 1)
                return last

            def mm_ffn(layer, g, strip, m):
                j = strip[2]
                cols = slice(0, S) if m is None else ts(m)
                for part in range(2):
                    for k in range(KD):
                        c = slice(part * PIECE + k * P, part * PIECE + (k + 1) * P)
                        last = mm3(banks[2 * (j % 4) + part][:, cols], w_hi[g % SLOTS][:, c],
                                   w_lo[g % SLOTS][:, c], h_hi[:, k, cols], h_lo[:, k, cols],
                                   k == 0, k == KD - 1)
                return last

            def block_of(layer, strip, m):
                g = layer * NS + SIDX[strip]
                kind, _, i = strip
                pe.wait_ge(lo_ready, 2 * (g + 1))
                if kind == "in":
                    last = mm_in(layer, g, strip, m)
                elif kind == "out":
                    if i == 3:
                        if m < 2:
                            pe.wait_ge(*evac(layer, "a", 2 * m + 1))
                        if m == 2:
                            pe.wait_ge(y_lo_ready, y_count(layer, ("swa_yT", 3)))
                    need = {2: ("ret_yT", 3), 3: ("swa_yT", 3), 1: ("ret_yT", 3), 0: ("gmlp_yT",)}[i]
                    if m == 3:
                        need = ("gmlp_yT",)
                    pe.wait_ge(y_lo_ready, y_count(layer, need))
                    last = mm_rows(y_hi, y_lo, 2 * i, g, m, i == 3, i == 0)
                elif kind == "ffn":
                    if m is not None:
                        pe.wait_ge(h_lo_ready, t_count(layer, "ffn", max(m, i) if i < 3 else m))
                    else:
                        if i >= 4:
                            pe.wait_ge(mid_lo_ready, layer * FCH + i - 3)
                        else:
                            pe.wait_ge(h_lo_ready, t_count(layer, "ffn", 3))
                    last = mm_ffn(layer, g, strip, m)
                elif kind == "fo":
                    if i == 0:
                        last_in_pair = max(j for j in range(FCH) if j % 4 == m)
                        pe.wait_ge(mid_lo_ready, layer * FCH + last_in_pair + 1)
                    pe.wait_ge(mid_lo_ready, layer * FCH + 2 * i + 2)
                    last = mm_rows(mid_hi, mid_lo, 2 * i, g, m, i == 0, i == FCH // 2 - 1)
                elif kind == "ple":
                    pe.wait_ge(h_lo_ready, t_count(layer, "gate", m))
                    pe.wait_ge(p_lo_ready, layer + 1)
                    last = mm_rows(p_hi, p_lo, 0, g, m, True, True)
                else:
                    if i == 0:
                        pe.wait_ge(ple_ready, layer * TILES + m + 1)
                    last = mm_rows(h_hi, h_lo, 2 * i, g, m, i == 0, i == 3)
                last.then_inc(mm_done, 1)

            def transposes(layer, stage, m):
                if stage == "gate":
                    pe.wait_ge(x_new, x_count(layer, "ffn", m))
                    src = x[:, m, :]
                else:
                    n = pre_count(layer, stage, m)
                    pe.wait_ge(xn_ready, n)
                    src = xn[(n - 1) % 2][:, :]
                for half in range(2):
                    for k in range(4):
                        kk = 4 * half + k
                        last = pe.transpose(banks[2 * m + half][:, k * P:(k + 1) * P],
                                            src[:, kk * P:(kk + 1) * P], T_("ident"))
                    last.then_inc(x_T, 1)

            def rows(g):
                return slice(HD * g, HD * (g + 1))

            pe.wait_ge(consts_loaded, 64)
            for layer in range(depth):
                for e in SCHEDULE:
                    kind = e[0]
                    if kind == "mm":
                        block_of(layer, e[1], e[2])
                    elif kind == "T":
                        transposes(layer, e[1], e[2])
                    elif kind == "swa_T":
                        c = e[1]
                        pe.wait_ge(cqk_roped, layer * TILES + c + 1)
                        if c:
                            pe.wait_ge(swa_cT, layer * TILES + c)
                        src = cqk[c % 2]
                        for j in range(3):
                            pe.transpose(banks[4][:, j * P:(j + 1) * P], src[:, j * P:(j + 1) * P], T_("ident"))
                        pe.transpose(banks[4][:, 3 * P:4 * P], src[:, 3 * P:4 * P],
                                     T_("ident")).then_inc(swa_T, 1)
                    elif kind in ("swa_cur", "swa_prev"):
                        c = e[1]
                        k0 = c if kind == "swa_cur" else c - 1
                        if k0 < 0:
                            continue
                        if kind == "swa_cur":
                            pe.wait_ge(swa_cT, layer * TILES + TILES)
                            if c:
                                pe.wait_ge(y_lo_ready, y_count(layer, ("swa_yT", c - 1)))
                        else:
                            pe.wait_ge(swa_S, layer * TILES + c + 1)
                        for g in range(2):
                            for j in range(3):
                                last = pe.matmul(banks[4 + g][:, j * P:(j + 1) * P],
                                                 cT[rows(g), j, ts(c)], cT[rows(g), 3, ts(k0)],
                                                 start=True, stop=True, skip_group_check=True)
                        last.then_inc(swa_cur if kind == "swa_cur" else swa_prev, 1)
                    elif kind == "swa_PT":
                        c = e[1]
                        pe.wait_ge(swa_exp, layer * TILES + c + 1)
                        for hh in range(C_HEADS):
                            last = pe.transpose(banks[4 + hh // 3][:, (hh % 3) * P:(hh % 3 + 1) * P],
                                                prob[:, hh, :], T_("ident"))
                        last.then_inc(swa_PT, 1)
                    elif kind == "swa_o":
                        c = e[1]
                        pe.wait_ge(swa_PTm, layer * TILES + c + 1)
                        for hh in range(C_HEADS):
                            o = banks[4][:, hh * HD:(hh + 1) * HD]
                            g = hh // 3
                            last = pe.matmul(o, ptl[:, hh, :], cv[:, c, rows(g)], start=True, stop=(c == 0),
                                             skip_group_check=True)
                            if c:
                                last = pe.matmul(o, ptu[:, hh, :], cv[:, c - 1, rows(g)], start=False,
                                                 stop=True, skip_group_check=True)
                        last.then_inc(swa_o, 1)
                    elif kind == "swa_yT":
                        c = e[1]
                        pe.wait_ge(swa_yr, layer * TILES + c + 1)
                        flat = swa_y[:, :, :].rearrange("p h d -> p (h d)")
                        for k in range(3):
                            last = pe.transpose(banks[5][:, k * P:(k + 1) * P], flat[:, k * P:(k + 1) * P],
                                                T_("ident"))
                        last.then_inc(y_T, 1)
                    elif kind == "ret_T":
                        c = e[1]
                        pe.wait_ge(b_roped, layer * 2 * TILES + TILES + c + 1)
                        if c:
                            pe.wait_ge(ret_oread, layer * TILES + c)
                            pe.wait_ge(ret_state, layer * 3 + c)
                        for i, src in enumerate((bk, bq)):
                            for j in range(3):
                                last = pe.transpose(banks[6 + i][:, j * P:(j + 1) * P],
                                                    src[:, c, j * P:(j + 1) * P], T_("ident"))
                        last.then_inc(ret_T, 1)
                    elif kind == "ret_sc":
                        c = e[1]
                        pe.wait_ge(ret_kqT, layer * TILES + c + 1)
                        if c:
                            pe.wait_ge(y_lo_ready, y_count(layer, ("ret_yT", c - 1)))
                        for g in range(2):
                            for j in range(3):
                                last = pe.matmul(banks[6 + g][:, j * P:(j + 1) * P], kqT[rows(g), 0, j, :],
                                                 kqT[rows(g), 1, j, :], start=True, stop=True,
                                                 skip_group_check=True)
                        last.then_inc(ret_sc, 1)
                    elif kind == "ret_o":
                        c = e[1]
                        pe.wait_ge(ret_scm, layer * TILES + c + 1)
                        if c == 0:
                            pe.wait_ge(evac_act, evac(layer, "bv", 3)[1])
                        else:
                            pe.wait_ge(ret_state, layer * 3 + c)
                        for j in range(3):
                            if c:
                                pe.matmul(banks[6][:, j * P:(j + 1) * P], kqT[:, 1, j, :], state[:, j, :],
                                          start=True, stop=False, skip_group_check=True)
                            for g in range(2):
                                cols = slice(j * P + g * HD, j * P + (g + 1) * HD)
                                last = pe.matmul(banks[6][:, cols], scm[:, g, j, :], bv[:, c, cols],
                                                 start=(c == 0), stop=True, skip_group_check=True)
                        last.then_inc(ret_o, 1)
                        if c < TILES - 1:
                            for j in range(3):
                                last = pe.matmul(banks[7][:, j * P:(j + 1) * P], bk[:, c, j * P:(j + 1) * P],
                                                 bv[:, c, j * P:(j + 1) * P], start=True, stop=True,
                                                 skip_group_check=True)
                            last.then_inc(ret_kv, 1)
                    elif kind == "ret_yT":
                        c = e[1]
                        pe.wait_ge(ret_yr, layer * TILES + c + 1)
                        if c < TILES - 1:
                            pe.wait_ge(ret_kqT, layer * TILES + c + 2)
                        for k in range(3):
                            last = pe.transpose(banks[6][:, k * P:(k + 1) * P], ret_y[:, k * P:(k + 1) * P],
                                                T_("ident"))
                        last.then_inc(y_T, 1)
                    elif kind == "gmlp_mix":
                        pe.wait_ge(gm_vn, layer * TILES + TILES)
                        pe.wait_ge(ws_ready, layer + 1)
                        pe.wait_ge(y_lo_ready, y_count(layer, ("ret_yT", 3)))
                        for c in range(TILES):
                            for hh in range(A_HEADS):
                                col = (c % 2) * AW + hh * HD
                                last = pe.matmul(banks[6 + c // 2][:, col:col + HD], wsT[:, hh, :],
                                                 vn[:, c, hh * HD:(hh + 1) * HD], start=True, stop=True,
                                                 skip_group_check=True)
                        last.then_inc(gm_mix, 1)
                    elif kind == "gmlp_yT":
                        pe.wait_ge(gm_ya, layer + 1)
                        for k in range(2):
                            for c in range(TILES):
                                last = pe.transpose(banks[6 + k][:, c * P:(c + 1) * P],
                                                    uv[:, c, k * P:(k + 1) * P], T_("ident"))
                            last.then_inc(y_T, 1)

        @block.scalar
        def _(act):
            def y_split(layer, e, bank, dst):
                n = y_count(layer, e)
                act.wait_ge(y_T, n)
                act.activation(dst, bank, ACT.Copy).then_inc(y_hi_ready, 1)

            def conv(g):
                if g >= depth * NS:
                    return
                n = piece_size(g)
                if g >= SLOTS:
                    act.wait_ge(mm_done, used_count(g - SLOTS))
                for j in range(2):
                    q = 2 * g + j
                    act.wait_ge(raw_loaded[q % RAWS], 16 * (q // RAWS + 1))
                    act.activation(w_hi[g % SLOTS][:, j * n:(j + 1) * n], raw[q % RAWS][:, 0:n],
                                   ACT.Copy).then_inc(hi_ready, 1)

            squares = [0, 0]

            def after_squares():
                if squares[0]:
                    act.wait_ge(pre_sq, squares[0])
                if squares[1]:
                    act.wait_ge(post_sq, squares[1])

            def pre(layer, stage, m):
                n = pre_count(layer, stage, m)
                if layer == 0 and stage == "mix":
                    act.wait_ge(x_loaded[m], 16)
                elif stage == "mix":
                    act.wait_ge(x_new, x_count(layer - 1, "gate", m))
                else:
                    act.wait_ge(x_new, x_count(layer, "mix", m))
                if n > 2:
                    act.wait_ge(pre_r, n - 2)
                after_squares()
                squares[0] += 1
                act.activation(junk[:], x[:, m, :], ACT.Square, scale=D ** -0.5,
                               accum_out=ss_pre[n % 2]).then_inc(pre_sq, 1)

            for m in range(TILES):
                pre(0, "mix", m)
                if m < SLOTS:
                    conv(m)
            for layer in range(depth):
                for e in SCHEDULE:
                    kind = e[0]
                    if kind == "conv":
                        conv(layer * NS + e[1])
                    elif kind == "T":
                        _, stage, m = e
                        for half in range(2):
                            dst = h_hi[:, 4 * half:4 * half + 4, m * P:(m + 1) * P]
                            if stage == "gate":
                                act.wait_ge(x_T, t_count(layer, stage, m, half))
                                src = banks[2 * m + half][:, :].rearrange("p (k t) -> p k t", k=4)
                            else:
                                act.wait_ge(hT_ready, hT_count(layer, stage, m, half))
                                src = hT[half][:]
                            act.activation(dst, src, ACT.Copy).then_inc(h_hi_ready, 1)
                    elif kind == "post":
                        _, stage, m = e
                        n = post_count(layer, stage, m)
                        strip = {"mix": ("out", None, 0), "ffn": ("fo", None, FCH // 2 - 1),
                                 "ple": ("ple", None, 0)}[stage]
                        act.wait_ge(mm_done, mm_count(layer, strip, m))
                        if n > 2:
                            act.wait_ge(post_r, n - 2)
                        after_squares()
                        squares[1] += 2
                        act.activation(junk[:, 0:512], banks[2 * m][:, :], ACT.Square, scale=D ** -0.5,
                                       accum_out=ss_post[n % 2][:, 0:1]).then_inc(post_sq, 1)
                        act.activation(junk[:, 512:D], banks[2 * m + 1][:, :], ACT.Square, scale=D ** -0.5,
                                       accum_out=ss_post[n % 2][:, 1:2]).then_inc(post_sq, 1)
                        if stage == "ffn" and m == 0:
                            act.wait_ge(p_loaded, 16 * (layer + 1))
                            act.activation(p_hi[:], p_raw[:], ACT.Copy).then_inc(p_hi_ready, 1)
                    elif kind == "pre":
                        _, stage, m = e
                        if stage == "ffn":
                            pre(layer, "ffn", m)
                        elif layer + 1 < depth:
                            pre(layer + 1, "mix", m)
                    elif kind == "gated":
                        m = e[1]
                        act.wait_ge(mm_done, mm_count(layer, ("gate", None, 3), m))
                        if m or layer:
                            act.wait_ge(x_new, x_count(layer, "gate", m) - 1)
                        act.activation(sig[:, 0:512], banks[2 * m][:, :], ACT.Sigmoid)
                        act.activation(sig[:, 512:D], banks[2 * m + 1][:, :], ACT.Sigmoid).then_inc(sig_ready, 1)
                    elif kind == "mid":
                        j = e[1]
                        act.wait_ge(mm_done, mm_count(layer, ("ffn", None, j), 3 if j < 3 else None))
                        if j or layer:
                            act.wait_ge(prod_ready, layer * FCH + j)
                        if j == 0:
                            act.wait_ge(gm_vn, (layer + 1) * TILES)
                        act.activation(silu_g[:], banks[2 * (j % 4)][:, :], ACT.Silu).then_inc(silu_ready, 1)
                        act.wait_ge(prod_ready, layer * FCH + j + 1)
                        act.activation(mid_hi[:, j, :], banks[2 * (j % 4) + 1][:, :],
                                       ACT.Copy).then_inc(mid_hi_ready, 1)
                    elif kind == "swa_T":
                        c = e[1]
                        act.wait_ge(swa_T, layer * TILES + c + 1)
                        act.activation(cT[:, :, c * P:(c + 1) * P],
                                       banks[4][:, :].rearrange("p (k t) -> p k t", k=4),
                                       ACT.Copy).then_inc(swa_cT, 1)
                    elif kind == "swa_cur":
                        c = e[1]
                        act.wait_ge(swa_cur, layer * TILES + c + 1)
                        if c:
                            act.wait_ge(y_T, y_count(layer, ("swa_yT", c - 1)))
                        for g in range(2):
                            last = act.activation(prob[:, 3 * g:3 * g + 3, :],
                                                  banks[4 + g][:, 0:BW].rearrange("p (h t) -> p h t", h=3),
                                                  ACT.Copy)
                        last.then_inc(swa_S, 1)
                    elif kind == "swa_prev":
                        c = e[1]
                        act.wait_ge(swa_m, layer * TILES + c + 1)
                        for hh in range(C_HEADS):
                            act.activation(prob[:, hh, :], prob[:, hh, :], ACT.Exp, bias=negm[:, hh:hh + 1],
                                           accum_out=lsum[:, hh:hh + 1])
                        act.activation(esink, dsink, ACT.Exp).then_inc(swa_exp, 1)
                    elif kind == "swa_yT":
                        c = e[1]
                        y_split(layer, e, banks[5][:, 0:BW].rearrange("p (k t) -> p k t", k=3),
                                y_hi[:, 5:8, c * P:(c + 1) * P])
                    elif kind == "ret_T":
                        c = e[1]
                        act.wait_ge(ret_T, layer * TILES + c + 1)
                        for i in range(2):
                            last = act.activation(kqT[:, i, :, :],
                                                  banks[6 + i][:, 0:BW].rearrange("p (k t) -> p k t", k=3),
                                                  ACT.Copy)
                        last.then_inc(ret_kqT, 1)
                    elif kind == "ret_yT":
                        c = e[1]
                        y_split(layer, e, banks[6][:, 0:BW].rearrange("p (k t) -> p k t", k=3),
                                y_hi[:, 2:5, c * P:(c + 1) * P])
                    elif kind == "gmlp_yT":
                        n = y_count(layer, e)
                        for k in range(2):
                            act.wait_ge(y_T, n - 1 + k)
                            act.activation(y_hi[:, k, :], banks[6 + k][:, :], ACT.Copy).then_inc(y_hi_ready, 1)
                    elif kind == "mm" and e[1][0] == "in":
                        _, strip, m = e
                        name = strip[1]
                        if strip != group_final(name) or name not in ACT_EVAC:
                            continue
                        act.wait_ge(mm_done, mm_count(layer, strip, m))
                        if name == "cqk":
                            if m >= 2:
                                act.wait_ge(swa_T, layer * TILES + m - 1)
                            act.activation(cqk[m % 2][:, 0:BW].rearrange("p (j g d) -> p g j d", j=3, g=2),
                                           banks[m][:, 0:BW].rearrange("p (g j d) -> p g j d", j=3, g=2),
                                           ACT.Copy, scale=HD ** -0.5)
                            act.activation(cqk[m % 2][:, BW:512], banks[m][:, BW:512],
                                           ACT.Copy).then_inc(evac_act, 1)
                        elif name == "cv":
                            act.activation(cv[:, m, :], banks[m][:, 0:P], ACT.Copy).then_inc(evac_act, 1)
                        elif name == "bv":
                            act.activation(bv[:, m, :], banks[m][:, 0:BW], ACT.Copy).then_inc(evac_act, 1)
                        elif name == "bg":
                            act.activation(bg[:, m, :], banks[m][:, 0:BW], ACT.Silu).then_inc(evac_act, 1)
                        else:
                            if m == 0:
                                act.wait_ge(swa_prev, (layer + 1) * 3)
                            act.activation(uv[:, m, :], banks[m][:, :], ACT.Gelu_apprx_tanh).then_inc(evac_act, 1)

        @block.gpsimd
        def _(pool):
            steps = [0]

            def step(ins):
                steps[0] += 1
                ins.then_inc(pool_step, 1)
                pool.wait_ge(pool_step, steps[0])

            pool.memset(half_neg, -0.5).then_inc(pool_init, 1)
            pool.memset(neg_big, NEG).then_inc(pool_init, 1)
            pool.wait_ge(pool_init, 2)
            def pre(layer, stage, m):
                n = pre_count(layer, stage, m)
                pool.wait_ge(pre_sq, n)
                if n > 2:
                    pool.wait_ge(xn_ready, n - 2)
                if n > 1:
                    pool.wait_ge(pre_r, n - 1)
                step(pool.tensor_scalar(t_pre, ss_pre[n % 2], EPS, None, ALU.add))
                pool.tensor_tensor(r_pre[n % 2], t_pre, half_neg[:, 0:1], ALU.pow).then_inc(pre_r, 1)

            for m in range(TILES):
                pre(0, "mix", m)
            for layer in range(depth):
                for e in SCHEDULE:
                    kind = e[0]
                    if kind == "post":
                        n = post_count(layer, e[1], e[2])
                        pool.wait_ge(post_sq, 2 * n)
                        if n > 2:
                            pool.wait_ge(*post_used(n - 2))
                        if n > 1:
                            pool.wait_ge(post_r, n - 1)
                        step(pool.tensor_scalar(t_post, ss_post[n % 2][:, 0:1], ss_post[n % 2][:, 1:2], EPS,
                                                ALU.add, ALU.add))
                        pool.tensor_tensor(r_post[n % 2], t_post, half_neg[:, 0:1], ALU.pow).then_inc(post_r, 1)
                    elif kind == "pre":
                        if e[1] == "ffn":
                            pre(layer, "ffn", e[2])
                        elif layer + 1 < depth:
                            pre(layer + 1, "mix", e[2])
                    elif kind == "swa_cur" and e[1] == 0:
                        pool.wait_ge(ws_loaded, 16 * (layer + 1))
                        pool.affine_select(out=wsT[:], in_=wsT[:], compare_op=ALU.is_ge, fill=0.0, base=0,
                                           pattern=[[0, A_HEADS], [1, P]],
                                           channel_multiplier=-1).then_inc(ws_ready, 1)
                    elif kind == "ret_o":
                        n = layer * TILES + e[1] + 1
                        pool.wait_ge(ret_v, n)
                        if n > 1:
                            pool.wait_ge(ret_r, n - 1)
                        step(pool.tensor_scalar(rvt, rvar, 1.0 / HD, EPS, ALU.mult, ALU.add))
                        pool.tensor_tensor(rr, rvt, half_neg, ALU.pow).then_inc(ret_r, 1)
                    elif kind == "mm" and e[1] == group_final("a"):
                        n = layer * TILES + e[2] + 1
                        pool.wait_ge(gm_v, n)
                        if n > 1:
                            pool.wait_ge(gm_r, n - 1)
                        step(pool.tensor_scalar(gvt, gvar, 1.0 / HD, EPS, ALU.mult, ALU.add))
                        pool.tensor_tensor(gr, gvt, half_neg[:, 0:A_HEADS], ALU.pow).then_inc(gm_r, 1)

        @block.vector
        def _(dve):
            counts = {}

            def done(ins, signal):
                counts[signal.name] = counts.get(signal.name, 0) + 1
                ins.then_inc(signal, 1)
                dve.wait_ge(signal, counts[signal.name])

            def step(ins):
                done(ins, dve_step)

            def heads(ap, n):
                return ap.rearrange("p (h d) -> p h d", h=n)

            def conv(g):
                if g >= depth * NS:
                    return
                n = piece_size(g)
                for j in range(2):
                    q = 2 * g + j
                    dve.wait_ge(hi_ready, q + 1)
                    done(dve.tensor_tensor(w_lo[g % SLOTS][:, j * n:(j + 1) * n], raw[q % RAWS][:, 0:n],
                                      w_hi[g % SLOTS][:, j * n:(j + 1) * n].bitcast(F32),
                                      ALU.subtract), lo_ready)

            def pre(layer, stage, m):
                n = pre_count(layer, stage, m)
                dve.wait_ge(pre_r, n)
                if n > 2:
                    q = n - 3
                    lay, r = divmod(q, 2 * TILES)
                    dve.wait_ge(x_T, t_count(lay, "ffn" if r >= TILES else "mix", r % TILES))
                done(dve.tensor_scalar(xn[(n - 1) % 2][:], x[:, m, :], r_pre[n % 2], None,
                                  ALU.mult), xn_ready)

            def rope_full(layer, which, m):
                dst = (bk, bq)[which]
                src = banks[m][:, 0:BW]
                sc = (T_("ks"), T_("qs"))[which]
                done(dve.tensor_tensor(heads(rope_x[:], 6), heads(src, 6), sc[:, :, None].to_broadcast([P, 6, HD]),
                                  ALU.mult), evac_dve)
                dve.wait_ge(evac_dve, evac(layer, DVE_EVAC[which], m)[1])
                xr = rope_x[:].rearrange("p (h s d) -> p h s d", h=6, s=2)
                ar = rope_a[:].rearrange("p (h s d) -> p h s d", h=6, s=2)
                br = rope_b[:].rearrange("p (h s d) -> p h s d", h=6, s=2)
                cos = T_("rcos")[:, m * 32:(m + 1) * 32][:, None, None, :].to_broadcast([P, 6, 2, 32])
                sin = T_("rsin")[:, m * 32:(m + 1) * 32][:, None, None, :].to_broadcast([P, 6, 2, 32])
                done(dve.tensor_tensor(ar, xr, cos, ALU.mult), dve_step)
                step(dve.tensor_tensor(br, xr, sin, ALU.mult))
                o = dst[:, m, :].rearrange("p (h s d) -> p h s d", h=6, s=2)
                done(dve.tensor_tensor(o[:, :, 0, :], ar[:, :, 0, :], br[:, :, 1, :], ALU.subtract), dve_step)
                done(dve.tensor_tensor(o[:, :, 1, :], ar[:, :, 1, :], br[:, :, 0, :], ALU.add), b_roped)

            def rope_part(layer, m):
                hs = heads(cqk[m % 2][:], 8)
                xr = hs[:, :, 0:16].rearrange("p h (s d) -> p h s d", s=2)
                ar = rope_a[:, 0:128].rearrange("p (h s d) -> p h s d", h=8, s=2)
                br = rope_b[:, 0:128].rearrange("p (h s d) -> p h s d", h=8, s=2)
                cos = T_("scos")[:, m * 8:(m + 1) * 8][:, None, None, :].to_broadcast([P, 8, 2, 8])
                sin = T_("ssin")[:, m * 8:(m + 1) * 8][:, None, None, :].to_broadcast([P, 8, 2, 8])
                done(dve.tensor_tensor(ar, xr, cos, ALU.mult), dve_step)
                step(dve.tensor_tensor(br, xr, sin, ALU.mult))
                done(dve.tensor_tensor(xr[:, :, 0, :], ar[:, :, 0, :], br[:, :, 1, :], ALU.subtract), dve_step)
                done(dve.tensor_tensor(xr[:, :, 1, :], ar[:, :, 1, :], br[:, :, 0, :], ALU.add), cqk_roped)

            def y_split(layer, e, bank, hi, lo):
                dve.wait_ge(y_hi_ready, y_count(layer, e))
                done(dve.tensor_tensor(lo, bank, hi.bitcast(F32), ALU.subtract), y_lo_ready)

            def mask3(ap):
                return ap[:, None, :].to_broadcast([P, 3, P])

            dve.wait_ge(pool_init, 2)
            dve.wait_ge(consts_loaded, 64)
            for m in range(TILES):
                pre(0, "mix", m) if m < 2 else None
                if m < SLOTS:
                    conv(m)
            for layer in range(depth):
                for e in SCHEDULE:
                    kind = e[0]
                    if kind == "conv":
                        conv(layer * NS + e[1])
                    elif kind == "T":
                        _, stage, m = e
                        for half in range(2):
                            bank = banks[2 * m + half][:, :].rearrange("p (k t) -> p k t", k=4)
                            hi = h_hi[:, 4 * half:4 * half + 4, m * P:(m + 1) * P]
                            lo = h_lo[:, 4 * half:4 * half + 4, m * P:(m + 1) * P]
                            src = bank
                            if stage != "gate":
                                dve.wait_ge(x_T, t_count(layer, stage, m, half))
                                w = prew[:, 0 if stage == "mix" else 1, layer, 4 * half:4 * half + 4]
                                done(dve.tensor_tensor(hT[half][:], bank, w[:, :, None].to_broadcast([P, 4, P]),
                                                  ALU.mult), hT_ready)
                        for half in range(2):
                            bank = banks[2 * m + half][:, :].rearrange("p (k t) -> p k t", k=4)
                            hi = h_hi[:, 4 * half:4 * half + 4, m * P:(m + 1) * P]
                            lo = h_lo[:, 4 * half:4 * half + 4, m * P:(m + 1) * P]
                            src = bank if stage == "gate" else hT[half][:]
                            dve.wait_ge(h_hi_ready, t_count(layer, stage, m, half))
                            done(dve.tensor_tensor(lo, src, hi.bitcast(F32), ALU.subtract), h_lo_ready)
                        if stage == "mix" and m < 2:
                            pre(layer, "mix", m + 2)
                    elif kind == "post":
                        _, stage, m = e
                        n = post_count(layer, stage, m)
                        if stage == "ple":
                            dve.wait_ge(ple_w_loaded, 16 * (layer + 1))
                        else:
                            dve.wait_ge(post_w_loaded, 16 * (2 * layer + (1 if stage == "mix" else 2)))
                        dve.wait_ge(post_r, n)
                        wrow = ple_w if stage == "ple" else post_w
                        for half in range(2):
                            c = slice(half * 512, half * 512 + 512)
                            dst = ple_n[:, m, c] if stage == "ple" else upd[:, c]
                            last = dve.scalar_tensor_tensor(out=dst, in0=banks[2 * m + half][:, :],
                                                            scalar=r_post[n % 2], in1=wrow[:, c],
                                                            op0=ALU.mult, op1=ALU.mult)
                        if stage == "ple":
                            done(last, ple_ready)
                        else:
                            step(last)
                            done(dve.tensor_tensor(x[:, m, :], x[:, m, :], upd[:], ALU.add), x_new)
                        if stage == "ffn" and m == 0:
                            dve.wait_ge(p_hi_ready, layer + 1)
                            done(dve.tensor_tensor(p_lo[:], p_raw[:], p_hi[:].bitcast(F32),
                                              ALU.subtract), p_lo_ready)
                    elif kind == "pre":
                        if e[1] == "ffn":
                            pre(layer, "ffn", e[2])
                        elif layer + 1 < depth and e[2] < 2:
                            pre(layer + 1, "mix", e[2])
                    elif kind == "gated":
                        m = e[1]
                        dve.wait_ge(sig_ready, layer * TILES + m + 1)
                        dve.wait_ge(ple_ready, layer * TILES + m + 1)
                        step(dve.tensor_tensor(sig[:], sig[:], ple_n[:, m, :], ALU.mult))
                        done(dve.tensor_tensor(x[:, m, :], x[:, m, :], sig[:], ALU.add), x_new)
                    elif kind == "mid":
                        j = e[1]
                        b = 2 * (j % 4) + 1
                        dve.wait_ge(silu_ready, layer * FCH + j + 1)
                        done(dve.tensor_tensor(banks[b][:, :], silu_g[:], banks[b][:, :], ALU.mult), prod_ready)
                        dve.wait_ge(mid_hi_ready, layer * FCH + j + 1)
                        done(dve.tensor_tensor(mid_lo[:, j, :], banks[b][:, :], mid_hi[:, j, :].bitcast(F32),
                                          ALU.subtract), mid_lo_ready)
                    elif kind == "swa_prev":
                        c = e[1]
                        dve.wait_ge(swa_S, layer * TILES + c + 1)
                        if c == 0:
                            dve.wait_ge(params_loaded, 16 * 5 * (layer + 1))
                        else:
                            dve.wait_ge(swa_prev, layer * 3 + c)
                        for g in range(2):
                            old = (banks[4 + g][:, 0:BW].rearrange("p (h t) -> p h t", h=3) if c
                                   else neg_big[:, :, None].to_broadcast([P, 3, P]))
                            last = dve.copy_predicated(prob[:, 3 * g:3 * g + 3, :], mask3(later_m[:]), old)
                        step(last)
                        step(dve.tensor_reduce(mx, prob[:], AX.X, ALU.max))
                        step(dve.tensor_tensor(mx, mx, snk, ALU.max))
                        done(dve.tensor_scalar(negm, mx, -1.0, None, ALU.mult), dve_step)
                        done(dve.tensor_tensor(dsink, snk, mx, ALU.subtract), swa_m)
                    elif kind == "swa_PT":
                        c = e[1]
                        dve.wait_ge(swa_PT, layer * TILES + c + 1)
                        for g in range(2):
                            b3 = banks[4 + g][:, 0:BW].rearrange("p (h t) -> p h t", h=3)
                            last = dve.tensor_tensor(ptl[:, 3 * g:3 * g + 3, :], b3, mask3(T_("lowT")), ALU.mult)
                            if c:
                                last = dve.tensor_tensor(ptu[:, 3 * g:3 * g + 3, :], b3, mask3(T_("upT")),
                                                         ALU.mult)
                        done(last, swa_PTm)
                    elif kind == "swa_o":
                        c = e[1]
                        dve.wait_ge(swa_exp, layer * TILES + c + 1)
                        step(dve.tensor_tensor(rl, lsum, esink, ALU.add))
                        step(dve.reciprocal(rl, rl))
                        dve.wait_ge(swa_o, layer * TILES + c + 1)
                        done(dve.tensor_tensor(swa_y[:], heads(banks[4][:, 0:BW], 6),
                                          rl[:, :, None].to_broadcast([P, 6, HD]), ALU.mult), swa_yr)
                    elif kind == "swa_yT":
                        c = e[1]
                        y_split(layer, e, banks[5][:, 0:BW].rearrange("p (k t) -> p k t", k=3),
                                y_hi[:, 5:8, c * P:(c + 1) * P], y_lo[:, 5:8, c * P:(c + 1) * P])
                    elif kind == "ret_sc":
                        c = e[1]
                        dve.wait_ge(ret_sc, layer * TILES + c + 1)
                        for g in range(2):
                            last = dve.tensor_tensor(scm[:, g, :, :],
                                                     banks[6 + g][:, 0:BW].rearrange("p (h t) -> p h t", h=3),
                                                     mask3(T_("lowT")), ALU.mult)
                        done(last, ret_scm)
                    elif kind == "ret_o":
                        c = e[1]
                        if c == 0:
                            step(dve.memset(state[:], 0.0))
                        dve.wait_ge(ret_o, layer * TILES + c + 1)
                        o = heads(banks[6][:, 0:BW], 6)
                        step(dve.tensor_reduce(rmu, o, AX.X, ALU.add))
                        step(dve.tensor_scalar(rmu, rmu, 1.0 / HD, None, ALU.mult))
                        if c:
                            pass
                        done(dve.tensor_tensor(heads(ret_oc[:], 6), o, rmu[:, :, None].to_broadcast([P, 6, HD]),
                                          ALU.subtract), ret_oread)
                        dve.wait_ge(ret_oread, layer * TILES + c + 1)
                        step(dve.tensor_tensor(ret_sq[:], ret_oc[:], ret_oc[:], ALU.mult))
                        done(dve.tensor_reduce(rvar, heads(ret_sq[:], 6), AX.X, ALU.add), ret_v)
                        if c < TILES - 1:
                            dve.wait_ge(ret_kv, layer * 3 + c + 1)
                            for g in range(2):
                                r, q = slice(HD * g, HD * (g + 1)), slice(HD * g, HD * (g + 1))
                                st = state[r, :, q]
                                kv = banks[7][:, 0:BW].rearrange("p (j e) -> p j e", j=3)[r, :, q]
                                step(dve.tensor_tensor(st, st, kv, ALU.add))
                                last = dve.tensor_tensor(st, st, T_("gcol")[r, :, None].to_broadcast([HD, 3, HD]),
                                                         ALU.mult)
                            done(last, ret_state)
                    elif kind == "ret_norm":
                        c = e[1]
                        dve.wait_ge(gs_ready, layer * TILES + c + 1)
                        dve.wait_ge(ret_r, layer * TILES + c + 1)
                        step(dve.tensor_tensor(heads(ret_oc[:], 6), heads(ret_oc[:], 6),
                                               rr[:, :, None].to_broadcast([P, 6, HD]), ALU.mult))
                        if c:
                            dve.wait_ge(y_T, y_count(layer, ("ret_yT", c - 1)))
                        done(dve.tensor_tensor(ret_y[:], ret_oc[:], bg[:, c, :], ALU.mult), ret_yr)
                    elif kind == "ret_yT":
                        c = e[1]
                        y_split(layer, e, banks[6][:, 0:BW].rearrange("p (k t) -> p k t", k=3),
                                y_hi[:, 2:5, c * P:(c + 1) * P], y_lo[:, 2:5, c * P:(c + 1) * P])
                    elif kind == "gmlp_mix":
                        dve.wait_ge(gm_mix, layer + 1)
                        for b in range(2):
                            mixed = banks[6 + b][:, :].rearrange("p (c h d) -> p c h d", c=2, h=A_HEADS)
                            bias = bs[:, None, :, None].to_broadcast([P, 2, A_HEADS, HD])
                            done(dve.tensor_tensor(vn[:, 2 * b:2 * b + 2, :].rearrange("p c (h d) -> p c h d", h=A_HEADS),
                                              mixed, bias, ALU.add), dve_step)
                        step(dve.tensor_scalar(gvt, gvt, 1.0, None, ALU.mult))
                        u = uv[:, :, 0:AW]
                        done(dve.tensor_tensor(u, u, vn[:], ALU.mult), gm_ya)
                    elif kind == "gmlp_yT":
                        n = y_count(layer, e)
                        for k in range(2):
                            dve.wait_ge(y_hi_ready, n - 1 + k)
                            done(dve.tensor_tensor(y_lo[:, k, :], banks[6 + k][:, :], y_hi[:, k, :].bitcast(F32),
                                              ALU.subtract), y_lo_ready)
                    elif kind == "mm" and e[1][0] == "in":
                        _, strip, m = e
                        name = strip[1]
                        if strip != group_final(name):
                            continue
                        if name == "cqk":
                            dve.wait_ge(evac_act, evac(layer, name, m)[1])
                            rope_part(layer, m)
                        elif name in DVE_EVAC:
                            dve.wait_ge(mm_done, mm_count(layer, strip, m))
                            rope_full(layer, DVE_EVAC.index(name), m)
                        elif name == "bg":
                            dve.wait_ge(evac_act, evac(layer, name, m)[1])
                            if m == 0:
                                dve.wait_ge(params_loaded, 16 * 5 * (layer + 1))
                            done(dve.tensor_tensor(bg[:, m, :], bg[:, m, :], gnw[:], ALU.mult), gs_ready)
                        elif name == "a":
                            dve.wait_ge(evac_act, evac(layer, name, m)[1])
                            v = heads(uv[:, m, AW:2 * AW], A_HEADS)
                            vch = heads(vc[:], A_HEADS)
                            step(dve.tensor_reduce(gmu, v, AX.X, ALU.add))
                            step(dve.tensor_scalar(gmu, gmu, 1.0 / HD, None, ALU.mult))
                            step(dve.tensor_tensor(vch, v, gmu[:, :, None].to_broadcast([P, A_HEADS, HD]),
                                                   ALU.subtract))
                            step(dve.tensor_tensor(vsq[:], vc[:], vc[:], ALU.mult))
                            done(dve.tensor_reduce(gvar, heads(vsq[:], A_HEADS), AX.X, ALU.add), gm_v)
                            dve.wait_ge(gm_r, layer * TILES + m + 1)
                            step(dve.tensor_tensor(vch, vch, gr[:, :, None].to_broadcast([P, A_HEADS, HD]),
                                                   ALU.mult))
                            step(dve.tensor_tensor(vc[:], vc[:], lnw[:], ALU.mult))
                            done(dve.tensor_tensor(vn[:, m, :], vc[:], lnb[:], ALU.add), gm_vn)


_ORDER = ["x_in", "p_t", "pre_mix", "w_in", "ln_w", "ln_b", "ws_t", "bs_t", "gn_w", "sinks", "w_out",
          "post_mix", "pre_ffn", "w_ffn_in", "w_ffn_out", "post_ffn", "w_gate", "w_ple", "ple_norm",
          "table", "later"]


def kernel(x, p, norm_mix_pre, w_in, gmlp_ln_w, gmlp_ln_b, gmlp_ws, gmlp_bs, ret_gn_w, attn_sinks,
           w_out, norm_mix_post, norm_ffn_pre, w_ffn_in, w_ffn_out, norm_ffn_post, w_ple_gate,
           w_ple_proj, ple_norm):
    import concourse.bacc as bacc
    from concourse.bass_utils import run_bass_kernel_spmd

    depth = w_in.shape[0]
    table, later = small_tables()
    cols = lambda w: np.asarray(w).reshape(depth, KD, P).transpose(2, 0, 1)
    values = {
        "x_in": np.asarray(x)[0],
        "p_t": np.asarray(p)[:, 0].transpose(0, 2, 1),
        "pre_mix": cols(norm_mix_pre), "pre_ffn": cols(norm_ffn_pre),
        "w_in": w_in, "ln_w": gmlp_ln_w, "ln_b": gmlp_ln_b,
        "ws_t": np.asarray(gmlp_ws).transpose(0, 3, 1, 2),
        "bs_t": np.asarray(gmlp_bs).transpose(0, 2, 1),
        "gn_w": ret_gn_w, "sinks": attn_sinks, "w_out": w_out, "post_mix": norm_mix_post,
        "w_ffn_in": w_ffn_in, "w_ffn_out": w_ffn_out, "post_ffn": norm_ffn_post,
        "w_gate": w_ple_gate, "w_ple": w_ple_proj, "ple_norm": ple_norm,
        "table": table, "later": later,
    }
    nc = bacc.Bacc("TRN2", target_bir_lowering=False, num_devices=1)
    arrays, args = {}, []
    for name in _ORDER:
        a = np.ascontiguousarray(values[name])
        arrays[f"in_{name}"] = a
        args.append(nc.dram_tensor(f"in_{name}", a.shape, mybir.dt.from_np(a.dtype), kind="ExternalInput").ap())
    out = nc.dram_tensor("out", [S, D], F32, kind="ExternalOutput").ap()
    build_trunk(nc, depth, *args, out)
    r = run_bass_kernel_spmd(nc, [arrays], core_ids=[0])
    return r.results[0]["out"].reshape(1, S, D)
```

```python
import numpy as np

import concourse.bass as bass
from concourse import mybir

F32 = mybir.dt.float32
F32R = mybir.dt.float32r
BF16 = mybir.dt.bfloat16
I32 = mybir.dt.int32
ALU = mybir.AluOpType
ACT = mybir.ActivationFunctionType
AX = mybir.AxisListType

P = 128
D = 1024
S = 512
TILES = S // P
KD = D // P
HD = 64
A_HEADS = 4
B_HEADS = 6
C_HEADS = 6
BW = B_HEADS * HD
AW = A_HEADS * HD
FF = 2816
FCH = FF // P
PLE = 256
EPS = 1e-6
NEG = -1e30
SLOTS = 3
RAWS = 3
PIECE = 1024

GROUPS = {
    "ckv": (2 * AW + 5 * BW, 256),
    "cq": (2 * AW + 4 * BW, BW),
    "bk": (2 * AW + BW, BW),
    "bq": (2 * AW, BW),
    "bv": (2 * AW + 2 * BW, BW),
    "bg": (2 * AW + 3 * BW, BW),
    "a": (0, 2 * AW),
}
GNAMES = list(GROUPS)


def plan_strips():
    strips = []
    for g, (_, width) in GROUPS.items():
        n = 1 if width == 256 else 2
        strips += [("in", g, i) for i in range(n)]
    strips += [("out", None, i) for i in (3, 2, 1, 0)]
    strips += [("ffn", None, j) for j in range(FCH)]
    strips += [("fo", None, i) for i in range(FCH // 2)]
    strips += [("ple", None, 0)]
    strips += [("gate", None, i) for i in range(4)]
    return strips


STRIPS = plan_strips()
NS = len(STRIPS)
SIDX = {s: i for i, s in enumerate(STRIPS)}


def plan_schedule():
    ev = []
    done = set()

    def mm(strip, m):
        ev.append(("mm", strip, m))

    def close(strip):
        ev.append(("conv", SIDX[strip] + SLOTS))
        done.add(strip)

    at = {}

    def put(u, *e):
        at.setdefault(u, []).append(e)

    for c in range(TILES):
        put(9 + c, "swa_T", c)
        u = 13 + 6 * c
        put(u, "swa_cur", c)
        put(u + 1, "swa_prev", c)
        put(u + 6, "swa_PT", c)
        put(u + 8, "swa_o", c)
        put(u + 10, "swa_yT", c)
    for c in range(TILES):
        u = 37 + 4 * c
        put(u, "ret_T", c)
        put(u + 2, "ret_sc", c)
        put(u + 3, "ret_o", c)
        put(u + 5, "ret_norm", c)
        if c < TILES - 1:
            put(u + 7, "ret_yT", c)
    at[40 + 12].insert(0, at[40 + 12].pop())
    for c in range(TILES - 2):
        at[44 + 4 * c].sort(key=lambda e: e[0] == "ret_o")
    put(55, "ret_yT", 3)
    ins = [s for s in STRIPS if s[0] == "in"]
    mm(ins[0], 0)
    mm(ins[0], 1)
    ev.append(("T", "mix", 2))
    mm(ins[0], 2)
    mm(ins[1], 0)
    mm(ins[1], 1)
    ev.append(("T", "mix", 3))
    mm(ins[0], 3)
    close(ins[0])
    u = 4
    for s in ins[1:]:
        for m in range(TILES):
            if u >= 6:
                mm(s, m)
            for e in at.pop(u, ()):
                ev.append(e)
            u += 1
        close(s)
    o = [s for s in STRIPS if s[0] == "out"]
    mm(o[0], 0)
    ev += at.pop(52)
    ev.append(("gmlp_mix",))
    mm(o[0], 1)
    ev += at.pop(54)
    mm(o[1], 0)
    ev += at.pop(55)
    ev.append(("gmlp_yT",))
    assert not at
    mm(o[1], 1)
    mm(o[0], 2)
    mm(o[0], 3)
    close(o[0])
    mm(o[1], 2)
    mm(o[1], 3)
    close(o[1])

    def tail(pair, renew, after):
        norm = {"ffn": ("pre", "ffn"), "next": ("pre", "mix"), "gate": None}[after]
        for m in range(TILES):
            mm(pair[0], m)
            if m >= 1:
                ev.append((*renew, m - 1))
            if m >= 2:
                ev.append(("T", after, m - 2))
            if m >= 1 and norm:
                ev.append((*norm, m - 1))
            mm(pair[1], m)
        close(pair[0])
        ev.append((*renew, TILES - 1))
        close(pair[1])

    tail(o[2:], ("post", "mix"), "ffn")
    f = [s for s in STRIPS if s[0] == "ffn"]
    mm(f[0], 0)
    ev.append(("T", "ffn", 2))
    ev.append(("pre", "ffn", 3))
    mm(f[1], 0)
    ev.append(("T", "ffn", 3))
    mm(f[2], 0)
    for j in range(3):
        mm(f[j], 1)
        close(f[j])
        ev.append(("mid", j))
    for j in range(3, FCH):
        mm(f[j], None)
        close(f[j])
        ev.append(("mid", j))
    fo = [s for s in STRIPS if s[0] == "fo"]
    for s in fo[:-2]:
        for m in (2, 3, 0, 1):
            mm(s, m)
        close(s)
    tail(fo[-2:], ("post", "ffn"), "gate")
    ple = ("ple", None, 0)
    g = [s for s in STRIPS if s[0] == "gate"]
    mm(ple, 0)
    ev.append(("T", "gate", 2))
    mm(ple, 1)
    ev.append(("post", "ple", 0))
    ev.append(("T", "gate", 3))
    mm(ple, 2)
    ev.append(("post", "ple", 1))
    mm(ple, 3)
    close(ple)
    ev.append(("post", "ple", 2))
    ev.append(("post", "ple", 3))
    for s in g[:2]:
        for m in range(TILES):
            mm(s, m)
        close(s)
    tail(g[2:], ("gated",), "next")
    ev.append(("pre", "mix", 3))
    return ev


SCHEDULE = plan_schedule()
BLOCKS = [e[1:] for e in SCHEDULE if e[0] == "mm"]
NB = len(BLOCKS)
BIDX = {b: i for i, b in enumerate(BLOCKS)}
STRIP_LAST = {s: max(i for i, b in enumerate(BLOCKS) if b[0] == s) for s in STRIPS}
ACT_EVAC = ["ckv", "cq", "bv", "bg", "a"]
DVE_EVAC = ["bk", "bq"]
POSTS = ["mix", "ffn", "ple"]
TSTAGES = ["mix", "ffn", "gate"]


def small_tables():
    f = np.float32
    pos = np.arange(S, dtype=f)

    def angles(half, theta):
        inv = (1.0 / (f(theta) ** (np.arange(half, dtype=f) / f(half)))).astype(f)
        a = (pos[:, None] * inv[None, :]).astype(f).reshape(TILES, P, half).transpose(1, 0, 2)
        return np.cos(a).astype(f).reshape(P, -1), np.sin(a).astype(f).reshape(P, -1)

    rc, rs = angles(HD // 2, 10000.0)
    sc, ss = angles(HD // 8, 500000.0)
    i = np.arange(P)
    lower_t = (i[:, None] <= i[None, :]).astype(f)
    upper_t = (i[:, None] > i[None, :]).astype(f)
    later = (i[None, :] > i[:, None]).astype(np.int32)
    g = np.log(1.0 - 2.0 ** (-5.0 - np.arange(B_HEADS, dtype=np.float64)))
    qs = np.exp((i[:, None] + 1.0) * g[None, :])
    ks = np.exp(-(i[:, None] + 1.0) * g[None, :]) * HD ** -0.5
    gc = np.exp(P * g)
    gcol = np.stack([np.where(i < HD, gc[2 * j], gc[2 * j + 1]) for j in range(3)], 1)
    table = np.concatenate([np.eye(P), rc, rs, sc, ss, lower_t, upper_t, qs, ks, gcol], 1)
    return np.ascontiguousarray(table.astype(f)), later


TABLE_COLS = {}
_at = 0
for _n, _w in (("ident", P), ("rcos", 128), ("rsin", 128), ("scos", 32), ("ssin", 32), ("lowT", P),
               ("upT", P), ("qs", 6), ("ks", 6), ("gcol", 3)):
    TABLE_COLS[_n] = (_at, _at + _w)
    _at += _w
TABLE_W = _at


def build_trunk(nc, depth, x_in, p_t, pre_mix, w_in, ln_w, ln_b, ws_t, bs_t, gn_w, sinks, w_out,
                post_mix, pre_ffn, w_ffn_in, w_ffn_out, post_ffn, w_gate, w_ple, ple_norm,
                table, later, out):
    KB = 1024
    BASE = (nc.sbuf_base + 31) // 32 * 32

    def place(name, shape, dt, kb):
        return nc.alloc_sbuf_tensor_at(name, shape, dt, offset=BASE + int(kb * KB))

    x = place("x", [P, TILES, D], F32, 0)
    h_hi = place("h_hi", [P, KD, S], F32R, 16)
    h_lo = place("h_lo", [P, KD, S], F32R, 32)
    mid_hi = place("mid_hi", [P, FCH, S], F32R, 48)
    mid_lo = place("mid_lo", [P, FCH, S], F32R, 92)
    raw = [place(f"raw{i}", [P, PIECE], F32, 136 + 4 * i) for i in range(RAWS)]
    w_hi = [place(f"w_hi{i}", [P, 2 * PIECE], F32R, 148 + 8 * i) for i in range(SLOTS)]
    w_lo = [place(f"w_lo{i}", [P, 2 * PIECE], F32R, 172 + 8 * i) for i in range(SLOTS)]
    post_w = place("post_w", [P, D], F32, 196)
    tab = place("tab", [P, TABLE_W], F32, 200)
    later_m = place("later_m", [P, P], I32, 203)
    tiny = place("tiny", [P, 192], F32, 203.5)
    gnw = place("gnw", [P, BW], F32, 204.25)
    lnw = place("lnw", [P, AW], F32, 205.75)
    lnb = place("lnb", [P, AW], F32, 206.75)
    silu_g = place("silu_g", [P, S], F32, 205.75)
    y_hi = place("y_hi", [P, KD, S], F32R, 48)
    y_lo = place("y_lo", [P, KD, S], F32R, 64)
    bg = place("bg", [P, TILES, BW], F32, 80)
    bv = place("bv", [P, TILES, BW], F32, 86)
    bk = place("bk", [P, TILES, BW], F32, 92)
    bq = place("bq", [P, TILES, BW], F32, 98)
    kqT = place("kqT", [P, 2, 3, P], F32, 104)
    scm = place("scm", [P, 2, 3, P], F32, 107)
    prob = [place(f"prob{i}", [P, C_HEADS, P], F32, (110, 48)[i]) for i in range(2)]
    ptl = [place(f"ptl{i}", [P, C_HEADS, P], F32, (113, 64)[i]) for i in range(2)]
    ptu = [place(f"ptu{i}", [P, C_HEADS, P], F32, (116, 54)[i]) for i in range(2)]
    swa_y = [place(f"swa_y{i}", [P, C_HEADS, HD], F32, (110, 48)[i]) for i in range(2)]
    cq = [place(f"cq{i}", [P, BW], F32, 113 + 1.5 * i) for i in range(2)]
    ck = place("ck", [P, TILES, P], F32, 116)
    rope_x = place("rope_x", [P, BW], F32, 119)
    rope_a = place("rope_a", [P, BW], F32, 120.5)
    rope_b = place("rope_b", [P, BW], F32, 122)
    ret_oc = place("ret_oc", [P, BW], F32, 119)
    ret_sq = place("ret_sq", [P, BW], F32, 120.5)
    ret_y = place("ret_y", [P, BW], F32, 122)
    cT = place("cT", [P, 4, S], F32, 123.5)
    uv = place("uv", [P, TILES, 2 * AW], F32, 123.5)
    cv = place("cv", [P, TILES, P], F32, 131.5)
    wsT = place("wsT", [P, A_HEADS, P], F32, 133.5)
    vn = place("vn", [P, TILES, AW], F32, 110)
    vc = place("vc", [P, AW], F32, 114)
    vsq = place("vsq", [P, AW], F32, 115)
    state = place("state", [P, 3, P], F32, 196)
    upd = place("upd", [P, D], F32, 92)
    xn = [place(f"xn{i}", [P, D], F32, 96 + 4 * i) for i in range(2)]
    junk = place("junk", [P, D], BF16, 104)
    hT = [place(f"hT{i}", [P, 4, P], F32, 106 + 2 * i) for i in range(2)]
    ple_n = place("ple_n", [P, TILES, D], F32, 48)
    ple_w = place("ple_w", [P, D], F32, 64)
    p_raw = place("p_raw", [P, 2, S], F32, 68)
    p_hi = place("p_hi", [P, 2, S], F32R, 72)
    p_lo = place("p_lo", [P, 2, S], F32R, 76)
    sig = place("sig", [P, D], F32, 80)

    def T_(name):
        a, b = TABLE_COLS[name]
        return tab[:, a:b]

    tiny_at = [0]

    def small(n):
        a = tiny_at[0]
        tiny_at[0] += n
        return tiny[:, a:a + n]

    prew = small(2 * depth * KD).rearrange("p (s l k) -> p s l k", s=2, l=depth)
    bs = small(A_HEADS)
    snk = small(C_HEADS)
    ss_post = [small(2) for _ in range(2)]
    r_post = [small(1) for _ in range(2)]
    ss_pre = [small(1) for _ in range(2)]
    t_pre = small(1)
    t_post = small(1)
    r_pre = [small(1) for _ in range(2)]
    half_neg = small(6)
    neg_big = small(1)
    mx = [small(6) for _ in range(2)]
    negm = [small(6) for _ in range(2)]
    lsum = [small(6) for _ in range(2)]
    esink = [small(6) for _ in range(2)]
    rl = [small(6) for _ in range(2)]
    dsink = [small(6) for _ in range(2)]
    rmu = small(6)
    rvar = small(6)
    rr = small(6)
    rvt = small(6)
    gmu = small(4)
    gvar = small(4)
    gvt = small(4)
    gr = small(4)

    banks = [nc.alloc_psum_tensor(f"bank{i}", [P, 512], F32) for i in range(8)]

    sems = {}

    def sem(name):
        sems[name] = nc.alloc_semaphore(name)
        return sems[name]

    x_loaded = [sem(f"x_loaded{m}") for m in range(TILES)]
    raw_loaded = [sem(f"raw_loaded{i}") for i in range(RAWS)]
    table_loaded = sem("table_loaded")
    consts_loaded = sem("consts_loaded")
    params_loaded = sem("params_loaded")
    ws_loaded = sem("ws_loaded")
    post_w_loaded = sem("post_w_loaded")
    ple_w_loaded = sem("ple_w_loaded")
    p_loaded = sem("p_loaded")
    stored = sem("stored")
    hi_ready = sem("hi_ready")
    lo_ready = sem("lo_ready")
    mm_done = sem("mm_done")
    x_T = sem("x_T")
    hT_ready = sem("hT_ready")
    h_hi_ready = sem("h_hi_ready")
    h_lo_ready = sem("h_lo_ready")
    post_sq = sem("post_sq")
    post_r = sem("post_r")
    x_new = sem("x_new")
    ple_ready = sem("ple_ready")
    pre_sq = sem("pre_sq")
    pre_r = sem("pre_r")
    xn_ready = sem("xn_ready")
    evac_act = sem("evac_act")
    evac_dve = sem("evac_dve")
    ck_roped = sem("ck_roped")
    cq_roped = sem("cq_roped")
    b_roped = sem("b_roped")
    gs_ready = sem("gs_ready")
    swa_T = sem("swa_T")
    swa_cT = sem("swa_cT")
    swa_cur = sem("swa_cur")
    swa_S = sem("swa_S")
    swa_prev = sem("swa_prev")
    swa_m = sem("swa_m")
    swa_exp = sem("swa_exp")
    swa_PT = sem("swa_PT")
    swa_PTm = sem("swa_PTm")
    swa_o = sem("swa_o")
    swa_yr = sem("swa_yr")
    ret_T = sem("ret_T")
    ret_kqT = sem("ret_kqT")
    ret_sc = sem("ret_sc")
    ret_scm = sem("ret_scm")
    ret_o = sem("ret_o")
    ret_kv = sem("ret_kv")
    ret_state = sem("ret_state")
    ret_oread = sem("ret_oread")
    ret_v = sem("ret_v")
    ret_r = sem("ret_r")
    ret_yr = sem("ret_yr")
    y_T = sem("y_T")
    y_hi_ready = sem("y_hi_ready")
    y_lo_ready = sem("y_lo_ready")
    ws_ready = sem("ws_ready")
    gm_v = sem("gm_v")
    gm_r = sem("gm_r")
    gm_vn = sem("gm_vn")
    gm_mix = sem("gm_mix")
    gm_ya = sem("gm_ya")
    silu_ready = sem("silu_ready")
    prod_ready = sem("prod_ready")
    mid_hi_ready = sem("mid_hi_ready")
    mid_lo_ready = sem("mid_lo_ready")
    p_hi_ready = sem("p_hi_ready")
    p_lo_ready = sem("p_lo_ready")
    sig_ready = sem("sig_ready")
    pool_step = sem("pool_step")
    pool_init = sem("pool_init")
    dve_step = sem("dve_step")

    order_yT = [e for e in SCHEDULE if e[0] in ("swa_yT", "ret_yT", "gmlp_yT")]
    NY = len(order_yT) + 1

    def y_count(layer, e):
        i = order_yT.index(e)
        return layer * NY + i + 1 + sum(f[0] == "gmlp_yT" for f in order_yT[:i + 1])

    order_T = [("T", "mix", 0), ("T", "mix", 1)] + [e for e in SCHEDULE if e[0] == "T" and e[1] != "next"]
    NT = 2 * len(order_T)

    def t_count(layer, stage, m, half=1):
        return layer * NT + 2 * order_T.index(("T", stage, m)) + half + 1

    order_hT = [e for e in order_T if e[1] != "gate"]
    NHT = 2 * len(order_hT)

    def hT_count(layer, stage, m, half):
        return layer * NHT + 2 * order_hT.index(("T", stage, m)) + half + 1

    order_post = [e for e in SCHEDULE if e[0] == "post"]

    def post_count(layer, stage, m):
        return layer * len(order_post) + order_post.index(("post", stage, m)) + 1

    def post_used(n):
        layer, i = divmod(n - 1, len(order_post))
        _, stage, m = order_post[i]
        if stage == "ple":
            return ple_ready, layer * TILES + m + 1
        return x_new, x_count(layer, stage, m)

    def of_stage(layer, stage):
        if stage != "next":
            return layer, stage
        return (layer + 1, "mix") if layer + 1 < depth else None

    def x_count(layer, stage, m):
        return layer * 3 * TILES + TSTAGES.index(stage) * TILES + m + 1

    def pre_count(layer, stage, m):
        return layer * 2 * TILES + (TILES if stage == "ffn" else 0) + m + 1

    def mm_count(layer, strip, m):
        return layer * NB + BIDX[(strip, m)] + 1

    def used_count(g):
        return (g // NS) * NB + STRIP_LAST[STRIPS[g % NS]] + 1

    def group_final(gname):
        n = 1 if GROUPS[gname][1] == 256 else 2
        return ("in", gname, n - 1)

    def evac(layer, gname, m):
        if gname in ACT_EVAC:
            return evac_act, layer * 4 * len(ACT_EVAC) + 4 * ACT_EVAC.index(gname) + m + 1
        return evac_dve, layer * 4 * len(DVE_EVAC) + 4 * DVE_EVAC.index(gname) + m + 1

    def pieces(g):
        layer, (kind, name, i) = g // NS, STRIPS[g % NS]

        def view(w, k0, kn, c0, cn):
            return w[layer, k0 * P:(k0 + kn) * P, c0:c0 + cn].rearrange("(k p) c -> p k c", p=P)

        if kind == "in":
            c0, width = GROUPS[name]
            kn = KD // (1 if width == 256 else 2)
            return [view(w_in, i * kn + j * kn // 2, kn // 2, c0, width) for j in range(2)]
        if kind == "ffn":
            return [view(w_ffn_in, 0, KD, j * FF + i * P, P) for j in range(2)]
        w = {"out": w_out, "fo": w_ffn_out, "gate": w_gate, "ple": w_ple}[kind]
        return [view(w, 2 * i + j, 1, 0, D) for j in range(2)]

    def piece_size(g):
        kind, name, _ = STRIPS[g % NS]
        return GROUPS[name][1] * (4 if GROUPS[name][1] == 256 else 2) if kind == "in" else PIECE

    def swa_bank(c, g):
        return banks[4 + 2 * (c % 2) + g]

    def ret_y_bank(c):
        return banks[7] if c < TILES - 1 else banks[5]

    with nc.Block() as block:

        @block.sync
        def _(sp):
            def load_x(m):
                sp.dma_start(x[:, m, :], x_in[m * P:(m + 1) * P, :]).then_inc(x_loaded[m], 16)

            load_x(0)
            sp.dma_start(tab[:], table).then_inc(table_loaded, 16)
            sp.dma_start(prew[:, 0], pre_mix).then_inc(table_loaded, 16)
            load_x(1)
            for g in range(depth * NS):
                layer, s = divmod(g, NS)
                if s == 3:
                    if layer:
                        sp.wait_ge(mm_done, used_count((layer - 1) * NS + SIDX[("gate", None, 0)]))
                        sp.wait_ge(x_new, x_count(layer - 1, "ffn", 3))
                    sp.dma_start(wsT[:], ws_t[layer]).then_inc(ws_loaded, 16)
                    sp.dma_start(bs, bs_t[layer]).then_inc(params_loaded, 16)
                    sp.dma_start(snk, sinks[layer:layer + 1, :].partition_broadcast(P)).then_inc(params_loaded, 16)
                    sp.dma_start(gnw[:], gn_w[layer:layer + 1, :].partition_broadcast(P)).then_inc(params_loaded, 16)
                    sp.dma_start(lnw[:], ln_w[layer:layer + 1, :].partition_broadcast(P)).then_inc(params_loaded, 16)
                    sp.dma_start(lnb[:], ln_b[layer:layer + 1, :].partition_broadcast(P)).then_inc(params_loaded, 16)
                if s == SIDX[("ffn", None, 0)]:
                    sp.wait_ge(ret_o, (layer + 1) * TILES)
                    sp.dma_start(post_w[:], post_mix[layer:layer + 1, :].partition_broadcast(P)).then_inc(post_w_loaded, 16)
                if s == SIDX[("ffn", None, 6)]:
                    sp.wait_ge(x_new, x_count(layer, "mix", 3))
                    sp.dma_start(post_w[:], post_ffn[layer:layer + 1, :].partition_broadcast(P)).then_inc(post_w_loaded, 16)
                if s == SIDX[("ple", None, 0)]:
                    sp.wait_ge(mm_done, used_count(layer * NS + SIDX[("fo", None, 5)]))
                    sp.dma_start(ple_w[:], ple_norm[layer:layer + 1, :].partition_broadcast(P)).then_inc(ple_w_loaded, 16)
                    sp.dma_start(p_raw[:], p_t[layer].rearrange("(k p) t -> p k t", p=P)).then_inc(p_loaded, 16)
                n = piece_size(g)
                for j, view in enumerate(pieces(g)):
                    q = 2 * g + j
                    if q >= RAWS:
                        sp.wait_ge(lo_ready, q - RAWS + 1)
                    dst = raw[q % RAWS][:, 0:n].rearrange("p (k c) -> p k c", k=view.shape[1])
                    sp.dma_start(dst, view).then_inc(raw_loaded[q % RAWS], 16)
                if g == 0:
                    load_x(2)
                    load_x(3)
                    sp.dma_start(later_m[:], later).then_inc(consts_loaded, 16)
                    sp.dma_start(prew[:, 1], pre_ffn).then_inc(consts_loaded, 16)
            for m in range(TILES):
                sp.wait_ge(x_new, x_count(depth - 1, "gate", m))
                sp.dma_start(out[m * P:(m + 1) * P, :], x[:, m, :]).then_inc(stored, 16)
            sp.wait_ge(stored, 16 * TILES)

        @block.tensor
        def _(pe):
            def mm3(out_ap, a_hi, a_lo, b_hi, b_lo, start, stop):
                pe.matmul(out_ap, a_hi, b_hi, start=start, stop=False, skip_group_check=True)
                pe.matmul(out_ap, a_hi, b_lo, start=False, stop=False, skip_group_check=True)
                return pe.matmul(out_ap, a_lo, b_hi, start=False, stop=stop, skip_group_check=True)

            def ts(m):
                return slice(m * P, (m + 1) * P)

            def mm_in(layer, g, strip, m):
                _, name, i = strip
                width = GROUPS[name][1]
                n = 1 if width == 256 else 2
                kn = KD // n
                if i == 0:
                    gi = GNAMES.index(name)
                    if gi:
                        pe.wait_ge(*evac(layer, GNAMES[gi - 1], m))
                    else:
                        pe.wait_ge(h_lo_ready, t_count(layer, "mix", m))
                hi = w_hi[g % SLOTS][:, 0:kn * width].rearrange("p (k c) -> p k c", k=kn)
                lo = w_lo[g % SLOTS][:, 0:kn * width].rearrange("p (k c) -> p k c", k=kn)
                for k in range(kn):
                    kk = i * kn + k
                    last = mm3(banks[m][:, 0:width], h_hi[:, kk, ts(m)], h_lo[:, kk, ts(m)],
                               hi[:, k, :], lo[:, k, :], kk == 0, kk == KD - 1)
                return last

            def mm_rows(a_hi, a_lo, k0, g, m, first, final):
                for k in range(2):
                    for half in range(2):
                        c = slice(k * D + half * 512, k * D + half * 512 + 512)
                        last = mm3(banks[2 * m + half][:, :], a_hi[:, k0 + k, ts(m)], a_lo[:, k0 + k, ts(m)],
                                   w_hi[g % SLOTS][:, c], w_lo[g % SLOTS][:, c],
                                   first and k == 0, final and k == 1)
                return last

            def mm_ffn(layer, g, strip, m):
                j = strip[2]
                cols = slice(0, S) if m is None else slice(m * S // 2, (m + 1) * S // 2)
                for part in range(2):
                    for k in range(KD):
                        c = slice(part * PIECE + k * P, part * PIECE + (k + 1) * P)
                        last = mm3(banks[2 * (j % 4) + part][:, cols], w_hi[g % SLOTS][:, c],
                                   w_lo[g % SLOTS][:, c], h_hi[:, k, cols], h_lo[:, k, cols],
                                   k == 0, k == KD - 1)
                return last

            def block_of(layer, strip, m):
                g = layer * NS + SIDX[strip]
                kind, _, i = strip
                pe.wait_ge(lo_ready, 2 * (g + 1))
                if kind == "in":
                    last = mm_in(layer, g, strip, m)
                elif kind == "out":
                    if i == 3:
                        if m < 2:
                            pe.wait_ge(*evac(layer, "a", 2 * m + 1))
                        if m == 2:
                            pe.wait_ge(y_lo_ready, y_count(layer, ("ret_yT", 3)))
                    need = {2: ("ret_yT", m), 3: ("swa_yT", m), 1: ("ret_yT", m), 0: ("gmlp_yT",)}[i]
                    if m == 3:
                        need = ("gmlp_yT",)
                    pe.wait_ge(y_lo_ready, y_count(layer, need))
                    last = mm_rows(y_hi, y_lo, 2 * i, g, m, i == 3, i == 0)
                elif kind == "ffn":
                    if m is not None:
                        pe.wait_ge(h_lo_ready, t_count(layer, "ffn", max(2 * m + 1, i)))
                    else:
                        if i >= 4:
                            pe.wait_ge(mid_lo_ready, layer * FCH + i - 3)
                        else:
                            pe.wait_ge(h_lo_ready, t_count(layer, "ffn", 3))
                    last = mm_ffn(layer, g, strip, m)
                elif kind == "fo":
                    if i == 0:
                        last_in_pair = max(j for j in range(FCH) if j % 4 == m)
                        pe.wait_ge(mid_lo_ready, layer * FCH + last_in_pair + 1)
                    pe.wait_ge(mid_lo_ready, layer * FCH + 2 * i + 2)
                    last = mm_rows(mid_hi, mid_lo, 2 * i, g, m, i == 0, i == FCH // 2 - 1)
                elif kind == "ple":
                    pe.wait_ge(h_lo_ready, t_count(layer, "gate", m))
                    pe.wait_ge(p_lo_ready, layer + 1)
                    last = mm_rows(p_hi, p_lo, 0, g, m, True, True)
                else:
                    if i == 0:
                        pe.wait_ge(ple_ready, layer * TILES + m + 1)
                    last = mm_rows(h_hi, h_lo, 2 * i, g, m, i == 0, i == 3)
                last.then_inc(mm_done, 1)

            def transposes(layer, stage, m):
                if stage == "gate":
                    pe.wait_ge(x_new, x_count(layer, "ffn", m))
                    src = x[:, m, :]
                else:
                    n = pre_count(layer, stage, m)
                    pe.wait_ge(xn_ready, n)
                    src = xn[(n - 1) % 2][:, :]
                for half in range(2):
                    for k in range(4):
                        kk = 4 * half + k
                        last = pe.transpose(banks[2 * m + half][:, k * P:(k + 1) * P],
                                            src[:, kk * P:(kk + 1) * P], T_("ident"))
                    last.then_inc(x_T, 1)

            def rows(g):
                return slice(HD * g, HD * (g + 1))

            pe.wait_ge(table_loaded, 32)
            transposes(0, "mix", 0)
            transposes(0, "mix", 1)
            for layer in range(depth):
                for e in SCHEDULE:
                    kind = e[0]
                    if kind == "mm":
                        block_of(layer, e[1], e[2])
                    elif kind == "T":
                        if of_stage(layer, e[1]):
                            transposes(*of_stage(layer, e[1]), e[2])
                    elif kind == "swa_T":
                        c = e[1]
                        pe.wait_ge(ck_roped, layer * TILES + c + 1)
                        pe.wait_ge(cq_roped, layer * TILES + c + 1)
                        if c:
                            pe.wait_ge(swa_cT, layer * TILES + c)
                        for j in range(3):
                            pe.transpose(banks[4][:, j * P:(j + 1) * P], cq[c % 2][:, j * P:(j + 1) * P],
                                         T_("ident"))
                        pe.transpose(banks[4][:, 3 * P:4 * P], ck[:, c, :],
                                     T_("ident")).then_inc(swa_T, 1)
                    elif kind in ("swa_cur", "swa_prev"):
                        c = e[1]
                        k0 = c if kind == "swa_cur" else c - 1
                        if k0 < 0:
                            continue
                        if kind == "swa_cur":
                            pe.wait_ge(swa_cT, layer * TILES + TILES)
                            if c >= 2:
                                pe.wait_ge(y_lo_ready, y_count(layer, ("swa_yT", c - 2)))
                        else:
                            pe.wait_ge(swa_S, layer * TILES + c + 1)
                        for g in range(2):
                            for j in range(3):
                                last = pe.matmul(swa_bank(c, g)[:, j * P:(j + 1) * P],
                                                 cT[rows(g), j, ts(c)], cT[rows(g), 3, ts(k0)],
                                                 start=True, stop=True, skip_group_check=True)
                        last.then_inc(swa_cur if kind == "swa_cur" else swa_prev, 1)
                    elif kind == "swa_PT":
                        c = e[1]
                        pe.wait_ge(swa_exp, layer * TILES + c + 1)
                        for hh in range(C_HEADS):
                            last = pe.transpose(swa_bank(c, hh // 3)[:, (hh % 3) * P:(hh % 3 + 1) * P],
                                                prob[c % 2][:, hh, :], T_("ident"))
                        last.then_inc(swa_PT, 1)
                    elif kind == "swa_o":
                        c = e[1]
                        pe.wait_ge(swa_PTm, layer * TILES + c + 1)
                        for hh in range(C_HEADS):
                            o = swa_bank(c, 0)[:, hh * HD:(hh + 1) * HD]
                            g = hh // 3
                            last = pe.matmul(o, ptl[c % 2][:, hh, :], cv[:, c, rows(g)], start=True, stop=(c == 0),
                                             skip_group_check=True)
                            if c:
                                last = pe.matmul(o, ptu[c % 2][:, hh, :], cv[:, c - 1, rows(g)], start=False,
                                                 stop=True, skip_group_check=True)
                        last.then_inc(swa_o, 1)
                    elif kind == "swa_yT":
                        c = e[1]
                        pe.wait_ge(swa_yr, layer * TILES + c + 1)
                        flat = swa_y[c % 2][:, :, :].rearrange("p h d -> p (h d)")
                        for k in range(3):
                            last = pe.transpose(swa_bank(c, 1)[:, k * P:(k + 1) * P], flat[:, k * P:(k + 1) * P],
                                                T_("ident"))
                        last.then_inc(y_T, 1)
                    elif kind == "ret_T":
                        c = e[1]
                        pe.wait_ge(b_roped, layer * 2 * TILES + TILES + c + 1)
                        if c:
                            pe.wait_ge(ret_oread, layer * TILES + c)
                            pe.wait_ge(ret_state, layer * 3 + c)
                        else:
                            pe.wait_ge(y_lo_ready, y_count(layer, ("swa_yT", 2)))
                        for i, src in enumerate((bk, bq)):
                            for j in range(3):
                                last = pe.transpose(banks[4 + i][:, j * P:(j + 1) * P],
                                                    src[:, c, j * P:(j + 1) * P], T_("ident"))
                        last.then_inc(ret_T, 1)
                    elif kind == "ret_sc":
                        c = e[1]
                        pe.wait_ge(ret_kqT, layer * TILES + c + 1)
                        for g in range(2):
                            for j in range(3):
                                last = pe.matmul(banks[4 + g][:, j * P:(j + 1) * P], kqT[rows(g), 0, j, :],
                                                 kqT[rows(g), 1, j, :], start=True, stop=True,
                                                 skip_group_check=True)
                        last.then_inc(ret_sc, 1)
                    elif kind == "ret_o":
                        c = e[1]
                        pe.wait_ge(ret_scm, layer * TILES + c + 1)
                        if c == 0:
                            pe.wait_ge(evac_act, evac(layer, "bv", 3)[1])
                        else:
                            pe.wait_ge(ret_state, layer * 3 + c)
                        for j in range(3):
                            if c:
                                pe.matmul(banks[4][:, j * P:(j + 1) * P], kqT[:, 1, j, :], state[:, j, :],
                                          start=True, stop=False, skip_group_check=True)
                            for g in range(2):
                                cols = slice(j * P + g * HD, j * P + (g + 1) * HD)
                                last = pe.matmul(banks[4][:, cols], scm[:, g, j, :], bv[:, c, cols],
                                                 start=(c == 0), stop=True, skip_group_check=True)
                        last.then_inc(ret_o, 1)
                        if c < TILES - 1:
                            for j in range(3):
                                last = pe.matmul(banks[5][:, j * P:(j + 1) * P], bk[:, c, j * P:(j + 1) * P],
                                                 bv[:, c, j * P:(j + 1) * P], start=True, stop=True,
                                                 skip_group_check=True)
                            last.then_inc(ret_kv, 1)
                    elif kind == "ret_yT":
                        c = e[1]
                        pe.wait_ge(ret_yr, layer * TILES + c + 1)
                        if c == 0:
                            pe.wait_ge(y_lo_ready, y_count(layer, ("swa_yT", 3)))
                        elif c < TILES - 1:
                            pe.wait_ge(y_lo_ready, y_count(layer, ("ret_yT", c - 1)))
                        for k in range(3):
                            last = pe.transpose(ret_y_bank(c)[:, k * P:(k + 1) * P], ret_y[:, k * P:(k + 1) * P],
                                                T_("ident"))
                        last.then_inc(y_T, 1)
                    elif kind == "gmlp_mix":
                        pe.wait_ge(gm_vn, layer * TILES + TILES)
                        pe.wait_ge(ws_ready, layer + 1)
                        pe.wait_ge(y_lo_ready, y_count(layer, ("ret_yT", 2)))
                        for c in range(TILES):
                            for hh in range(A_HEADS):
                                col = (c % 2) * AW + hh * HD
                                last = pe.matmul(banks[6 + c // 2][:, col:col + HD], wsT[:, hh, :],
                                                 vn[:, c, hh * HD:(hh + 1) * HD], start=True, stop=True,
                                                 skip_group_check=True)
                        last.then_inc(gm_mix, 1)
                    elif kind == "gmlp_yT":
                        pe.wait_ge(gm_ya, layer + 1)
                        for k in range(2):
                            for c in range(TILES):
                                last = pe.transpose(banks[6 + k][:, c * P:(c + 1) * P],
                                                    uv[:, c, k * P:(k + 1) * P], T_("ident"))
                            last.then_inc(y_T, 1)

        @block.scalar
        def _(act):
            def y_split(layer, e, bank, dst):
                n = y_count(layer, e)
                act.wait_ge(y_T, n)
                act.activation(dst, bank, ACT.Copy).then_inc(y_hi_ready, 1)

            def conv(g):
                if g >= depth * NS:
                    return
                n = piece_size(g)
                if g >= SLOTS:
                    act.wait_ge(mm_done, used_count(g - SLOTS))
                for j in range(2):
                    q = 2 * g + j
                    act.wait_ge(raw_loaded[q % RAWS], 16 * (q // RAWS + 1))
                    act.activation(w_hi[g % SLOTS][:, j * n:(j + 1) * n], raw[q % RAWS][:, 0:n],
                                   ACT.Copy).then_inc(hi_ready, 1)

            squares = [0, 0]

            def after_squares():
                if squares[0]:
                    act.wait_ge(pre_sq, squares[0])
                if squares[1]:
                    act.wait_ge(post_sq, squares[1])

            def pre(layer, stage, m):
                n = pre_count(layer, stage, m)
                if layer == 0 and stage == "mix":
                    act.wait_ge(x_loaded[m], 16)
                elif stage == "mix":
                    act.wait_ge(x_new, x_count(layer - 1, "gate", m))
                else:
                    act.wait_ge(x_new, x_count(layer, "mix", m))
                if n > 2:
                    act.wait_ge(pre_r, n - 2)
                after_squares()
                squares[0] += 1
                act.activation(junk[:], x[:, m, :], ACT.Square, scale=D ** -0.5,
                               accum_out=ss_pre[n % 2]).then_inc(pre_sq, 1)

            def split_T(layer, stage, m):
                for half in range(2):
                    dst = h_hi[:, 4 * half:4 * half + 4, m * P:(m + 1) * P]
                    if stage == "gate":
                        act.wait_ge(x_T, t_count(layer, stage, m, half))
                        src = banks[2 * m + half][:, :].rearrange("p (k t) -> p k t", k=4)
                    else:
                        act.wait_ge(hT_ready, hT_count(layer, stage, m, half))
                        src = hT[half][:]
                    act.activation(dst, src, ACT.Copy).then_inc(h_hi_ready, 1)

            pre(0, "mix", 0)
            pre(0, "mix", 1)
            conv(0)
            split_T(0, "mix", 0)
            pre(0, "mix", 2)
            split_T(0, "mix", 1)
            pre(0, "mix", 3)
            conv(1)
            conv(2)
            for layer in range(depth):
                for e in SCHEDULE:
                    kind = e[0]
                    if kind == "conv":
                        conv(layer * NS + e[1])
                    elif kind == "T":
                        if of_stage(layer, e[1]):
                            split_T(*of_stage(layer, e[1]), e[2])
                    elif kind == "post":
                        _, stage, m = e
                        n = post_count(layer, stage, m)
                        strip = {"mix": ("out", None, 0), "ffn": ("fo", None, FCH // 2 - 1),
                                 "ple": ("ple", None, 0)}[stage]
                        act.wait_ge(mm_done, mm_count(layer, strip, m))
                        if n > 2:
                            act.wait_ge(post_r, n - 2)
                        after_squares()
                        squares[1] += 2
                        act.activation(junk[:, 0:512], banks[2 * m][:, :], ACT.Square, scale=D ** -0.5,
                                       accum_out=ss_post[n % 2][:, 0:1]).then_inc(post_sq, 1)
                        act.activation(junk[:, 512:D], banks[2 * m + 1][:, :], ACT.Square, scale=D ** -0.5,
                                       accum_out=ss_post[n % 2][:, 1:2]).then_inc(post_sq, 1)
                        if stage == "ffn" and m == 0:
                            act.wait_ge(p_loaded, 16 * (layer + 1))
                            act.activation(p_hi[:], p_raw[:], ACT.Copy).then_inc(p_hi_ready, 1)
                    elif kind == "pre":
                        _, stage, m = e
                        if stage == "ffn":
                            pre(layer, "ffn", m)
                        elif layer + 1 < depth:
                            pre(layer + 1, "mix", m)
                    elif kind == "gated":
                        m = e[1]
                        act.wait_ge(mm_done, mm_count(layer, ("gate", None, 3), m))
                        if m or layer:
                            act.wait_ge(x_new, x_count(layer, "gate", m) - 1)
                        act.activation(sig[:, 0:512], banks[2 * m][:, :], ACT.Sigmoid)
                        act.activation(sig[:, 512:D], banks[2 * m + 1][:, :], ACT.Sigmoid).then_inc(sig_ready, 1)
                    elif kind == "mid":
                        j = e[1]
                        act.wait_ge(mm_done, mm_count(layer, ("ffn", None, j), 1 if j < 3 else None))
                        if j or layer:
                            act.wait_ge(prod_ready, layer * FCH + j)
                        if j == 0:
                            act.wait_ge(gm_vn, (layer + 1) * TILES)
                        act.activation(silu_g[:], banks[2 * (j % 4)][:, :], ACT.Silu).then_inc(silu_ready, 1)
                        act.wait_ge(prod_ready, layer * FCH + j + 1)
                        act.activation(mid_hi[:, j, :], banks[2 * (j % 4) + 1][:, :],
                                       ACT.Copy).then_inc(mid_hi_ready, 1)
                    elif kind == "swa_T":
                        c = e[1]
                        act.wait_ge(swa_T, layer * TILES + c + 1)
                        act.activation(cT[:, :, c * P:(c + 1) * P],
                                       banks[4][:, :].rearrange("p (k t) -> p k t", k=4),
                                       ACT.Copy).then_inc(swa_cT, 1)
                    elif kind == "swa_cur":
                        c = e[1]
                        act.wait_ge(swa_cur, layer * TILES + c + 1)
                        if c >= 2:
                            act.wait_ge(y_T, y_count(layer, ("swa_yT", c - 2)))
                        for g in range(2):
                            last = act.activation(prob[c % 2][:, 3 * g:3 * g + 3, :],
                                                  swa_bank(c, g)[:, 0:BW].rearrange("p (h t) -> p h t", h=3),
                                                  ACT.Copy)
                        last.then_inc(swa_S, 1)
                    elif kind == "swa_prev":
                        c = e[1]
                        act.wait_ge(swa_m, layer * TILES + c + 1)
                        for hh in range(C_HEADS):
                            act.activation(prob[c % 2][:, hh, :], prob[c % 2][:, hh, :], ACT.Exp,
                                           bias=negm[c % 2][:, hh:hh + 1],
                                           accum_out=lsum[c % 2][:, hh:hh + 1])
                        act.activation(esink[c % 2], dsink[c % 2], ACT.Exp).then_inc(swa_exp, 1)
                    elif kind == "swa_yT":
                        c = e[1]
                        y_split(layer, e, swa_bank(c, 1)[:, 0:BW].rearrange("p (k t) -> p k t", k=3),
                                y_hi[:, 5:8, c * P:(c + 1) * P])
                    elif kind == "ret_T":
                        c = e[1]
                        act.wait_ge(ret_T, layer * TILES + c + 1)
                        for i in range(2):
                            last = act.activation(kqT[:, i, :, :],
                                                  banks[4 + i][:, 0:BW].rearrange("p (k t) -> p k t", k=3),
                                                  ACT.Copy)
                        last.then_inc(ret_kqT, 1)
                    elif kind == "ret_yT":
                        c = e[1]
                        y_split(layer, e, ret_y_bank(c)[:, 0:BW].rearrange("p (k t) -> p k t", k=3),
                                y_hi[:, 2:5, c * P:(c + 1) * P])
                    elif kind == "gmlp_yT":
                        n = y_count(layer, e)
                        for k in range(2):
                            act.wait_ge(y_T, n - 1 + k)
                            act.activation(y_hi[:, k, :], banks[6 + k][:, :], ACT.Copy).then_inc(y_hi_ready, 1)
                    elif kind == "mm" and e[1][0] == "in":
                        _, strip, m = e
                        name = strip[1]
                        if strip != group_final(name) or name not in ACT_EVAC:
                            continue
                        act.wait_ge(mm_done, mm_count(layer, strip, m))
                        if name == "ckv":
                            act.activation(ck[:, m, :], banks[m][:, 0:P], ACT.Copy)
                            act.activation(cv[:, m, :], banks[m][:, P:2 * P], ACT.Copy).then_inc(evac_act, 1)
                        elif name == "cq":
                            if m >= 2:
                                act.wait_ge(swa_T, layer * TILES + m - 1)
                            act.activation(cq[m % 2][:].rearrange("p (j g d) -> p g j d", j=3, g=2),
                                           banks[m][:, 0:BW].rearrange("p (g j d) -> p g j d", j=3, g=2),
                                           ACT.Copy, scale=HD ** -0.5).then_inc(evac_act, 1)
                        elif name == "bv":
                            act.activation(bv[:, m, :], banks[m][:, 0:BW], ACT.Copy).then_inc(evac_act, 1)
                        elif name == "bg":
                            act.activation(bg[:, m, :], banks[m][:, 0:BW], ACT.Silu).then_inc(evac_act, 1)
                        else:
                            if m == 0:
                                act.wait_ge(swa_prev, (layer + 1) * 3)
                            act.activation(uv[:, m, :], banks[m][:, :], ACT.Gelu_apprx_tanh).then_inc(evac_act, 1)

        @block.gpsimd
        def _(pool):
            steps = [0]

            def step(ins):
                steps[0] += 1
                ins.then_inc(pool_step, 1)
                pool.wait_ge(pool_step, steps[0])

            pool.memset(half_neg, -0.5).then_inc(pool_init, 1)
            pool.memset(neg_big, NEG).then_inc(pool_init, 1)
            pool.wait_ge(pool_init, 2)
            def pre(layer, stage, m):
                n = pre_count(layer, stage, m)
                pool.wait_ge(pre_sq, n)
                if n > 2:
                    pool.wait_ge(xn_ready, n - 2)
                if n > 1:
                    pool.wait_ge(pre_r, n - 1)
                step(pool.tensor_scalar(t_pre, ss_pre[n % 2], EPS, None, ALU.add))
                pool.tensor_tensor(r_pre[n % 2], t_pre, half_neg[:, 0:1], ALU.pow).then_inc(pre_r, 1)

            for m in range(TILES):
                pre(0, "mix", m)
            for layer in range(depth):
                for e in SCHEDULE:
                    kind = e[0]
                    if kind == "post":
                        n = post_count(layer, e[1], e[2])
                        pool.wait_ge(post_sq, 2 * n)
                        if n > 2:
                            pool.wait_ge(*post_used(n - 2))
                        if n > 1:
                            pool.wait_ge(post_r, n - 1)
                        step(pool.tensor_scalar(t_post, ss_post[n % 2][:, 0:1], ss_post[n % 2][:, 1:2], EPS,
                                                ALU.add, ALU.add))
                        pool.tensor_tensor(r_post[n % 2], t_post, half_neg[:, 0:1], ALU.pow).then_inc(post_r, 1)
                    elif kind == "pre":
                        if e[1] == "ffn":
                            pre(layer, "ffn", e[2])
                        elif layer + 1 < depth:
                            pre(layer + 1, "mix", e[2])
                    elif kind == "swa_cur" and e[1] == 0:
                        pool.wait_ge(ws_loaded, 16 * (layer + 1))
                        pool.affine_select(out=wsT[:], in_=wsT[:], compare_op=ALU.is_ge, fill=0.0, base=0,
                                           pattern=[[0, A_HEADS], [1, P]],
                                           channel_multiplier=-1).then_inc(ws_ready, 1)
                    elif kind == "ret_o":
                        n = layer * TILES + e[1] + 1
                        pool.wait_ge(ret_v, n)
                        if n > 1:
                            pool.wait_ge(ret_r, n - 1)
                        step(pool.tensor_scalar(rvt, rvar, 1.0 / HD, EPS, ALU.mult, ALU.add))
                        pool.tensor_tensor(rr, rvt, half_neg, ALU.pow).then_inc(ret_r, 1)
                    elif kind == "mm" and e[1] == group_final("a"):
                        n = layer * TILES + e[2] + 1
                        pool.wait_ge(gm_v, n)
                        if n > 1:
                            pool.wait_ge(gm_r, n - 1)
                        step(pool.tensor_scalar(gvt, gvar, 1.0 / HD, EPS, ALU.mult, ALU.add))
                        pool.tensor_tensor(gr, gvt, half_neg[:, 0:A_HEADS], ALU.pow).then_inc(gm_r, 1)

        @block.vector
        def _(dve):
            counts = {}

            def done(ins, signal):
                counts[signal.name] = counts.get(signal.name, 0) + 1
                ins.then_inc(signal, 1)
                dve.wait_ge(signal, counts[signal.name])

            def step(ins):
                done(ins, dve_step)

            def heads(ap, n):
                return ap.rearrange("p (h d) -> p h d", h=n)

            def conv(g):
                if g >= depth * NS:
                    return
                n = piece_size(g)
                for j in range(2):
                    q = 2 * g + j
                    dve.wait_ge(hi_ready, q + 1)
                    done(dve.tensor_tensor(w_lo[g % SLOTS][:, j * n:(j + 1) * n], raw[q % RAWS][:, 0:n],
                                      w_hi[g % SLOTS][:, j * n:(j + 1) * n].bitcast(F32),
                                      ALU.subtract), lo_ready)

            def pre(layer, stage, m):
                n = pre_count(layer, stage, m)
                dve.wait_ge(pre_r, n)
                if n > 2:
                    q = n - 3
                    lay, r = divmod(q, 2 * TILES)
                    dve.wait_ge(x_T, t_count(lay, "ffn" if r >= TILES else "mix", r % TILES))
                done(dve.tensor_scalar(xn[(n - 1) % 2][:], x[:, m, :], r_pre[n % 2], None,
                                  ALU.mult), xn_ready)

            def rope_full(layer, which, m):
                dst = (bk, bq)[which]
                src = banks[m][:, 0:BW]
                sc = (T_("ks"), T_("qs"))[which]
                done(dve.tensor_tensor(heads(rope_x[:], 6), heads(src, 6), sc[:, :, None].to_broadcast([P, 6, HD]),
                                  ALU.mult), evac_dve)
                dve.wait_ge(evac_dve, evac(layer, DVE_EVAC[which], m)[1])
                xr = rope_x[:].rearrange("p (h s d) -> p h s d", h=6, s=2)
                ar = rope_a[:].rearrange("p (h s d) -> p h s d", h=6, s=2)
                br = rope_b[:].rearrange("p (h s d) -> p h s d", h=6, s=2)
                cos = T_("rcos")[:, m * 32:(m + 1) * 32][:, None, None, :].to_broadcast([P, 6, 2, 32])
                sin = T_("rsin")[:, m * 32:(m + 1) * 32][:, None, None, :].to_broadcast([P, 6, 2, 32])
                done(dve.tensor_tensor(ar, xr, cos, ALU.mult), dve_step)
                step(dve.tensor_tensor(br, xr, sin, ALU.mult))
                o = dst[:, m, :].rearrange("p (h s d) -> p h s d", h=6, s=2)
                done(dve.tensor_tensor(o[:, :, 0, :], ar[:, :, 0, :], br[:, :, 1, :], ALU.subtract), dve_step)
                done(dve.tensor_tensor(o[:, :, 1, :], ar[:, :, 1, :], br[:, :, 0, :], ALU.add), b_roped)

            def rope_part(buf, n, m, signal):
                xr = heads(buf, n)[:, :, 0:16].rearrange("p h (s d) -> p h s d", s=2)
                ar = rope_a[:, 0:16 * n].rearrange("p (h s d) -> p h s d", h=n, s=2)
                br = rope_b[:, 0:16 * n].rearrange("p (h s d) -> p h s d", h=n, s=2)
                cos = T_("scos")[:, m * 8:(m + 1) * 8][:, None, None, :].to_broadcast([P, n, 2, 8])
                sin = T_("ssin")[:, m * 8:(m + 1) * 8][:, None, None, :].to_broadcast([P, n, 2, 8])
                done(dve.tensor_tensor(ar, xr, cos, ALU.mult), dve_step)
                step(dve.tensor_tensor(br, xr, sin, ALU.mult))
                done(dve.tensor_tensor(xr[:, :, 0, :], ar[:, :, 0, :], br[:, :, 1, :], ALU.subtract), dve_step)
                done(dve.tensor_tensor(xr[:, :, 1, :], ar[:, :, 1, :], br[:, :, 0, :], ALU.add), signal)

            def y_split(layer, e, bank, hi, lo):
                dve.wait_ge(y_hi_ready, y_count(layer, e))
                done(dve.tensor_tensor(lo, bank, hi.bitcast(F32), ALU.subtract), y_lo_ready)

            def mask3(ap):
                return ap[:, None, :].to_broadcast([P, 3, P])

            dve.wait_ge(pool_init, 2)
            def split_T(layer, stage, m):
                for half in range(2):
                    bank = banks[2 * m + half][:, :].rearrange("p (k t) -> p k t", k=4)
                    if stage != "gate":
                        dve.wait_ge(x_T, t_count(layer, stage, m, half))
                        w = prew[:, 0 if stage == "mix" else 1, layer, 4 * half:4 * half + 4]
                        done(dve.tensor_tensor(hT[half][:], bank, w[:, :, None].to_broadcast([P, 4, P]),
                                               ALU.mult), hT_ready)
                for half in range(2):
                    bank = banks[2 * m + half][:, :].rearrange("p (k t) -> p k t", k=4)
                    hi = h_hi[:, 4 * half:4 * half + 4, m * P:(m + 1) * P]
                    lo = h_lo[:, 4 * half:4 * half + 4, m * P:(m + 1) * P]
                    src = bank if stage == "gate" else hT[half][:]
                    dve.wait_ge(h_hi_ready, t_count(layer, stage, m, half))
                    done(dve.tensor_tensor(lo, src, hi.bitcast(F32), ALU.subtract), h_lo_ready)

            pre(0, "mix", 0)
            pre(0, "mix", 1)
            conv(0)
            dve.wait_ge(table_loaded, 32)
            split_T(0, "mix", 0)
            pre(0, "mix", 2)
            split_T(0, "mix", 1)
            pre(0, "mix", 3)
            conv(1)
            conv(2)
            dve.wait_ge(consts_loaded, 32)
            for layer in range(depth):
                for e in SCHEDULE:
                    kind = e[0]
                    if kind == "conv":
                        conv(layer * NS + e[1])
                    elif kind == "T":
                        if of_stage(layer, e[1]):
                            split_T(*of_stage(layer, e[1]), e[2])
                    elif kind == "post":
                        _, stage, m = e
                        n = post_count(layer, stage, m)
                        if stage == "ple":
                            dve.wait_ge(ple_w_loaded, 16 * (layer + 1))
                        else:
                            dve.wait_ge(post_w_loaded, 16 * (2 * layer + (1 if stage == "mix" else 2)))
                        dve.wait_ge(post_r, n)
                        wrow = ple_w if stage == "ple" else post_w
                        for half in range(2):
                            c = slice(half * 512, half * 512 + 512)
                            dst = ple_n[:, m, c] if stage == "ple" else upd[:, c]
                            last = dve.scalar_tensor_tensor(out=dst, in0=banks[2 * m + half][:, :],
                                                            scalar=r_post[n % 2], in1=wrow[:, c],
                                                            op0=ALU.mult, op1=ALU.mult)
                        if stage == "ple":
                            done(last, ple_ready)
                        else:
                            step(last)
                            done(dve.tensor_tensor(x[:, m, :], x[:, m, :], upd[:], ALU.add), x_new)
                        if stage == "ffn" and m == 0:
                            dve.wait_ge(p_hi_ready, layer + 1)
                            done(dve.tensor_tensor(p_lo[:], p_raw[:], p_hi[:].bitcast(F32),
                                              ALU.subtract), p_lo_ready)
                    elif kind == "pre":
                        if e[1] == "ffn":
                            pre(layer, "ffn", e[2])
                        elif layer + 1 < depth:
                            pre(layer + 1, "mix", e[2])
                    elif kind == "gated":
                        m = e[1]
                        dve.wait_ge(sig_ready, layer * TILES + m + 1)
                        dve.wait_ge(ple_ready, layer * TILES + m + 1)
                        step(dve.tensor_tensor(sig[:], sig[:], ple_n[:, m, :], ALU.mult))
                        done(dve.tensor_tensor(x[:, m, :], x[:, m, :], sig[:], ALU.add), x_new)
                    elif kind == "mid":
                        j = e[1]
                        b = 2 * (j % 4) + 1
                        dve.wait_ge(silu_ready, layer * FCH + j + 1)
                        done(dve.tensor_tensor(banks[b][:, :], silu_g[:], banks[b][:, :], ALU.mult), prod_ready)
                        dve.wait_ge(mid_hi_ready, layer * FCH + j + 1)
                        done(dve.tensor_tensor(mid_lo[:, j, :], banks[b][:, :], mid_hi[:, j, :].bitcast(F32),
                                          ALU.subtract), mid_lo_ready)
                    elif kind == "swa_prev":
                        c = e[1]
                        dve.wait_ge(swa_S, layer * TILES + c + 1)
                        if c == 0:
                            dve.wait_ge(params_loaded, 16 * 5 * (layer + 1))
                        else:
                            dve.wait_ge(swa_prev, layer * 3 + c)
                        o = c % 2
                        for g in range(2):
                            old = (swa_bank(c, g)[:, 0:BW].rearrange("p (h t) -> p h t", h=3) if c
                                   else neg_big[:, :, None].to_broadcast([P, 3, P]))
                            last = dve.copy_predicated(prob[o][:, 3 * g:3 * g + 3, :], mask3(later_m[:]), old)
                        step(last)
                        step(dve.tensor_reduce(mx[o], prob[o][:], AX.X, ALU.max))
                        step(dve.tensor_tensor(mx[o], mx[o], snk, ALU.max))
                        done(dve.tensor_scalar(negm[o], mx[o], -1.0, None, ALU.mult), dve_step)
                        done(dve.tensor_tensor(dsink[o], snk, mx[o], ALU.subtract), swa_m)
                    elif kind == "swa_PT":
                        c = e[1]
                        dve.wait_ge(swa_PT, layer * TILES + c + 1)
                        for g in range(2):
                            b3 = swa_bank(c, g)[:, 0:BW].rearrange("p (h t) -> p h t", h=3)
                            h3 = slice(3 * g, 3 * g + 3)
                            last = dve.tensor_tensor(ptl[c % 2][:, h3, :], b3, mask3(T_("lowT")), ALU.mult)
                            if c:
                                last = dve.tensor_tensor(ptu[c % 2][:, h3, :], b3, mask3(T_("upT")), ALU.mult)
                        done(last, swa_PTm)
                    elif kind == "swa_o":
                        c = e[1]
                        o = c % 2
                        dve.wait_ge(swa_exp, layer * TILES + c + 1)
                        step(dve.tensor_tensor(rl[o], lsum[o], esink[o], ALU.add))
                        step(dve.reciprocal(rl[o], rl[o]))
                        dve.wait_ge(swa_o, layer * TILES + c + 1)
                        done(dve.tensor_tensor(swa_y[o][:], heads(swa_bank(c, 0)[:, 0:BW], 6),
                                               rl[o][:, :, None].to_broadcast([P, 6, HD]), ALU.mult), swa_yr)
                    elif kind == "swa_yT":
                        c = e[1]
                        y_split(layer, e, swa_bank(c, 1)[:, 0:BW].rearrange("p (k t) -> p k t", k=3),
                                y_hi[:, 5:8, c * P:(c + 1) * P], y_lo[:, 5:8, c * P:(c + 1) * P])
                    elif kind == "ret_sc":
                        c = e[1]
                        dve.wait_ge(ret_sc, layer * TILES + c + 1)
                        for g in range(2):
                            last = dve.tensor_tensor(scm[:, g, :, :],
                                                     banks[4 + g][:, 0:BW].rearrange("p (h t) -> p h t", h=3),
                                                     mask3(T_("lowT")), ALU.mult)
                        done(last, ret_scm)
                    elif kind == "ret_o":
                        c = e[1]
                        if c == 0:
                            step(dve.memset(state[:], 0.0))
                        dve.wait_ge(ret_o, layer * TILES + c + 1)
                        o = heads(banks[4][:, 0:BW], 6)
                        step(dve.tensor_reduce(rmu, o, AX.X, ALU.add))
                        step(dve.tensor_scalar(rmu, rmu, 1.0 / HD, None, ALU.mult))
                        done(dve.tensor_tensor(heads(ret_oc[:], 6), o, rmu[:, :, None].to_broadcast([P, 6, HD]),
                                          ALU.subtract), ret_oread)
                        dve.wait_ge(ret_oread, layer * TILES + c + 1)
                        step(dve.tensor_tensor(ret_sq[:], ret_oc[:], ret_oc[:], ALU.mult))
                        done(dve.tensor_reduce(rvar, heads(ret_sq[:], 6), AX.X, ALU.add), ret_v)
                        if c < TILES - 1:
                            dve.wait_ge(ret_kv, layer * 3 + c + 1)
                            for g in range(2):
                                r, q = slice(HD * g, HD * (g + 1)), slice(HD * g, HD * (g + 1))
                                st = state[r, :, q]
                                kv = banks[5][:, 0:BW].rearrange("p (j e) -> p j e", j=3)[r, :, q]
                                step(dve.tensor_tensor(st, st, kv, ALU.add))
                                last = dve.tensor_tensor(st, st, T_("gcol")[r, :, None].to_broadcast([HD, 3, HD]),
                                                         ALU.mult)
                            done(last, ret_state)
                    elif kind == "ret_norm":
                        c = e[1]
                        dve.wait_ge(gs_ready, layer * TILES + c + 1)
                        dve.wait_ge(ret_r, layer * TILES + c + 1)
                        step(dve.tensor_tensor(heads(ret_oc[:], 6), heads(ret_oc[:], 6),
                                               rr[:, :, None].to_broadcast([P, 6, HD]), ALU.mult))
                        if c:
                            dve.wait_ge(y_T, y_count(layer, ("ret_yT", c - 1)))
                        done(dve.tensor_tensor(ret_y[:], ret_oc[:], bg[:, c, :], ALU.mult), ret_yr)
                    elif kind == "ret_yT":
                        c = e[1]
                        y_split(layer, e, ret_y_bank(c)[:, 0:BW].rearrange("p (k t) -> p k t", k=3),
                                y_hi[:, 2:5, c * P:(c + 1) * P], y_lo[:, 2:5, c * P:(c + 1) * P])
                    elif kind == "gmlp_mix":
                        dve.wait_ge(gm_mix, layer + 1)
                        for b in range(2):
                            mixed = banks[6 + b][:, :].rearrange("p (c h d) -> p c h d", c=2, h=A_HEADS)
                            bias = bs[:, None, :, None].to_broadcast([P, 2, A_HEADS, HD])
                            done(dve.tensor_tensor(vn[:, 2 * b:2 * b + 2, :].rearrange("p c (h d) -> p c h d", h=A_HEADS),
                                              mixed, bias, ALU.add), dve_step)
                        u = uv[:, :, 0:AW]
                        done(dve.tensor_tensor(u, u, vn[:], ALU.mult), gm_ya)
                    elif kind == "gmlp_yT":
                        n = y_count(layer, e)
                        for k in range(2):
                            dve.wait_ge(y_hi_ready, n - 1 + k)
                            done(dve.tensor_tensor(y_lo[:, k, :], banks[6 + k][:, :], y_hi[:, k, :].bitcast(F32),
                                              ALU.subtract), y_lo_ready)
                    elif kind == "mm" and e[1][0] == "in":
                        _, strip, m = e
                        name = strip[1]
                        if strip != group_final(name):
                            continue
                        if name == "ckv":
                            dve.wait_ge(evac_act, evac(layer, name, m)[1])
                            rope_part(ck[:, m, :], 2, m, ck_roped)
                        elif name == "cq":
                            dve.wait_ge(evac_act, evac(layer, name, m)[1])
                            rope_part(cq[m % 2][:], 6, m, cq_roped)
                        elif name in DVE_EVAC:
                            dve.wait_ge(mm_done, mm_count(layer, strip, m))
                            rope_full(layer, DVE_EVAC.index(name), m)
                        elif name == "bg":
                            dve.wait_ge(evac_act, evac(layer, name, m)[1])
                            if m == 0:
                                dve.wait_ge(params_loaded, 16 * 5 * (layer + 1))
                            done(dve.tensor_tensor(bg[:, m, :], bg[:, m, :], gnw[:], ALU.mult), gs_ready)
                        elif name == "a":
                            dve.wait_ge(evac_act, evac(layer, name, m)[1])
                            v = heads(uv[:, m, AW:2 * AW], A_HEADS)
                            vch = heads(vc[:], A_HEADS)
                            step(dve.tensor_reduce(gmu, v, AX.X, ALU.add))
                            step(dve.tensor_scalar(gmu, gmu, 1.0 / HD, None, ALU.mult))
                            step(dve.tensor_tensor(vch, v, gmu[:, :, None].to_broadcast([P, A_HEADS, HD]),
                                                   ALU.subtract))
                            step(dve.tensor_tensor(vsq[:], vc[:], vc[:], ALU.mult))
                            done(dve.tensor_reduce(gvar, heads(vsq[:], A_HEADS), AX.X, ALU.add), gm_v)
                            dve.wait_ge(gm_r, layer * TILES + m + 1)
                            step(dve.tensor_tensor(vch, vch, gr[:, :, None].to_broadcast([P, A_HEADS, HD]),
                                                   ALU.mult))
                            step(dve.tensor_tensor(vc[:], vc[:], lnw[:], ALU.mult))
                            done(dve.tensor_tensor(vn[:, m, :], vc[:], lnb[:], ALU.add), gm_vn)


_ORDER = ["x_in", "p_t", "pre_mix", "w_in", "ln_w", "ln_b", "ws_t", "bs_t", "gn_w", "sinks", "w_out",
          "post_mix", "pre_ffn", "w_ffn_in", "w_ffn_out", "post_ffn", "w_gate", "w_ple", "ple_norm",
          "table", "later"]


def kernel(x, p, norm_mix_pre, w_in, gmlp_ln_w, gmlp_ln_b, gmlp_ws, gmlp_bs, ret_gn_w, attn_sinks,
           w_out, norm_mix_post, norm_ffn_pre, w_ffn_in, w_ffn_out, norm_ffn_post, w_ple_gate,
           w_ple_proj, ple_norm):
    import concourse.bacc as bacc
    from concourse.bass_utils import run_bass_kernel_spmd

    depth = w_in.shape[0]
    table, later = small_tables()
    cols = lambda w: np.asarray(w).reshape(depth, KD, P).transpose(2, 0, 1)
    values = {
        "x_in": np.asarray(x)[0],
        "p_t": np.asarray(p)[:, 0].transpose(0, 2, 1),
        "pre_mix": cols(norm_mix_pre), "pre_ffn": cols(norm_ffn_pre),
        "w_in": w_in, "ln_w": gmlp_ln_w, "ln_b": gmlp_ln_b,
        "ws_t": np.asarray(gmlp_ws).transpose(0, 3, 1, 2),
        "bs_t": np.asarray(gmlp_bs).transpose(0, 2, 1),
        "gn_w": ret_gn_w, "sinks": attn_sinks, "w_out": w_out, "post_mix": norm_mix_post,
        "w_ffn_in": w_ffn_in, "w_ffn_out": w_ffn_out, "post_ffn": norm_ffn_post,
        "w_gate": w_ple_gate, "w_ple": w_ple_proj, "ple_norm": ple_norm,
        "table": table, "later": later,
    }
    nc = bacc.Bacc("TRN2", target_bir_lowering=False, num_devices=1)
    arrays, args = {}, []
    for name in _ORDER:
        a = np.ascontiguousarray(values[name])
        arrays[f"in_{name}"] = a
        args.append(nc.dram_tensor(f"in_{name}", a.shape, mybir.dt.from_np(a.dtype), kind="ExternalInput").ap())
    out = nc.dram_tensor("out", [S, D], F32, kind="ExternalOutput").ap()
    build_trunk(nc, depth, *args, out)
    r = run_bass_kernel_spmd(nc, [arrays], core_ids=[0])
    return r.results[0]["out"].reshape(1, S, D)
```

```python
import numpy as np

import concourse.bass as bass
from concourse import mybir

F32 = mybir.dt.float32
F32R = mybir.dt.float32r
BF16 = mybir.dt.bfloat16
I32 = mybir.dt.int32
ALU = mybir.AluOpType
ACT = mybir.ActivationFunctionType
AX = mybir.AxisListType

P = 128
D = 1024
S = 512
TILES = S // P
KD = D // P
HD = 64
A_HEADS = 4
B_HEADS = 6
C_HEADS = 6
BW = B_HEADS * HD
AW = A_HEADS * HD
FF = 2816
FCH = FF // P
PLE = 256
EPS = 1e-6
NEG = -1e30
SLOTS = 3
RAWS = 3
PIECE = 1024

GROUPS = {
    "ckv": (2 * AW + 5 * BW, 256),
    "cq": (2 * AW + 4 * BW, BW),
    "bk": (2 * AW + BW, BW),
    "bq": (2 * AW, BW),
    "bv": (2 * AW + 2 * BW, BW),
    "a": (0, 2 * AW),
    "bg": (2 * AW + 3 * BW, BW),
}
GNAMES = list(GROUPS)


def plan_strips():
    strips = []
    for g, (_, width) in GROUPS.items():
        n = 1 if width == 256 else 2
        strips += [("in", g, i) for i in range(n)]
    strips += [("out", None, i) for i in (3, 2, 1, 0)]
    strips += [("ffn", None, j) for j in range(FCH)]
    strips += [("fo", None, i) for i in range(FCH // 2)]
    strips += [("ple", None, 0)]
    strips += [("gate", None, i) for i in range(4)]
    return strips


STRIPS = plan_strips()
NS = len(STRIPS)
SIDX = {s: i for i, s in enumerate(STRIPS)}


def plan_mixers():
    at = {}

    def put(u, *e):
        at.setdefault(u, []).append(e)

    for c in range(TILES):
        put(9 + c, "swa_T", c)
        u = (13, 18, 24, 29)[c]
        for step, name in ((0, "swa_cur"), (1, "swa_prev"), (4, "swa_PT"), (6, "swa_o"), (9, "swa_yT")):
            put(u + step, name, c)
        u = 34 + 4 * c
        for step, name in ((0, "ret_T"), (2, "ret_sc"), (3, "ret_o")):
            put(u + step, name, c)
        put(41 + c, "gmlp_v", c)
        put(42 + c, "gmlp_n", c)
    for c in range(TILES):
        put(48 + c, "ret_norm", c)
        put(50 + c, "ret_yT", c)
    return at


def plan_schedule(depth):
    ev = []
    strips = {kind: [s for s in STRIPS if s[0] == kind] for kind, _, _ in STRIPS}
    ins, o, f, fo, g = (strips[kind] for kind in ("in", "out", "ffn", "fo", "gate"))
    ple = ("ple", None, 0)
    layer = 0

    def add(*e, lay=None):
        ev.append((layer if lay is None else lay, e))

    def mm(strip, m, lay=None):
        add("mm", strip, m, lay=lay)

    def close(strip):
        add("conv", SIDX[strip] + SLOTS)

    def tail(pair, renew, after):
        lay = layer + (after == "mix")
        for m in range(TILES):
            mm(pair[0], m)
            if m >= 1:
                add(*renew, m - 1)
            if m >= 2 and lay < depth:
                add("T", after, m - 2, lay=lay)
            if m >= 1 and after != "gate" and lay < depth:
                add("pre", after, m - 1, lay=lay)
            if m == TILES - 1:
                close(pair[0])
            mm(pair[1], m)

    for m, stage in ((0, "pre"), (1, "pre"), (0, "conv"), (0, "T"), (2, "pre"), (1, "T"), (3, "pre")):
        add("conv", 0) if stage == "conv" else add(stage, "mix", m)
    for layer in range(depth):
        if layer == 0:
            mm(ins[0], 0)
            add("T", "mix", 2)
            add("conv", 1)
            mm(ins[0], 1)
            mm(ins[0], 2)
            add("T", "mix", 3)
            add("conv", 2)
            mm(ins[1], 0)
            mm(ins[1], 1)
            mm(ins[0], 3)
            close(ins[0])
        at = plan_mixers()
        u = 4
        for s in ins[1:]:
            for m in range(TILES):
                if u >= 6:
                    mm(s, m)
                for e in at.pop(u, ()):
                    add(*e)
                u += 1
            close(s)
        mm(o[0], 0)
        for e in at.pop(52):
            add(*e)
        mm(o[1], 0)
        for e in at.pop(53):
            add(*e)
        add("gmlp_mix")
        mm(o[0], 1)
        mm(o[1], 1)
        add("gmlp_yT")
        mm(o[0], 2)
        mm(o[1], 2)
        assert not at, at
        mm(o[0], 3)
        close(o[0])
        mm(o[1], 3)
        close(o[1])
        tail(o[2:], ("post", "mix"), "ffn")
        add("post", "mix", 3)
        close(o[3])
        mm(f[0], 0)
        add("T", "ffn", 2)
        add("pre", "ffn", 3)
        mm(f[1], 0)
        add("T", "ffn", 3)
        mm(f[2], 0)
        for j in range(3):
            mm(f[j], 1)
            close(f[j])
            add("mid", j)
        for j in range(3, FCH):
            mm(f[j], None)
            close(f[j])
            add("mid", j)
        for s in fo[:-2]:
            for m in (2, 3, 0, 1):
                mm(s, m)
            close(s)
        tail(fo[-2:], ("post", "ffn"), "gate")
        add("post", "ffn", 3)
        mm(ple, 0)
        add("T", "gate", 2)
        close(fo[-1])
        mm(ple, 1)
        add("T", "gate", 3)
        add("post", "ple", 0)
        mm(ple, 2)
        add("post", "ple", 1)
        mm(ple, 3)
        close(ple)
        add("post", "ple", 2)
        add("post", "ple", 3)
        for s in g[:2]:
            for m in range(TILES):
                mm(s, m)
            close(s)
        tail(g[2:], ("gated",), "mix")
        nxt = layer + 1
        if nxt < depth:
            mm(ins[0], 0, nxt)
            add("T", "mix", 2, lay=nxt)
            add("gated", 3)
            close(g[3])
            mm(ins[0], 1, nxt)
            mm(ins[0], 2, nxt)
            add("pre", "mix", 3, lay=nxt)
            mm(ins[1], 0, nxt)
            mm(ins[1], 1, nxt)
            add("T", "mix", 3, lay=nxt)
            mm(ins[0], 3, nxt)
            add("conv", SIDX[ins[0]] + SLOTS, lay=nxt)
        else:
            add("gated", 3)
    return ev


ACT_EVAC = ["ckv", "cq", "bv", "a", "bg"]
DVE_EVAC = ["bk", "bq"]
POSTS = ["mix", "ffn", "ple"]
TSTAGES = ["mix", "ffn", "gate"]


def small_tables():
    f = np.float32
    pos = np.arange(S, dtype=f)

    def angles(half, theta):
        inv = (1.0 / (f(theta) ** (np.arange(half, dtype=f) / f(half)))).astype(f)
        a = (pos[:, None] * inv[None, :]).astype(f).reshape(TILES, P, half).transpose(1, 0, 2)
        return np.cos(a).astype(f).reshape(P, -1), np.sin(a).astype(f).reshape(P, -1)

    rc, rs = angles(HD // 2, 10000.0)
    sc, ss = angles(HD // 8, 500000.0)
    i = np.arange(P)
    lower_t = (i[:, None] <= i[None, :]).astype(f)
    upper_t = (i[:, None] > i[None, :]).astype(f)
    later = (i[None, :] > i[:, None]).astype(np.int32)
    g = np.log(1.0 - 2.0 ** (-5.0 - np.arange(B_HEADS, dtype=np.float64)))
    qs = np.exp((i[:, None] + 1.0) * g[None, :])
    ks = np.exp(-(i[:, None] + 1.0) * g[None, :]) * HD ** -0.5
    gc = np.exp(P * g)
    gcol = np.stack([np.where(i < HD, gc[2 * j], gc[2 * j + 1]) for j in range(3)], 1)
    table = np.concatenate([np.eye(P), rc, rs, sc, ss, lower_t, upper_t, qs, ks, gcol], 1)
    return np.ascontiguousarray(table.astype(f)), later


TABLE_COLS = {}
_at = 0
for _n, _w in (("ident", P), ("rcos", 128), ("rsin", 128), ("scos", 32), ("ssin", 32), ("lowT", P),
               ("upT", P), ("qs", 6), ("ks", 6), ("gcol", 3)):
    TABLE_COLS[_n] = (_at, _at + _w)
    _at += _w
TABLE_W = _at


def build_trunk(nc, depth, x_in, p_t, pre_mix, w_in, ln_w, ln_b, ws_t, bs_t, gn_w, sinks, w_out,
                post_mix, pre_ffn, w_ffn_in, w_ffn_out, post_ffn, w_gate, w_ple, ple_norm,
                table, later, out):
    KB = 1024
    BASE = (nc.sbuf_base + 31) // 32 * 32

    def place(name, shape, dt, kb):
        return nc.alloc_sbuf_tensor_at(name, shape, dt, offset=BASE + int(kb * KB))

    x = place("x", [P, TILES, D], F32, 0)
    h_hi = place("h_hi", [P, KD, S], F32R, 16)
    h_lo = place("h_lo", [P, KD, S], F32R, 32)
    mid_hi = place("mid_hi", [P, FCH, S], F32R, 48)
    mid_lo = place("mid_lo", [P, FCH, S], F32R, 92)
    raw = [place(f"raw{i}", [P, PIECE], F32, 136 + 4 * i) for i in range(RAWS)]
    w_hi = [place(f"w_hi{i}", [P, 2 * PIECE], F32R, 148 + 8 * i) for i in range(SLOTS)]
    w_lo = [place(f"w_lo{i}", [P, 2 * PIECE], F32R, 172 + 8 * i) for i in range(SLOTS)]
    post_w = place("post_w", [P, D], F32, 196)
    tab = place("tab", [P, TABLE_W], F32, 200)
    later_m = place("later_m", [P, P], I32, 202.84375)
    tiny = place("tiny", [P, 232], F32, 203.34375)
    gnw = place("gnw", [P, BW], F32, 204.25)
    lnw = place("lnw", [P, AW], F32, 205.75)
    lnb = place("lnb", [P, AW], F32, 206.75)
    silu_g = place("silu_g", [P, S], F32, 205.75)
    y_hi = place("y_hi", [P, KD, S], F32R, 48)
    y_lo = place("y_lo", [P, KD, S], F32R, 64)
    bg = place("bg", [P, TILES, BW], F32, 80)
    bv = place("bv", [P, TILES, BW], F32, 86)
    bk = place("bk", [P, TILES, BW], F32, 92)
    bq = place("bq", [P, TILES, BW], F32, 98)
    kqT = place("kqT", [P, 2, 3, P], F32, 104)
    scm = place("scm", [P, 2, 3, P], F32, 107)
    prob = [place(f"prob{i}", [P, C_HEADS, P], F32, (110, 48)[i]) for i in range(2)]
    ptl = [place(f"ptl{i}", [P, C_HEADS, P], F32, (113, 64)[i]) for i in range(2)]
    ptu = [place(f"ptu{i}", [P, C_HEADS, P], F32, (116, 54)[i]) for i in range(2)]
    swa_y = [place(f"swa_y{i}", [P, C_HEADS, HD], F32, (110, 48)[i]) for i in range(2)]
    cq = [place(f"cq{i}", [P, BW], F32, 113 + 1.5 * i) for i in range(2)]
    ck = place("ck", [P, TILES, P], F32, 116)
    rope_x = place("rope_x", [P, BW], F32, 119)
    rope_a = place("rope_a", [P, BW], F32, 120.5)
    rope_b = place("rope_b", [P, BW], F32, 122)
    ret_oc = bq
    ret_y = bk
    ret_sq = place("ret_sq", [P, BW], F32, 120.5)
    cT = place("cT", [P, 4, S], F32, 123.5)
    uv = place("uv", [P, TILES, 2 * AW], F32, 123.5)
    cv = place("cv", [P, TILES, P], F32, 131.5)
    wsT = place("wsT", [P, A_HEADS, P], F32, 133.5)
    vn = place("vn", [P, TILES, AW], F32, 110)
    vsq = place("vsq", [P, AW], F32, 115)
    state = place("state", [P, 3, P], F32, 196)
    upd = place("upd", [P, D], F32, 92)
    xn = [place(f"xn{i}", [P, D], F32, 96 + 4 * i) for i in range(2)]
    junk = place("junk", [P, D], BF16, 104)
    pre_w = place("pre_w", [P, D], F32, 106)
    ple_n = place("ple_n", [P, TILES, D], F32, 48)
    ple_w = place("ple_w", [P, D], F32, 64)
    p_raw = place("p_raw", [P, 2, S], F32, 68)
    p_hi = place("p_hi", [P, 2, S], F32R, 72)
    p_lo = place("p_lo", [P, 2, S], F32R, 76)
    sig = place("sig", [P, D], F32, 80)

    def T_(name):
        a, b = TABLE_COLS[name]
        return tab[:, a:b]

    tiny_at = [0]

    def small(n):
        a = tiny_at[0]
        tiny_at[0] += n
        return tiny[:, a:a + n]

    bs = small(A_HEADS)
    snk = small(C_HEADS)
    ss_post = [small(2) for _ in range(2)]
    r_post = [small(1) for _ in range(2)]
    ss_pre = [small(1) for _ in range(2)]
    t_pre = small(1)
    t_post = small(1)
    r_pre = [small(1) for _ in range(2)]
    half_neg = small(6)
    neg_big = small(1)
    mx = [small(6) for _ in range(2)]
    negm = [small(6) for _ in range(2)]
    lsum = [small(6) for _ in range(2)]
    esink = [small(6) for _ in range(2)]
    rl = [small(6) for _ in range(2)]
    dsink = [small(6) for _ in range(2)]
    rmu = small(6)
    rvar = small(6)
    rr = [small(6) for _ in range(TILES)]
    rvt = small(6)
    gmu = small(4)
    gvar = small(4)
    gvt = small(4)
    gr = [small(4) for _ in range(2)]

    banks = [nc.alloc_psum_tensor(f"bank{i}", [P, 512], F32) for i in range(8)]

    sems = {}

    def sem(name):
        sems[name] = nc.alloc_semaphore(name)
        return sems[name]

    x_loaded = [sem(f"x_loaded{m}") for m in range(TILES)]
    raw_loaded = [sem(f"raw_loaded{i}") for i in range(RAWS)]
    table_loaded = sem("table_loaded")
    consts_loaded = sem("consts_loaded")
    params_loaded = sem("params_loaded")
    ws_loaded = sem("ws_loaded")
    post_w_loaded = sem("post_w_loaded")
    pre_w_loaded = sem("pre_w_loaded")
    ple_w_loaded = sem("ple_w_loaded")
    p_loaded = sem("p_loaded")
    stored = sem("stored")
    hi_ready = sem("hi_ready")
    lo_ready = sem("lo_ready")
    mm_done = sem("mm_done")
    x_T = sem("x_T")
    h_hi_ready = sem("h_hi_ready")
    h_lo_ready = sem("h_lo_ready")
    post_sq = sem("post_sq")
    post_r = sem("post_r")
    x_new = sem("x_new")
    ple_ready = sem("ple_ready")
    pre_sq = sem("pre_sq")
    pre_r = sem("pre_r")
    xn_ready = sem("xn_ready")
    evac_act = sem("evac_act")
    evac_dve = sem("evac_dve")
    ck_roped = sem("ck_roped")
    cq_roped = sem("cq_roped")
    b_roped = sem("b_roped")
    gs_ready = sem("gs_ready")
    swa_T = sem("swa_T")
    swa_cT = sem("swa_cT")
    swa_cur = sem("swa_cur")
    swa_S = sem("swa_S")
    swa_prev = sem("swa_prev")
    swa_m = sem("swa_m")
    swa_exp = sem("swa_exp")
    swa_PT = sem("swa_PT")
    swa_PTm = sem("swa_PTm")
    swa_o = sem("swa_o")
    swa_yr = sem("swa_yr")
    ret_T = sem("ret_T")
    ret_kqT = sem("ret_kqT")
    ret_sc = sem("ret_sc")
    ret_scm = sem("ret_scm")
    ret_o = sem("ret_o")
    ret_kv = sem("ret_kv")
    ret_state = sem("ret_state")
    ret_oread = sem("ret_oread")
    ret_v = sem("ret_v")
    ret_r = sem("ret_r")
    ret_yr = sem("ret_yr")
    y_T = sem("y_T")
    y_hi_ready = sem("y_hi_ready")
    y_lo_ready = sem("y_lo_ready")
    ws_ready = sem("ws_ready")
    gm_v = sem("gm_v")
    gm_r = sem("gm_r")
    gm_vn = sem("gm_vn")
    gm_mix = sem("gm_mix")
    gm_ya = sem("gm_ya")
    silu_ready = sem("silu_ready")
    prod_ready = sem("prod_ready")
    mid_hi_ready = sem("mid_hi_ready")
    mid_lo_ready = sem("mid_lo_ready")
    p_hi_ready = sem("p_hi_ready")
    p_lo_ready = sem("p_lo_ready")
    sig_ready = sem("sig_ready")
    pool_step = sem("pool_step")
    pool_init = sem("pool_init")
    dve_step = sem("dve_step")

    schedule = plan_schedule(depth)
    order_mm = {(layer, *e[1:]): i for i, (layer, e) in enumerate(
        [entry for entry in schedule if entry[1][0] == "mm"])}
    last_use = {layer * NS + SIDX[strip]: i for (layer, strip, _), i in order_mm.items()}
    order_yT = []
    for layer, e in schedule:
        if e[0] in ("swa_yT", "ret_yT", "gmlp_yT"):
            order_yT += [(layer, e)] * (2 if e[0] == "gmlp_yT" else 1)

    def y_count(layer, e):
        return len(order_yT) - order_yT[::-1].index((layer, e))

    order_T = [(layer, *e[1:]) for layer, e in schedule if e[0] == "T"]

    def t_count(layer, stage, m, half=1):
        return 2 * order_T.index((layer, stage, m)) + half + 1

    order_post = [(layer, *e[1:]) for layer, e in schedule if e[0] == "post"]

    def post_count(layer, stage, m):
        return order_post.index((layer, stage, m)) + 1

    def post_used(n):
        layer, stage, m = order_post[n - 1]
        if stage == "ple":
            return ple_ready, layer * TILES + m + 1
        return x_new, x_count(layer, stage, m)

    def x_count(layer, stage, m):
        return layer * 3 * TILES + TSTAGES.index(stage) * TILES + m + 1

    def pre_count(layer, stage, m):
        return layer * 2 * TILES + (TILES if stage == "ffn" else 0) + m + 1

    def mm_count(layer, strip, m):
        return order_mm[(layer, strip, m)] + 1

    def used_count(g):
        return last_use[g] + 1

    def group_final(gname):
        n = 1 if GROUPS[gname][1] == 256 else 2
        return ("in", gname, n - 1)

    def evac(layer, gname, m):
        if gname in ACT_EVAC:
            return evac_act, layer * 4 * len(ACT_EVAC) + 4 * ACT_EVAC.index(gname) + m + 1
        return evac_dve, layer * 4 * len(DVE_EVAC) + 4 * DVE_EVAC.index(gname) + m + 1

    def pieces(g):
        layer, (kind, name, i) = g // NS, STRIPS[g % NS]

        def view(w, k0, kn, c0, cn):
            return w[layer, k0 * P:(k0 + kn) * P, c0:c0 + cn].rearrange("(k p) c -> p k c", p=P)

        if kind == "in":
            c0, width = GROUPS[name]
            kn = KD // (1 if width == 256 else 2)
            return [view(w_in, i * kn + j * kn // 2, kn // 2, c0, width) for j in range(2)]
        if kind == "ffn":
            return [view(w_ffn_in, 0, KD, j * FF + i * P, P) for j in range(2)]
        w = {"out": w_out, "fo": w_ffn_out, "gate": w_gate, "ple": w_ple}[kind]
        return [view(w, 2 * i + j, 1, 0, D) for j in range(2)]

    def piece_size(g):
        kind, name, _ = STRIPS[g % NS]
        return GROUPS[name][1] * (4 if GROUPS[name][1] == 256 else 2) if kind == "in" else PIECE

    def swa_bank(c, g):
        return banks[4 + 2 * (c % 2) + g]

    def ret_y_bank(c):
        return banks[7] if c < TILES - 1 else banks[5]

    with nc.Block() as block:

        @block.sync
        def _(sp):
            def load_x(m):
                sp.dma_start(x[:, m, :], x_in[m * P:(m + 1) * P, :]).then_inc(x_loaded[m], 16)

            load_x(0)
            sp.dma_start(pre_w[:], pre_mix[0:1, :].partition_broadcast(P)).then_inc(pre_w_loaded, 16)
            sp.dma_start(tab[:], table).then_inc(table_loaded, 16)
            load_x(1)
            for g in range(depth * NS):
                layer, s = divmod(g, NS)
                if s == 3:
                    if layer:
                        sp.wait_ge(mm_done, used_count((layer - 1) * NS + SIDX[("gate", None, 0)]))
                        sp.wait_ge(x_new, x_count(layer - 1, "ffn", 3))
                    sp.dma_start(wsT[:], ws_t[layer]).then_inc(ws_loaded, 16)
                    sp.dma_start(bs, bs_t[layer]).then_inc(params_loaded, 16)
                    sp.dma_start(snk, sinks[layer:layer + 1, :].partition_broadcast(P)).then_inc(params_loaded, 16)
                    sp.dma_start(gnw[:], gn_w[layer:layer + 1, :].partition_broadcast(P)).then_inc(params_loaded, 16)
                    sp.dma_start(lnw[:], ln_w[layer:layer + 1, :].partition_broadcast(P)).then_inc(params_loaded, 16)
                    sp.dma_start(lnb[:], ln_b[layer:layer + 1, :].partition_broadcast(P)).then_inc(params_loaded, 16)
                if s == SIDX[("ffn", None, 0)]:
                    sp.wait_ge(ret_o, (layer + 1) * TILES)
                    sp.dma_start(post_w[:], post_mix[layer:layer + 1, :].partition_broadcast(P)).then_inc(post_w_loaded, 16)
                    sp.dma_start(pre_w[:], pre_ffn[layer:layer + 1, :].partition_broadcast(P)).then_inc(pre_w_loaded, 16)
                if s == SIDX[("ffn", None, 6)]:
                    sp.wait_ge(x_new, x_count(layer, "mix", 3))
                    sp.dma_start(post_w[:], post_ffn[layer:layer + 1, :].partition_broadcast(P)).then_inc(post_w_loaded, 16)
                if s == SIDX[("ple", None, 0)]:
                    sp.wait_ge(mm_done, used_count(layer * NS + SIDX[("fo", None, 5)]))
                    sp.dma_start(ple_w[:], ple_norm[layer:layer + 1, :].partition_broadcast(P)).then_inc(ple_w_loaded, 16)
                    if layer + 1 < depth:
                        sp.dma_start(pre_w[:], pre_mix[layer + 1:layer + 2, :].partition_broadcast(P)).then_inc(
                            pre_w_loaded, 16)
                    sp.dma_start(p_raw[:], p_t[layer].rearrange("(k p) t -> p k t", p=P)).then_inc(p_loaded, 16)
                n = piece_size(g)
                for j, view in enumerate(pieces(g)):
                    q = 2 * g + j
                    if q >= RAWS:
                        sp.wait_ge(lo_ready, q - RAWS + 1)
                    dst = raw[q % RAWS][:, 0:n].rearrange("p (k c) -> p k c", k=view.shape[1])
                    sp.dma_start(dst, view).then_inc(raw_loaded[q % RAWS], 16)
                if g == 0:
                    load_x(2)
                    load_x(3)
                    sp.dma_start(later_m[:], later).then_inc(consts_loaded, 16)
            for m in range(TILES):
                sp.wait_ge(x_new, x_count(depth - 1, "gate", m))
                sp.dma_start(out[m * P:(m + 1) * P, :], x[:, m, :]).then_inc(stored, 16)
            sp.wait_ge(stored, 16 * TILES)

        @block.tensor
        def _(pe):
            def mm3(out_ap, a_hi, a_lo, b_hi, b_lo, start, stop):
                pe.matmul(out_ap, a_hi, b_hi, start=start, stop=False, skip_group_check=True)
                pe.matmul(out_ap, a_hi, b_lo, start=False, stop=False, skip_group_check=True)
                return pe.matmul(out_ap, a_lo, b_hi, start=False, stop=stop, skip_group_check=True)

            def ts(m):
                return slice(m * P, (m + 1) * P)

            def mm_in(layer, g, strip, m):
                _, name, i = strip
                width = GROUPS[name][1]
                n = 1 if width == 256 else 2
                kn = KD // n
                if i == 0:
                    gi = GNAMES.index(name)
                    if gi:
                        pe.wait_ge(*evac(layer, GNAMES[gi - 1], m))
                    else:
                        pe.wait_ge(h_lo_ready, t_count(layer, "mix", m))
                hi = w_hi[g % SLOTS][:, 0:kn * width].rearrange("p (k c) -> p k c", k=kn)
                lo = w_lo[g % SLOTS][:, 0:kn * width].rearrange("p (k c) -> p k c", k=kn)
                for k in range(kn):
                    kk = i * kn + k
                    last = mm3(banks[m][:, 0:width], h_hi[:, kk, ts(m)], h_lo[:, kk, ts(m)],
                               hi[:, k, :], lo[:, k, :], kk == 0, kk == KD - 1)
                return last

            def mm_rows(a_hi, a_lo, k0, g, m, first, final):
                for k in range(2):
                    for half in range(2):
                        c = slice(k * D + half * 512, k * D + half * 512 + 512)
                        last = mm3(banks[2 * m + half][:, :], a_hi[:, k0 + k, ts(m)], a_lo[:, k0 + k, ts(m)],
                                   w_hi[g % SLOTS][:, c], w_lo[g % SLOTS][:, c],
                                   first and k == 0, final and k == 1)
                return last

            def mm_ffn(layer, g, strip, m):
                j = strip[2]
                cols = slice(0, S) if m is None else slice(m * S // 2, (m + 1) * S // 2)
                for part in range(2):
                    for k in range(KD):
                        c = slice(part * PIECE + k * P, part * PIECE + (k + 1) * P)
                        last = mm3(banks[2 * (j % 4) + part][:, cols], w_hi[g % SLOTS][:, c],
                                   w_lo[g % SLOTS][:, c], h_hi[:, k, cols], h_lo[:, k, cols],
                                   k == 0, k == KD - 1)
                return last

            def block_of(layer, strip, m):
                g = layer * NS + SIDX[strip]
                kind, _, i = strip
                pe.wait_ge(lo_ready, 2 * (g + 1))
                if kind == "in":
                    last = mm_in(layer, g, strip, m)
                elif kind == "out":
                    if i == 3:
                        if m < 2:
                            pe.wait_ge(*evac(layer, GNAMES[-1], 2 * m + 1))
                        if m == 2:
                            pe.wait_ge(y_lo_ready, y_count(layer, ("ret_yT", 3)))
                    need = {2: ("ret_yT", m), 3: ("swa_yT", m), 1: ("ret_yT", m), 0: ("gmlp_yT",)}[i]
                    if m == 3:
                        need = ("gmlp_yT",)
                    pe.wait_ge(y_lo_ready, y_count(layer, need))
                    last = mm_rows(y_hi, y_lo, 2 * i, g, m, i == 3, i == 0)
                elif kind == "ffn":
                    if m is not None:
                        pe.wait_ge(h_lo_ready, t_count(layer, "ffn", max(2 * m + 1, i)))
                    else:
                        if i >= 4:
                            pe.wait_ge(mid_lo_ready, layer * FCH + i - 3)
                        else:
                            pe.wait_ge(h_lo_ready, t_count(layer, "ffn", 3))
                    last = mm_ffn(layer, g, strip, m)
                elif kind == "fo":
                    if i == 0:
                        last_in_pair = max(j for j in range(FCH) if j % 4 == m)
                        pe.wait_ge(mid_lo_ready, layer * FCH + last_in_pair + 1)
                    pe.wait_ge(mid_lo_ready, layer * FCH + 2 * i + 2)
                    last = mm_rows(mid_hi, mid_lo, 2 * i, g, m, i == 0, i == FCH // 2 - 1)
                elif kind == "ple":
                    pe.wait_ge(h_lo_ready, t_count(layer, "gate", m))
                    pe.wait_ge(p_lo_ready, layer + 1)
                    last = mm_rows(p_hi, p_lo, 0, g, m, True, True)
                else:
                    if i == 0:
                        pe.wait_ge(ple_ready, layer * TILES + m + 1)
                    last = mm_rows(h_hi, h_lo, 2 * i, g, m, i == 0, i == 3)
                last.then_inc(mm_done, 1)

            def transposes(layer, stage, m):
                if stage == "gate":
                    pe.wait_ge(x_new, x_count(layer, "ffn", m))
                    src = x[:, m, :]
                else:
                    n = pre_count(layer, stage, m)
                    pe.wait_ge(xn_ready, n)
                    src = xn[(n - 1) % 2][:, :]
                for half in range(2):
                    for k in range(4):
                        kk = 4 * half + k
                        last = pe.transpose(banks[2 * m + half][:, k * P:(k + 1) * P],
                                            src[:, kk * P:(kk + 1) * P], T_("ident"))
                    last.then_inc(x_T, 1)

            def rows(g):
                return slice(HD * g, HD * (g + 1))

            pe.wait_ge(table_loaded, 16)
            for layer, e in schedule:
                kind = e[0]
                if kind == "mm":
                    block_of(layer, e[1], e[2])
                elif kind == "T":
                    transposes(layer, e[1], e[2])
                elif kind == "swa_T":
                    c = e[1]
                    pe.wait_ge(ck_roped, layer * TILES + c + 1)
                    pe.wait_ge(cq_roped, layer * TILES + c + 1)
                    if c:
                        pe.wait_ge(swa_cT, layer * TILES + c)
                    for j in range(3):
                        pe.transpose(banks[4][:, j * P:(j + 1) * P], cq[c % 2][:, j * P:(j + 1) * P],
                                     T_("ident"))
                    pe.transpose(banks[4][:, 3 * P:4 * P], ck[:, c, :],
                                 T_("ident")).then_inc(swa_T, 1)
                elif kind in ("swa_cur", "swa_prev"):
                    c = e[1]
                    k0 = c if kind == "swa_cur" else c - 1
                    if k0 < 0:
                        continue
                    if kind == "swa_cur":
                        pe.wait_ge(swa_cT, layer * TILES + TILES)
                        if c >= 2:
                            pe.wait_ge(y_lo_ready, y_count(layer, ("swa_yT", c - 2)))
                    else:
                        pe.wait_ge(swa_S, layer * TILES + c + 1)
                    for g in range(2):
                        for j in range(3):
                            last = pe.matmul(swa_bank(c, g)[:, j * P:(j + 1) * P],
                                             cT[rows(g), j, ts(c)], cT[rows(g), 3, ts(k0)],
                                             start=True, stop=True, skip_group_check=True)
                    last.then_inc(swa_cur if kind == "swa_cur" else swa_prev, 1)
                elif kind == "swa_PT":
                    c = e[1]
                    pe.wait_ge(swa_exp, layer * TILES + c + 1)
                    for hh in range(C_HEADS):
                        last = pe.transpose(swa_bank(c, hh // 3)[:, (hh % 3) * P:(hh % 3 + 1) * P],
                                            prob[c % 2][:, hh, :], T_("ident"))
                    last.then_inc(swa_PT, 1)
                elif kind == "swa_o":
                    c = e[1]
                    pe.wait_ge(swa_PTm, layer * TILES + c + 1)
                    for hh in range(C_HEADS):
                        o = swa_bank(c, 0)[:, hh * HD:(hh + 1) * HD]
                        g = hh // 3
                        last = pe.matmul(o, ptl[c % 2][:, hh, :], cv[:, c, rows(g)], start=True, stop=(c == 0),
                                         skip_group_check=True)
                        if c:
                            last = pe.matmul(o, ptu[c % 2][:, hh, :], cv[:, c - 1, rows(g)], start=False,
                                             stop=True, skip_group_check=True)
                    last.then_inc(swa_o, 1)
                elif kind == "swa_yT":
                    c = e[1]
                    pe.wait_ge(swa_yr, layer * TILES + c + 1)
                    flat = swa_y[c % 2][:, :, :].rearrange("p h d -> p (h d)")
                    for k in range(3):
                        last = pe.transpose(swa_bank(c, 1)[:, k * P:(k + 1) * P], flat[:, k * P:(k + 1) * P],
                                            T_("ident"))
                    last.then_inc(y_T, 1)
                elif kind == "ret_T":
                    c = e[1]
                    pe.wait_ge(b_roped, layer * 2 * TILES + TILES + c + 1)
                    if c:
                        pe.wait_ge(ret_oread, layer * TILES + c)
                        pe.wait_ge(ret_state, layer * 3 + c)
                    else:
                        pe.wait_ge(y_lo_ready, y_count(layer, ("swa_yT", 2)))
                    for i, src in enumerate((bk, bq)):
                        for j in range(3):
                            last = pe.transpose(banks[4 + i][:, j * P:(j + 1) * P],
                                                src[:, c, j * P:(j + 1) * P], T_("ident"))
                    last.then_inc(ret_T, 1)
                elif kind == "ret_sc":
                    c = e[1]
                    pe.wait_ge(ret_kqT, layer * TILES + c + 1)
                    for g in range(2):
                        for j in range(3):
                            last = pe.matmul(banks[4 + g][:, j * P:(j + 1) * P], kqT[rows(g), 0, j, :],
                                             kqT[rows(g), 1, j, :], start=True, stop=True,
                                             skip_group_check=True)
                    last.then_inc(ret_sc, 1)
                elif kind == "ret_o":
                    c = e[1]
                    pe.wait_ge(ret_scm, layer * TILES + c + 1)
                    if c == 0:
                        pe.wait_ge(evac_act, evac(layer, "bv", 3)[1])
                    else:
                        pe.wait_ge(ret_state, layer * 3 + c)
                    for j in range(3):
                        if c:
                            pe.matmul(banks[4][:, j * P:(j + 1) * P], kqT[:, 1, j, :], state[:, j, :],
                                      start=True, stop=False, skip_group_check=True)
                        for g in range(2):
                            cols = slice(j * P + g * HD, j * P + (g + 1) * HD)
                            last = pe.matmul(banks[4][:, cols], scm[:, g, j, :], bv[:, c, cols],
                                             start=(c == 0), stop=True, skip_group_check=True)
                    last.then_inc(ret_o, 1)
                    if c < TILES - 1:
                        for j in range(3):
                            last = pe.matmul(banks[5][:, j * P:(j + 1) * P], bk[:, c, j * P:(j + 1) * P],
                                             bv[:, c, j * P:(j + 1) * P], start=True, stop=True,
                                             skip_group_check=True)
                        last.then_inc(ret_kv, 1)
                elif kind == "ret_yT":
                    c = e[1]
                    pe.wait_ge(ret_yr, layer * TILES + c + 1)
                    if c == 0:
                        pe.wait_ge(y_lo_ready, y_count(layer, ("swa_yT", 3)))
                    elif c < TILES - 1:
                        pe.wait_ge(y_lo_ready, y_count(layer, ("ret_yT", c - 1)))
                    for k in range(3):
                        last = pe.transpose(ret_y_bank(c)[:, k * P:(k + 1) * P], ret_y[:, c, k * P:(k + 1) * P],
                                            T_("ident"))
                    last.then_inc(y_T, 1)
                elif kind == "gmlp_mix":
                    pe.wait_ge(gm_vn, layer * TILES + TILES)
                    pe.wait_ge(ws_ready, layer + 1)
                    pe.wait_ge(y_lo_ready, y_count(layer, ("ret_yT", 2)))
                    for c in range(TILES):
                        for hh in range(A_HEADS):
                            col = (c % 2) * AW + hh * HD
                            last = pe.matmul(banks[6 + c // 2][:, col:col + HD], wsT[:, hh, :],
                                             vn[:, c, hh * HD:(hh + 1) * HD], start=True, stop=True,
                                             skip_group_check=True)
                    last.then_inc(gm_mix, 1)
                elif kind == "gmlp_yT":
                    pe.wait_ge(gm_ya, layer + 1)
                    for k in range(2):
                        for c in range(TILES):
                            last = pe.transpose(banks[6 + k][:, c * P:(c + 1) * P],
                                                uv[:, c, k * P:(k + 1) * P], T_("ident"))
                        last.then_inc(y_T, 1)

        @block.scalar
        def _(act):
            def y_split(layer, e, bank, dst):
                n = y_count(layer, e)
                act.wait_ge(y_T, n)
                act.activation(dst, bank, ACT.Copy).then_inc(y_hi_ready, 1)

            def conv(g):
                if g >= depth * NS:
                    return
                n = piece_size(g)
                if g >= SLOTS:
                    act.wait_ge(mm_done, used_count(g - SLOTS))
                for j in range(2):
                    q = 2 * g + j
                    act.wait_ge(raw_loaded[q % RAWS], 16 * (q // RAWS + 1))
                    act.activation(w_hi[g % SLOTS][:, j * n:(j + 1) * n], raw[q % RAWS][:, 0:n],
                                   ACT.Copy).then_inc(hi_ready, 1)

            squares = [0, 0]

            def after_squares():
                if squares[0]:
                    act.wait_ge(pre_sq, squares[0])
                if squares[1]:
                    act.wait_ge(post_sq, squares[1])

            def pre(layer, stage, m):
                n = pre_count(layer, stage, m)
                if layer == 0 and stage == "mix":
                    act.wait_ge(x_loaded[m], 16)
                elif stage == "mix":
                    act.wait_ge(x_new, x_count(layer - 1, "gate", m))
                else:
                    act.wait_ge(x_new, x_count(layer, "mix", m))
                if n > 2:
                    act.wait_ge(pre_r, n - 2)
                after_squares()
                squares[0] += 1
                act.activation(junk[:], x[:, m, :], ACT.Square, scale=D ** -0.5,
                               accum_out=ss_pre[n % 2]).then_inc(pre_sq, 1)

            def split_T(layer, stage, m):
                for half in range(2):
                    dst = h_hi[:, 4 * half:4 * half + 4, m * P:(m + 1) * P]
                    act.wait_ge(x_T, t_count(layer, stage, m, half))
                    src = banks[2 * m + half][:, :].rearrange("p (k t) -> p k t", k=4)
                    act.activation(dst, src, ACT.Copy).then_inc(h_hi_ready, 1)

            for layer, e in schedule:
                kind = e[0]
                if kind == "conv":
                    conv(layer * NS + e[1])
                elif kind == "T":
                    split_T(layer, e[1], e[2])
                elif kind == "post":
                    _, stage, m = e
                    n = post_count(layer, stage, m)
                    strip = {"mix": ("out", None, 0), "ffn": ("fo", None, FCH // 2 - 1),
                             "ple": ("ple", None, 0)}[stage]
                    act.wait_ge(mm_done, mm_count(layer, strip, m))
                    if n > 2:
                        act.wait_ge(post_r, n - 2)
                    after_squares()
                    squares[1] += 2
                    act.activation(junk[:, 0:512], banks[2 * m][:, :], ACT.Square, scale=D ** -0.5,
                                   accum_out=ss_post[n % 2][:, 0:1]).then_inc(post_sq, 1)
                    act.activation(junk[:, 512:D], banks[2 * m + 1][:, :], ACT.Square, scale=D ** -0.5,
                                   accum_out=ss_post[n % 2][:, 1:2]).then_inc(post_sq, 1)
                    if stage == "ffn" and m == 0:
                        act.wait_ge(p_loaded, 16 * (layer + 1))
                        act.activation(p_hi[:], p_raw[:], ACT.Copy).then_inc(p_hi_ready, 1)
                elif kind == "pre":
                    pre(layer, e[1], e[2])
                elif kind == "gated":
                    m = e[1]
                    act.wait_ge(mm_done, mm_count(layer, ("gate", None, 3), m))
                    if m or layer:
                        act.wait_ge(x_new, x_count(layer, "gate", m) - 1)
                    act.activation(sig[:, 0:512], banks[2 * m][:, :], ACT.Sigmoid)
                    act.activation(sig[:, 512:D], banks[2 * m + 1][:, :], ACT.Sigmoid).then_inc(sig_ready, 1)
                elif kind == "mid":
                    j = e[1]
                    act.wait_ge(mm_done, mm_count(layer, ("ffn", None, j), 1 if j < 3 else None))
                    if j or layer:
                        act.wait_ge(prod_ready, layer * FCH + j)
                    if j == 0:
                        act.wait_ge(gm_vn, (layer + 1) * TILES)
                    act.activation(silu_g[:], banks[2 * (j % 4)][:, :], ACT.Silu).then_inc(silu_ready, 1)
                    act.wait_ge(prod_ready, layer * FCH + j + 1)
                    act.activation(mid_hi[:, j, :], banks[2 * (j % 4) + 1][:, :],
                                   ACT.Copy).then_inc(mid_hi_ready, 1)
                elif kind == "swa_T":
                    c = e[1]
                    act.wait_ge(swa_T, layer * TILES + c + 1)
                    act.activation(cT[:, :, c * P:(c + 1) * P],
                                   banks[4][:, :].rearrange("p (k t) -> p k t", k=4),
                                   ACT.Copy).then_inc(swa_cT, 1)
                elif kind == "swa_cur":
                    c = e[1]
                    act.wait_ge(swa_cur, layer * TILES + c + 1)
                    if c >= 2:
                        act.wait_ge(y_T, y_count(layer, ("swa_yT", c - 2)))
                    for g in range(2):
                        last = act.activation(prob[c % 2][:, 3 * g:3 * g + 3, :],
                                              swa_bank(c, g)[:, 0:BW].rearrange("p (h t) -> p h t", h=3),
                                              ACT.Copy)
                    last.then_inc(swa_S, 1)
                elif kind == "swa_prev":
                    c = e[1]
                    act.wait_ge(swa_m, layer * TILES + c + 1)
                    for hh in range(C_HEADS):
                        act.activation(prob[c % 2][:, hh, :], prob[c % 2][:, hh, :], ACT.Exp,
                                       bias=negm[c % 2][:, hh:hh + 1],
                                       accum_out=lsum[c % 2][:, hh:hh + 1])
                    act.activation(esink[c % 2], dsink[c % 2], ACT.Exp).then_inc(swa_exp, 1)
                elif kind == "swa_yT":
                    c = e[1]
                    y_split(layer, e, swa_bank(c, 1)[:, 0:BW].rearrange("p (k t) -> p k t", k=3),
                            y_hi[:, 5:8, c * P:(c + 1) * P])
                elif kind == "ret_T":
                    c = e[1]
                    act.wait_ge(ret_T, layer * TILES + c + 1)
                    for i in range(2):
                        last = act.activation(kqT[:, i, :, :],
                                              banks[4 + i][:, 0:BW].rearrange("p (k t) -> p k t", k=3),
                                              ACT.Copy)
                    last.then_inc(ret_kqT, 1)
                elif kind == "ret_yT":
                    c = e[1]
                    y_split(layer, e, ret_y_bank(c)[:, 0:BW].rearrange("p (k t) -> p k t", k=3),
                            y_hi[:, 2:5, c * P:(c + 1) * P])
                elif kind == "gmlp_yT":
                    n = y_count(layer, e)
                    for k in range(2):
                        act.wait_ge(y_T, n - 1 + k)
                        act.activation(y_hi[:, k, :], banks[6 + k][:, :], ACT.Copy).then_inc(y_hi_ready, 1)
                elif kind == "mm" and e[1][0] == "in":
                    _, strip, m = e
                    name = strip[1]
                    if strip != group_final(name) or name not in ACT_EVAC:
                        continue
                    act.wait_ge(mm_done, mm_count(layer, strip, m))
                    if name == "ckv":
                        act.activation(ck[:, m, :], banks[m][:, 0:P], ACT.Copy)
                        act.activation(cv[:, m, :], banks[m][:, P:2 * P], ACT.Copy).then_inc(evac_act, 1)
                    elif name == "cq":
                        if m >= 2:
                            act.wait_ge(swa_T, layer * TILES + m - 1)
                        act.activation(cq[m % 2][:].rearrange("p (j g d) -> p g j d", j=3, g=2),
                                       banks[m][:, 0:BW].rearrange("p (g j d) -> p g j d", j=3, g=2),
                                       ACT.Copy, scale=HD ** -0.5).then_inc(evac_act, 1)
                    elif name == "bv":
                        act.activation(bv[:, m, :], banks[m][:, 0:BW], ACT.Copy).then_inc(evac_act, 1)
                    elif name == "bg":
                        act.activation(bg[:, m, :], banks[m][:, 0:BW], ACT.Silu).then_inc(evac_act, 1)
                    else:
                        if m == 0:
                            act.wait_ge(swa_prev, (layer + 1) * 3)
                        act.activation(uv[:, m, :], banks[m][:, :], ACT.Gelu_apprx_tanh).then_inc(evac_act, 1)

        @block.gpsimd
        def _(pool):
            steps = [0]

            def step(ins):
                steps[0] += 1
                ins.then_inc(pool_step, 1)
                pool.wait_ge(pool_step, steps[0])

            pool.memset(half_neg, -0.5).then_inc(pool_init, 1)
            pool.memset(neg_big, NEG).then_inc(pool_init, 1)
            pool.wait_ge(pool_init, 2)
            def pre(layer, stage, m):
                n = pre_count(layer, stage, m)
                pool.wait_ge(pre_sq, n)
                if n > 2:
                    pool.wait_ge(xn_ready, n - 2)
                if n > 1:
                    pool.wait_ge(pre_r, n - 1)
                step(pool.tensor_scalar(t_pre, ss_pre[n % 2], EPS, None, ALU.add))
                pool.tensor_tensor(r_pre[n % 2], t_pre, half_neg[:, 0:1], ALU.pow).then_inc(pre_r, 1)

            for layer, e in schedule:
                kind = e[0]
                if kind == "post":
                    n = post_count(layer, e[1], e[2])
                    pool.wait_ge(post_sq, 2 * n)
                    if n > 2:
                        pool.wait_ge(*post_used(n - 2))
                    if n > 1:
                        pool.wait_ge(post_r, n - 1)
                    step(pool.tensor_scalar(t_post, ss_post[n % 2][:, 0:1], ss_post[n % 2][:, 1:2], EPS,
                                            ALU.add, ALU.add))
                    pool.tensor_tensor(r_post[n % 2], t_post, half_neg[:, 0:1], ALU.pow).then_inc(post_r, 1)
                elif kind == "pre":
                    pre(layer, e[1], e[2])
                elif kind == "swa_cur" and e[1] == 0:
                    pool.wait_ge(ws_loaded, 16 * (layer + 1))
                    pool.affine_select(out=wsT[:], in_=wsT[:], compare_op=ALU.is_ge, fill=0.0, base=0,
                                       pattern=[[0, A_HEADS], [1, P]],
                                       channel_multiplier=-1).then_inc(ws_ready, 1)
                elif kind == "ret_o":
                    n = layer * TILES + e[1] + 1
                    pool.wait_ge(ret_v, n)
                    if n > 1:
                        pool.wait_ge(ret_r, n - 1)
                    step(pool.tensor_scalar(rvt, rvar, 1.0 / HD, EPS, ALU.mult, ALU.add))
                    pool.tensor_tensor(rr[e[1]], rvt, half_neg, ALU.pow).then_inc(ret_r, 1)
                elif kind == "gmlp_v":
                    n = layer * TILES + e[1] + 1
                    pool.wait_ge(gm_v, n)
                    if n > 2:
                        pool.wait_ge(gm_vn, n - 2)
                    if n > 1:
                        pool.wait_ge(gm_r, n - 1)
                    step(pool.tensor_scalar(gvt, gvar, 1.0 / HD, EPS, ALU.mult, ALU.add))
                    pool.tensor_tensor(gr[e[1] % 2], gvt, half_neg[:, 0:A_HEADS], ALU.pow).then_inc(gm_r, 1)

        @block.vector
        def _(dve):
            counts = {}

            def done(ins, signal):
                counts[signal.name] = counts.get(signal.name, 0) + 1
                ins.then_inc(signal, 1)
                dve.wait_ge(signal, counts[signal.name])

            def step(ins):
                done(ins, dve_step)

            def heads(ap, n):
                return ap.rearrange("p (h d) -> p h d", h=n)

            def conv(g):
                if g >= depth * NS:
                    return
                n = piece_size(g)
                for j in range(2):
                    q = 2 * g + j
                    dve.wait_ge(hi_ready, q + 1)
                    done(dve.tensor_tensor(w_lo[g % SLOTS][:, j * n:(j + 1) * n], raw[q % RAWS][:, 0:n],
                                      w_hi[g % SLOTS][:, j * n:(j + 1) * n].bitcast(F32),
                                      ALU.subtract), lo_ready)

            def pre(layer, stage, m):
                n = pre_count(layer, stage, m)
                dve.wait_ge(pre_r, n)
                if n > 2:
                    q = n - 3
                    lay, r = divmod(q, 2 * TILES)
                    dve.wait_ge(x_T, t_count(lay, "ffn" if r >= TILES else "mix", r % TILES))
                dve.wait_ge(pre_w_loaded, 16 * (2 * layer + (1 if stage == "mix" else 2)))
                done(dve.scalar_tensor_tensor(out=xn[(n - 1) % 2][:], in0=x[:, m, :], scalar=r_pre[n % 2],
                                              in1=pre_w[:], op0=ALU.mult, op1=ALU.mult), xn_ready)

            def rope_full(layer, which, m):
                dst = (bk, bq)[which]
                src = banks[m][:, 0:BW]
                sc = (T_("ks"), T_("qs"))[which]
                done(dve.tensor_tensor(heads(rope_x[:], 6), heads(src, 6), sc[:, :, None].to_broadcast([P, 6, HD]),
                                  ALU.mult), evac_dve)
                dve.wait_ge(evac_dve, evac(layer, DVE_EVAC[which], m)[1])
                xr = rope_x[:].rearrange("p (h s d) -> p h s d", h=6, s=2)
                ar = rope_a[:].rearrange("p (h s d) -> p h s d", h=6, s=2)
                br = rope_b[:].rearrange("p (h s d) -> p h s d", h=6, s=2)
                cos = T_("rcos")[:, m * 32:(m + 1) * 32][:, None, None, :].to_broadcast([P, 6, 2, 32])
                sin = T_("rsin")[:, m * 32:(m + 1) * 32][:, None, None, :].to_broadcast([P, 6, 2, 32])
                done(dve.tensor_tensor(ar, xr, cos, ALU.mult), dve_step)
                step(dve.tensor_tensor(br, xr, sin, ALU.mult))
                o = dst[:, m, :].rearrange("p (h s d) -> p h s d", h=6, s=2)
                done(dve.tensor_tensor(o[:, :, 0, :], ar[:, :, 0, :], br[:, :, 1, :], ALU.subtract), dve_step)
                done(dve.tensor_tensor(o[:, :, 1, :], ar[:, :, 1, :], br[:, :, 0, :], ALU.add), b_roped)

            def rope_part(buf, n, m, signal):
                xr = heads(buf, n)[:, :, 0:16].rearrange("p h (s d) -> p h s d", s=2)
                ar = rope_a[:, 0:16 * n].rearrange("p (h s d) -> p h s d", h=n, s=2)
                br = rope_b[:, 0:16 * n].rearrange("p (h s d) -> p h s d", h=n, s=2)
                cos = T_("scos")[:, m * 8:(m + 1) * 8][:, None, None, :].to_broadcast([P, n, 2, 8])
                sin = T_("ssin")[:, m * 8:(m + 1) * 8][:, None, None, :].to_broadcast([P, n, 2, 8])
                done(dve.tensor_tensor(ar, xr, cos, ALU.mult), dve_step)
                step(dve.tensor_tensor(br, xr, sin, ALU.mult))
                done(dve.tensor_tensor(xr[:, :, 0, :], ar[:, :, 0, :], br[:, :, 1, :], ALU.subtract), dve_step)
                done(dve.tensor_tensor(xr[:, :, 1, :], ar[:, :, 1, :], br[:, :, 0, :], ALU.add), signal)

            def y_split(layer, e, bank, hi, lo):
                dve.wait_ge(y_hi_ready, y_count(layer, e))
                done(dve.tensor_tensor(lo, bank, hi.bitcast(F32), ALU.subtract), y_lo_ready)

            def mask3(ap):
                return ap[:, None, :].to_broadcast([P, 3, P])

            dve.wait_ge(pool_init, 2)
            def split_T(layer, stage, m):
                for half in range(2):
                    src = banks[2 * m + half][:, :].rearrange("p (k t) -> p k t", k=4)
                    hi = h_hi[:, 4 * half:4 * half + 4, m * P:(m + 1) * P]
                    lo = h_lo[:, 4 * half:4 * half + 4, m * P:(m + 1) * P]
                    dve.wait_ge(h_hi_ready, t_count(layer, stage, m, half))
                    done(dve.tensor_tensor(lo, src, hi.bitcast(F32), ALU.subtract), h_lo_ready)

            for layer, e in schedule:
                kind = e[0]
                if kind == "conv":
                    conv(layer * NS + e[1])
                elif kind == "T":
                    split_T(layer, e[1], e[2])
                elif kind == "post":
                    _, stage, m = e
                    n = post_count(layer, stage, m)
                    if stage == "ple":
                        dve.wait_ge(ple_w_loaded, 16 * (layer + 1))
                    else:
                        dve.wait_ge(post_w_loaded, 16 * (2 * layer + (1 if stage == "mix" else 2)))
                    dve.wait_ge(post_r, n)
                    wrow = ple_w if stage == "ple" else post_w
                    for half in range(2):
                        c = slice(half * 512, half * 512 + 512)
                        dst = ple_n[:, m, c] if stage == "ple" else upd[:, c]
                        last = dve.scalar_tensor_tensor(out=dst, in0=banks[2 * m + half][:, :],
                                                        scalar=r_post[n % 2], in1=wrow[:, c],
                                                        op0=ALU.mult, op1=ALU.mult)
                    if stage == "ple":
                        done(last, ple_ready)
                    else:
                        step(last)
                        done(dve.tensor_tensor(x[:, m, :], x[:, m, :], upd[:], ALU.add), x_new)
                    if stage == "ffn" and m == 0:
                        dve.wait_ge(p_hi_ready, layer + 1)
                        done(dve.tensor_tensor(p_lo[:], p_raw[:], p_hi[:].bitcast(F32),
                                          ALU.subtract), p_lo_ready)
                elif kind == "pre":
                    pre(layer, e[1], e[2])
                elif kind == "gated":
                    m = e[1]
                    dve.wait_ge(sig_ready, layer * TILES + m + 1)
                    dve.wait_ge(ple_ready, layer * TILES + m + 1)
                    step(dve.tensor_tensor(sig[:], sig[:], ple_n[:, m, :], ALU.mult))
                    done(dve.tensor_tensor(x[:, m, :], x[:, m, :], sig[:], ALU.add), x_new)
                elif kind == "mid":
                    j = e[1]
                    b = 2 * (j % 4) + 1
                    dve.wait_ge(silu_ready, layer * FCH + j + 1)
                    done(dve.tensor_tensor(banks[b][:, :], silu_g[:], banks[b][:, :], ALU.mult), prod_ready)
                    dve.wait_ge(mid_hi_ready, layer * FCH + j + 1)
                    done(dve.tensor_tensor(mid_lo[:, j, :], banks[b][:, :], mid_hi[:, j, :].bitcast(F32),
                                      ALU.subtract), mid_lo_ready)
                elif kind == "swa_prev":
                    c = e[1]
                    dve.wait_ge(swa_S, layer * TILES + c + 1)
                    if c == 0:
                        dve.wait_ge(params_loaded, 16 * 5 * (layer + 1))
                        dve.wait_ge(consts_loaded, 16)
                    else:
                        dve.wait_ge(swa_prev, layer * 3 + c)
                    o = c % 2
                    for g in range(2):
                        old = (swa_bank(c, g)[:, 0:BW].rearrange("p (h t) -> p h t", h=3) if c
                               else neg_big[:, :, None].to_broadcast([P, 3, P]))
                        last = dve.copy_predicated(prob[o][:, 3 * g:3 * g + 3, :], mask3(later_m[:]), old)
                    step(last)
                    step(dve.tensor_reduce(mx[o], prob[o][:], AX.X, ALU.max))
                    step(dve.tensor_tensor(mx[o], mx[o], snk, ALU.max))
                    done(dve.tensor_scalar(negm[o], mx[o], -1.0, None, ALU.mult), dve_step)
                    done(dve.tensor_tensor(dsink[o], snk, mx[o], ALU.subtract), swa_m)
                elif kind == "swa_PT":
                    c = e[1]
                    dve.wait_ge(swa_PT, layer * TILES + c + 1)
                    for g in range(2):
                        b3 = swa_bank(c, g)[:, 0:BW].rearrange("p (h t) -> p h t", h=3)
                        h3 = slice(3 * g, 3 * g + 3)
                        last = dve.tensor_tensor(ptl[c % 2][:, h3, :], b3, mask3(T_("lowT")), ALU.mult)
                        if c:
                            last = dve.tensor_tensor(ptu[c % 2][:, h3, :], b3, mask3(T_("upT")), ALU.mult)
                    done(last, swa_PTm)
                elif kind == "swa_o":
                    c = e[1]
                    o = c % 2
                    dve.wait_ge(swa_exp, layer * TILES + c + 1)
                    step(dve.tensor_tensor(rl[o], lsum[o], esink[o], ALU.add))
                    step(dve.reciprocal(rl[o], rl[o]))
                    dve.wait_ge(swa_o, layer * TILES + c + 1)
                    done(dve.tensor_tensor(swa_y[o][:], heads(swa_bank(c, 0)[:, 0:BW], 6),
                                           rl[o][:, :, None].to_broadcast([P, 6, HD]), ALU.mult), swa_yr)
                elif kind == "swa_yT":
                    c = e[1]
                    y_split(layer, e, swa_bank(c, 1)[:, 0:BW].rearrange("p (k t) -> p k t", k=3),
                            y_hi[:, 5:8, c * P:(c + 1) * P], y_lo[:, 5:8, c * P:(c + 1) * P])
                elif kind == "ret_sc":
                    c = e[1]
                    dve.wait_ge(ret_sc, layer * TILES + c + 1)
                    for g in range(2):
                        last = dve.tensor_tensor(scm[:, g, :, :],
                                                 banks[4 + g][:, 0:BW].rearrange("p (h t) -> p h t", h=3),
                                                 mask3(T_("lowT")), ALU.mult)
                    done(last, ret_scm)
                elif kind == "ret_o":
                    c = e[1]
                    if c == 0:
                        step(dve.memset(state[:], 0.0))
                    dve.wait_ge(ret_o, layer * TILES + c + 1)
                    o = heads(banks[4][:, 0:BW], 6)
                    step(dve.tensor_reduce(rmu, o, AX.X, ALU.add))
                    step(dve.tensor_scalar(rmu, rmu, 1.0 / HD, None, ALU.mult))
                    done(dve.tensor_tensor(heads(ret_oc[:, c, :], 6), o, rmu[:, :, None].to_broadcast([P, 6, HD]),
                                      ALU.subtract), ret_oread)
                    dve.wait_ge(ret_oread, layer * TILES + c + 1)
                    step(dve.tensor_tensor(ret_sq[:], ret_oc[:, c, :], ret_oc[:, c, :], ALU.mult))
                    if c or layer:
                        dve.wait_ge(ret_r, layer * TILES + c)
                    done(dve.tensor_reduce(rvar, heads(ret_sq[:], 6), AX.X, ALU.add), ret_v)
                    if c < TILES - 1:
                        dve.wait_ge(ret_kv, layer * 3 + c + 1)
                        for g in range(2):
                            r, q = slice(HD * g, HD * (g + 1)), slice(HD * g, HD * (g + 1))
                            st = state[r, :, q]
                            kv = banks[5][:, 0:BW].rearrange("p (j e) -> p j e", j=3)[r, :, q]
                            step(dve.tensor_tensor(st, st, kv, ALU.add))
                            last = dve.tensor_tensor(st, st, T_("gcol")[r, :, None].to_broadcast([HD, 3, HD]),
                                                     ALU.mult)
                        done(last, ret_state)
                elif kind == "ret_norm":
                    c = e[1]
                    dve.wait_ge(gs_ready, layer * TILES + c + 1)
                    dve.wait_ge(ret_r, layer * TILES + c + 1)
                    oc = heads(ret_oc[:, c, :], 6)
                    step(dve.tensor_tensor(oc, oc, rr[c][:, :, None].to_broadcast([P, 6, HD]), ALU.mult))
                    done(dve.tensor_tensor(ret_y[:, c, :], ret_oc[:, c, :], bg[:, c, :], ALU.mult), ret_yr)
                elif kind == "ret_yT":
                    c = e[1]
                    y_split(layer, e, ret_y_bank(c)[:, 0:BW].rearrange("p (k t) -> p k t", k=3),
                            y_hi[:, 2:5, c * P:(c + 1) * P], y_lo[:, 2:5, c * P:(c + 1) * P])
                elif kind == "gmlp_v":
                    m = e[1]
                    dve.wait_ge(evac_act, evac(layer, "a", m)[1])
                    v = heads(uv[:, m, AW:2 * AW], A_HEADS)
                    step(dve.tensor_reduce(gmu, v, AX.X, ALU.add))
                    step(dve.tensor_scalar(gmu, gmu, 1.0 / HD, None, ALU.mult))
                    step(dve.tensor_tensor(heads(vn[:, m, :], A_HEADS), v,
                                           gmu[:, :, None].to_broadcast([P, A_HEADS, HD]), ALU.subtract))
                    step(dve.tensor_tensor(vsq[:], vn[:, m, :], vn[:, m, :], ALU.mult))
                    if m or layer:
                        dve.wait_ge(gm_r, layer * TILES + m)
                    done(dve.tensor_reduce(gvar, heads(vsq[:], A_HEADS), AX.X, ALU.add), gm_v)
                elif kind == "gmlp_n":
                    m = e[1]
                    dve.wait_ge(gm_r, layer * TILES + m + 1)
                    vch = heads(vn[:, m, :], A_HEADS)
                    step(dve.tensor_tensor(vch, vch, gr[m % 2][:, :, None].to_broadcast([P, A_HEADS, HD]),
                                           ALU.mult))
                    step(dve.tensor_tensor(vn[:, m, :], vn[:, m, :], lnw[:], ALU.mult))
                    done(dve.tensor_tensor(vn[:, m, :], vn[:, m, :], lnb[:], ALU.add), gm_vn)
                elif kind == "gmlp_mix":
                    dve.wait_ge(gm_mix, layer + 1)
                    for b in range(2):
                        mixed = banks[6 + b][:, :].rearrange("p (c h d) -> p c h d", c=2, h=A_HEADS)
                        bias = bs[:, None, :, None].to_broadcast([P, 2, A_HEADS, HD])
                        done(dve.tensor_tensor(vn[:, 2 * b:2 * b + 2, :].rearrange("p c (h d) -> p c h d", h=A_HEADS),
                                          mixed, bias, ALU.add), dve_step)
                    u = uv[:, :, 0:AW]
                    done(dve.tensor_tensor(u, u, vn[:], ALU.mult), gm_ya)
                elif kind == "gmlp_yT":
                    n = y_count(layer, e)
                    for k in range(2):
                        dve.wait_ge(y_hi_ready, n - 1 + k)
                        done(dve.tensor_tensor(y_lo[:, k, :], banks[6 + k][:, :], y_hi[:, k, :].bitcast(F32),
                                          ALU.subtract), y_lo_ready)
                elif kind == "mm" and e[1][0] == "in":
                    _, strip, m = e
                    name = strip[1]
                    if strip != group_final(name):
                        continue
                    if name == "ckv":
                        dve.wait_ge(table_loaded, 16)
                        dve.wait_ge(evac_act, evac(layer, name, m)[1])
                        rope_part(ck[:, m, :], 2, m, ck_roped)
                    elif name == "cq":
                        dve.wait_ge(evac_act, evac(layer, name, m)[1])
                        rope_part(cq[m % 2][:], 6, m, cq_roped)
                    elif name in DVE_EVAC:
                        dve.wait_ge(mm_done, mm_count(layer, strip, m))
                        rope_full(layer, DVE_EVAC.index(name), m)
                    elif name == "bg":
                        dve.wait_ge(evac_act, evac(layer, name, m)[1])
                        if m == 0:
                            dve.wait_ge(params_loaded, 16 * 5 * (layer + 1))
                        done(dve.tensor_tensor(bg[:, m, :], bg[:, m, :], gnw[:], ALU.mult), gs_ready)


_ORDER = ["x_in", "p_t", "pre_mix", "w_in", "ln_w", "ln_b", "ws_t", "bs_t", "gn_w", "sinks", "w_out",
          "post_mix", "pre_ffn", "w_ffn_in", "w_ffn_out", "post_ffn", "w_gate", "w_ple", "ple_norm",
          "table", "later"]


def kernel(x, p, norm_mix_pre, w_in, gmlp_ln_w, gmlp_ln_b, gmlp_ws, gmlp_bs, ret_gn_w, attn_sinks,
           w_out, norm_mix_post, norm_ffn_pre, w_ffn_in, w_ffn_out, norm_ffn_post, w_ple_gate,
           w_ple_proj, ple_norm):
    import concourse.bacc as bacc
    from concourse.bass_utils import run_bass_kernel_spmd

    depth = w_in.shape[0]
    table, later = small_tables()
    values = {
        "x_in": np.asarray(x)[0],
        "p_t": np.asarray(p)[:, 0].transpose(0, 2, 1),
        "pre_mix": norm_mix_pre, "pre_ffn": norm_ffn_pre,
        "w_in": w_in, "ln_w": gmlp_ln_w, "ln_b": gmlp_ln_b,
        "ws_t": np.asarray(gmlp_ws).transpose(0, 3, 1, 2),
        "bs_t": np.asarray(gmlp_bs).transpose(0, 2, 1),
        "gn_w": ret_gn_w, "sinks": attn_sinks, "w_out": w_out, "post_mix": norm_mix_post,
        "w_ffn_in": w_ffn_in, "w_ffn_out": w_ffn_out, "post_ffn": norm_ffn_post,
        "w_gate": w_ple_gate, "w_ple": w_ple_proj, "ple_norm": ple_norm,
        "table": table, "later": later,
    }
    nc = bacc.Bacc("TRN2", target_bir_lowering=False, num_devices=1)
    arrays, args = {}, []
    for name in _ORDER:
        a = np.ascontiguousarray(values[name])
        arrays[f"in_{name}"] = a
        args.append(nc.dram_tensor(f"in_{name}", a.shape, mybir.dt.from_np(a.dtype), kind="ExternalInput").ap())
    out = nc.dram_tensor("out", [S, D], F32, kind="ExternalOutput").ap()
    build_trunk(nc, depth, *args, out)
    r = run_bass_kernel_spmd(nc, [arrays], core_ids=[0])
    return r.results[0]["out"].reshape(1, S, D)
```
